# Optimizing a Trainium2 kernel written in Bass

```python
import math
import jax, jax.numpy as jnp
from jax import lax
import numpy as np

D_MODEL = 1024
BATCH = 1
SEQ = 512
DEPTH = 1

CHUNK = 64
Q_BLOCK = 128
MIX_W = 512
N_BRANCH = 3
EPS = 1e-6
FOX_HEADS = 8
FOX_HD = MIX_W // FOX_HEADS
GLA_HEADS = 4
GLA_DK = 64
GLA_DV = MIX_W // GLA_HEADS
GLA_RANK = 16
GLA_GATE_NORM = 16.0
SSM_HEADS = 8
SSM_HD = MIX_W // SSM_HEADS
SSM_GROUPS = 2
SSM_STATE = 64
SSM_CONV = 4
SSM_CONV_DIM = MIX_W + 2 * SSM_GROUPS * SSM_STATE
N_EGROUPS = 4
EXP_PER_GROUP = 4
N_EXPERTS = N_EGROUPS * EXP_PER_GROUP
TOP_K = 2
D_EXPERT = 512
FOX_COLS = 3 * MIX_W + FOX_HEADS
GLA_COLS = 2 * GLA_HEADS * GLA_DK + 2 * MIX_W + GLA_RANK
SSM_COLS = MIX_W + SSM_CONV_DIM + SSM_HEADS
GATE_COLS = N_BRANCH * D_MODEL
IN_COLS = FOX_COLS + GLA_COLS + SSM_COLS + GATE_COLS

kernel_name = "hybrid_fox_gla_ssd_hiermoe_block"

def rms_norm(x, gain):
    xf = x.astype(jnp.float32)
    y = xf * lax.rsqrt(jnp.mean(xf * xf, axis=-1, keepdims=True) + EPS)
    return (y * gain.astype(jnp.float32)).astype(x.dtype)

def _to_chunks(t):
    b, s, h = t.shape[:3]
    rest = t.shape[3:]
    t = t.reshape((b, s // CHUNK, CHUNK, h) + rest)
    perm = (0, 3, 1, 2) + tuple(range(4, t.ndim))
    return jnp.transpose(t, perm).astype(jnp.float32)

def _scan_chunk_states(decay, upd):
    dec = jnp.moveaxis(decay, 2, 0)
    up = jnp.moveaxis(upd, 2, 0)

    def step(state, inp):
        d, u = inp
        return d * state + u, state

    _, prev = lax.scan(step, jnp.zeros(up.shape[1:], up.dtype), (dec, up))
    return jnp.moveaxis(prev, 0, 2)

def forgetting_attention(q, k, v, f_logit, q_gain, k_gain):
    b, s, h, hd = q.shape
    q = rms_norm(q, q_gain) * (hd ** -0.5)
    k = rms_norm(k, k_gain)
    c = jnp.cumsum(jax.nn.log_sigmoid(f_logit.astype(jnp.float32)), axis=1)
    c = jnp.transpose(c, (0, 2, 1))
    qh = jnp.transpose(q, (0, 2, 1, 3))
    kh = jnp.transpose(k, (0, 2, 1, 3))
    vh = jnp.transpose(v, (0, 2, 1, 3))
    nqb = s // Q_BLOCK
    qb = jnp.transpose(qh.reshape(b, h, nqb, Q_BLOCK, hd), (2, 0, 1, 3, 4))
    cb = jnp.transpose(c.reshape(b, h, nqb, Q_BLOCK), (2, 0, 1, 3))
    qpos = jnp.arange(nqb)[:, None] * Q_BLOCK + jnp.arange(Q_BLOCK)[None, :]
    kpos = jnp.arange(s)

    def block(args):
        qi, ci, pi = args
        sc = jnp.einsum('bhqd,bhkd->bhqk', qi, kh).astype(jnp.float32)
        sc = sc + ci[..., None] - c[:, :, None, :]
        sc = jnp.where(pi[:, None] >= kpos[None, :], sc, -jnp.inf)
        p = jax.nn.softmax(sc, axis=-1)
        return jnp.einsum('bhqk,bhkd->bhqd', p.astype(vh.dtype), vh)

    o = lax.map(block, (qb, cb, qpos))
    return jnp.transpose(o, (1, 0, 3, 2, 4)).reshape(b, s, h * hd)

def gla_chunked(q, k, v, log_a):
    b, s, h, dk = q.shape
    dv = v.shape[-1]
    qc = _to_chunks(q) * (dk ** -0.5)
    kc = _to_chunks(k)
    vc = _to_chunks(v)
    g = _to_chunks(log_a)
    bcum = jnp.cumsum(g, axis=3)
    b_last = bcum[:, :, :, -1:, :]
    q_dec = qc * jnp.exp(bcum)
    k_dec = kc * jnp.exp(-bcum)
    causal = jnp.tril(jnp.ones((CHUNK, CHUNK), dtype=bool))
    attn = jnp.where(causal, jnp.einsum('bhctd,bhcsd->bhcts', q_dec, k_dec), 0.0)
    o_intra = jnp.einsum('bhcts,bhcsv->bhctv', attn, vc)
    kv = jnp.einsum('bhcsd,bhcsv->bhcdv', kc * jnp.exp(b_last - bcum), vc)
    prev = _scan_chunk_states(jnp.exp(b_last[:, :, :, 0, :])[..., None], kv)
    o = o_intra + jnp.einsum('bhctd,bhcdv->bhctv', q_dec, prev)
    return jnp.transpose(o, (0, 2, 3, 1, 4)).reshape(b, s, h, dv).astype(q.dtype)

def causal_depthwise_conv(u, w, bias):
    ch = u.shape[-1]
    out = lax.conv_general_dilated(u, w[:, None, :].astype(u.dtype), window_strides=(1,),
                                   padding=[(w.shape[0] - 1, 0)],
                                   dimension_numbers=('NWC', 'WIO', 'NWC'),
                                   feature_group_count=ch)
    return out + bias

def ssd_chunked(x, dt, a, bm, cm):
    hpg = SSM_HEADS // SSM_GROUPS
    bc = _to_chunks(jnp.repeat(bm, hpg, axis=2))
    cc = _to_chunks(jnp.repeat(cm, hpg, axis=2))
    xc = _to_chunks(x)
    dtc = _to_chunks(dt)
    acs = jnp.cumsum(dtc * a[:, None, None], axis=-1)
    causal = jnp.tril(jnp.ones((CHUNK, CHUNK), dtype=bool))
    decay = jnp.exp(jnp.where(causal, acs[..., :, None] - acs[..., None, :], -jnp.inf))
    xdt = xc * dtc[..., None]
    scores = jnp.einsum('bhctn,bhcsn->bhcts', cc, bc) * decay
    y_intra = jnp.einsum('bhcts,bhcsp->bhctp', scores, xdt)
    to_end = jnp.exp(acs[..., -1:] - acs)
    states = jnp.einsum('bhcsn,bhcsp->bhcnp', bc * to_end[..., None], xdt)
    prev = _scan_chunk_states(jnp.exp(acs[..., -1])[..., None, None], states)
    y = y_intra + jnp.einsum('bhctn,bhcnp->bhctp', cc * jnp.exp(acs)[..., None], prev)
    b, h, nc, c, p = y.shape
    return jnp.transpose(y, (0, 2, 3, 1, 4)).reshape(b, nc * c, h, p)

def mamba2_branch(z, xbc, dt_raw, conv_w, conv_b, dt_bias, a_log, d_skip, out_norm):
    b, s, _ = z.shape
    xbc = jax.nn.silu(causal_depthwise_conv(xbc, conv_w, conv_b))
    xs, bm, cm = jnp.split(xbc, [MIX_W, MIX_W + SSM_GROUPS * SSM_STATE], axis=-1)
    xs_h = xs.reshape(b, s, SSM_HEADS, SSM_HD)
    dt = jax.nn.softplus((dt_raw + dt_bias).astype(jnp.float32))
    a = -jnp.exp(a_log.astype(jnp.float32))
    y = ssd_chunked(xs_h, dt, a, bm.reshape(b, s, SSM_GROUPS, SSM_STATE),
                    cm.reshape(b, s, SSM_GROUPS, SSM_STATE))
    y = y + d_skip.astype(jnp.float32)[:, None] * xs_h.astype(jnp.float32)
    y = y.reshape(b, s, MIX_W).astype(z.dtype) * jax.nn.silu(z)
    y = rms_norm(y.reshape(b, s, SSM_GROUPS, MIX_W // SSM_GROUPS),
                 out_norm.reshape(SSM_GROUPS, MIX_W // SSM_GROUPS))
    return y.reshape(b, s, MIX_W)

def hierarchical_moe(h, w_router_grp, b_router_grp, w_router_exp, b_router_exp,
                     w_exp_gate, w_exp_up, w_exp_down):
    b, s, d = h.shape
    t = h.reshape(b * s, d)
    g_prob = jax.nn.softmax((t @ w_router_grp + b_router_grp).astype(jnp.float32), axis=-1)
    g_w, g_sel = lax.top_k(g_prob, 1)
    e_logits = (t @ w_router_exp + b_router_exp).astype(jnp.float32)
    e_logits = e_logits.reshape(-1, N_EGROUPS, EXP_PER_GROUP)
    e_in = jnp.einsum('tg,tge->te', jax.nn.one_hot(g_sel[:, 0], N_EGROUPS, dtype=jnp.float32), e_logits)
    top_w, top_i = lax.top_k(jax.nn.softmax(e_in, axis=-1), TOP_K)
    top_w = top_w / jnp.sum(top_w, axis=-1, keepdims=True) * g_w
    expert_id = g_sel * EXP_PER_GROUP + top_i
    combine = jnp.sum(jax.nn.one_hot(expert_id, N_EXPERTS, dtype=jnp.float32) * top_w[..., None], axis=1)
    combine = combine.astype(t.dtype)
    out = jnp.zeros_like(t)
    for e in range(N_EXPERTS):
        hid = jax.nn.silu(t @ w_exp_gate[e]) * (t @ w_exp_up[e])
        out = out + combine[:, e:e + 1] * (hid @ w_exp_down[e])
    return out.reshape(b, s, d)

def _layer(x, norm_mix, w_in, fox_f_bias, fox_q_norm, fox_k_norm, gla_w_lr, gla_b_gate,
           gla_out_norm, ssm_conv_w, ssm_conv_b, ssm_dt_bias, ssm_a_log, ssm_d, ssm_out_norm,
           w_branch, b_branch_gate, w_out, norm_ffn, w_router_grp, b_router_grp,
           w_router_exp, b_router_exp, w_exp_gate, w_exp_up, w_exp_down):
    b, s, _ = x.shape
    h = rms_norm(x, norm_mix)
    proj = h @ w_in
    sizes = [MIX_W, MIX_W, MIX_W, FOX_HEADS,
             GLA_HEADS * GLA_DK, GLA_HEADS * GLA_DK, MIX_W, MIX_W, GLA_RANK,
             MIX_W, SSM_CONV_DIM, SSM_HEADS, GATE_COLS]
    offsets = [int(o) for o in np.cumsum(sizes)[:-1]]
    (fq, fk, fv, ff, gq, gk, gv, gr, glr, sz, sxbc, sdt, gate_pre) = jnp.split(proj, offsets, axis=-1)
    o_a = forgetting_attention(fq.reshape(b, s, FOX_HEADS, FOX_HD), fk.reshape(b, s, FOX_HEADS, FOX_HD),
                               fv.reshape(b, s, FOX_HEADS, FOX_HD), ff + fox_f_bias,
                               fox_q_norm, fox_k_norm)
    log_a = jax.nn.log_sigmoid((glr @ gla_w_lr + gla_b_gate).astype(jnp.float32)) / GLA_GATE_NORM
    o_b = gla_chunked(gq.reshape(b, s, GLA_HEADS, GLA_DK), gk.reshape(b, s, GLA_HEADS, GLA_DK),
                      gv.reshape(b, s, GLA_HEADS, GLA_DV), log_a.reshape(b, s, GLA_HEADS, GLA_DK))
    o_b = rms_norm(o_b, gla_out_norm).reshape(b, s, MIX_W) * jax.nn.silu(gr)
    o_c = mamba2_branch(sz, sxbc, sdt, ssm_conv_w, ssm_conv_b, ssm_dt_bias, ssm_a_log, ssm_d, ssm_out_norm)
    branches = jnp.stack([o_a, o_b, o_c], axis=2)
    proj_b = jnp.einsum('bsrc,rcd->bsrd', branches, w_branch)
    gates = jax.nn.sigmoid(gate_pre.reshape(b, s, N_BRANCH, D_MODEL) + b_branch_gate)
    x = x + jnp.sum(gates * proj_b, axis=2) @ w_out
    x = x + hierarchical_moe(rms_norm(x, norm_ffn), w_router_grp, b_router_grp, w_router_exp,
                             b_router_exp, w_exp_gate, w_exp_up, w_exp_down)
    return x

def setup_inputs(seed: int = 0) -> dict:
    key = jax.random.key(seed)
    ks = jax.random.split(key, 32)
    L, D = DEPTH, D_MODEL
    f32 = jnp.float32

    def nrm(k, shape, scale):
        return jax.random.normal(k, shape, f32) * scale

    dt = jnp.exp(jax.random.uniform(ks[12], (L, SSM_HEADS), f32) * (math.log(0.1) - math.log(0.001))
                 + math.log(0.001))
    return {
        "x": nrm(ks[0], (BATCH, SEQ, D), 1.0),
        "norm_mix": 1.0 + nrm(ks[1], (L, D), 0.05),
        "w_in": nrm(ks[2], (L, D, IN_COLS), D ** -0.5),
        "fox_f_bias": 2.0 + nrm(ks[3], (L, FOX_HEADS), 0.5),
        "fox_q_norm": 1.0 + nrm(ks[4], (L, FOX_HD), 0.05),
        "fox_k_norm": 1.0 + nrm(ks[5], (L, FOX_HD), 0.05),
        "gla_w_lr": nrm(ks[6], (L, GLA_RANK, GLA_HEADS * GLA_DK), GLA_RANK ** -0.5),
        "gla_b_gate": nrm(ks[7], (L, GLA_HEADS * GLA_DK), 0.1),
        "gla_out_norm": 1.0 + nrm(ks[8], (L, GLA_DV), 0.05),
        "ssm_conv_w": nrm(ks[9], (L, SSM_CONV, SSM_CONV_DIM), SSM_CONV ** -0.5),
        "ssm_conv_b": nrm(ks[10], (L, SSM_CONV_DIM), 0.02),
        "ssm_dt_bias": dt + jnp.log(-jnp.expm1(-dt)),
        "ssm_a_log": jnp.log(jax.random.uniform(ks[11], (L, SSM_HEADS), f32, 1.0, 16.0)),
        "ssm_d": 1.0 + nrm(ks[13], (L, SSM_HEADS), 0.05),
        "ssm_out_norm": 1.0 + nrm(ks[14], (L, MIX_W), 0.05),
        "w_branch": nrm(ks[15], (L, N_BRANCH, MIX_W, D), MIX_W ** -0.5),
        "b_branch_gate": nrm(ks[16], (L, N_BRANCH, D), 0.1),
        "w_out": nrm(ks[17], (L, D, D), D ** -0.5),
        "norm_ffn": 1.0 + nrm(ks[18], (L, D), 0.05),
        "w_router_grp": nrm(ks[19], (L, D, N_EGROUPS), D ** -0.5),
        "b_router_grp": nrm(ks[20], (L, N_EGROUPS), 0.01),
        "w_router_exp": nrm(ks[21], (L, D, N_EXPERTS), D ** -0.5),
        "b_router_exp": nrm(ks[22], (L, N_EXPERTS), 0.01),
        "w_exp_gate": nrm(ks[23], (L, N_EXPERTS, D, D_EXPERT), D ** -0.5),
        "w_exp_up": nrm(ks[24], (L, N_EXPERTS, D, D_EXPERT), D ** -0.5),
        "w_exp_down": nrm(ks[25], (L, N_EXPERTS, D_EXPERT, D), D_EXPERT ** -0.5),
    }

def reference(x, norm_mix, w_in, fox_f_bias, fox_q_norm, fox_k_norm, gla_w_lr, gla_b_gate,
              gla_out_norm, ssm_conv_w, ssm_conv_b, ssm_dt_bias, ssm_a_log, ssm_d, ssm_out_norm,
              w_branch, b_branch_gate, w_out, norm_ffn, w_router_grp, b_router_grp,
              w_router_exp, b_router_exp, w_exp_gate, w_exp_up, w_exp_down):
    for l in range(DEPTH):
        x = _layer(x, norm_mix[l], w_in[l], fox_f_bias[l], fox_q_norm[l], fox_k_norm[l],
                   gla_w_lr[l], gla_b_gate[l], gla_out_norm[l], ssm_conv_w[l], ssm_conv_b[l],
                   ssm_dt_bias[l], ssm_a_log[l], ssm_d[l], ssm_out_norm[l], w_branch[l],
                   b_branch_gate[l], w_out[l], norm_ffn[l], w_router_grp[l], b_router_grp[l],
                   w_router_exp[l], b_router_exp[l], w_exp_gate[l], w_exp_up[l], w_exp_down[l])
    return x


_drawn_inputs = setup_inputs


def setup_inputs(seed=0):
    import zlib

    import numpy as np

    out = dict(_drawn_inputs(seed))
    spreads = {}
    factors = {'fox_q_norm': 3.15,
     'fox_k_norm': 3.321,
     'gla_b_gate': 3.23,
     'ssm_d': 3.118,
     'b_router_grp': 4.913,
     'b_router_exp': 5.933}
    for name, (base, spread) in spreads.items():
        noise = np.random.default_rng([zlib.crc32(name.encode()), seed]).standard_normal(out[name].shape)
        drawn = base * np.exp(spread * noise) if base else spread * noise
        out[name] = __import__('jax').numpy.asarray(drawn.astype(out[name].dtype))
    for name, factor in factors.items():
        out[name] = (out[name] * factor).astype(out[name].dtype)
    return out
```

```python
from contextlib import ExitStack

import numpy as np

import concourse.bass as bass
from concourse import mybir

F32 = mybir.dt.float32
F32R = mybir.dt.float32r
BF16 = mybir.dt.bfloat16
I32 = mybir.dt.int32
ALU = mybir.AluOpType
ACT = mybir.ActivationFunctionType
AX = mybir.AxisListType.X

P = 128
T, D = 512, 1024
NT, KD = T // P, D // P
MIX = 512
CHUNK = 64
EPS = 1e-6
FOX_H, FOX_HD = 8, 64
GLA_H, GLA_DK, GLA_RANK = 4, 64, 16
SSM_H, SSM_G, SSM_CONV = 8, 2, 4
NEG, NEXP, EPG, DE = 4, 16, 4, 512
NEGBIG = -1e30

C_FQ, C_FK, C_FV, C_FF = 0, 512, 1024, 1536
C_GQK, C_GV, C_GR, C_GLR = 1544, 2056, 2568, 3080
C_Z, C_XBC, C_DT, C_GATE = 3096, 3608, 4376, 4384

RING = 3
UW = 512

BLOCKS = [("fq", C_FQ, 512, "T"), ("fk", C_FK, 512, "T"), ("fv", C_FV, 512, "tok"),
          ("xs", C_XBC, 512, "T"), ("bc", C_XBC + 512, 256, "T"), ("gqk", C_GQK, 512, "T"),
          ("gv", C_GV, 512, "tok"), ("gr", C_GR, 512, "T"), ("z", C_Z, 512, "tok")]
NB = len(BLOCKS)
SUBS = [4 if b[3] == "tok" else b[2] // P for b in BLOCKS]

U_GATE = 2 * NB
U_OUT = U_GATE + 18
U_MOE = U_OUT + 4
U_OVF = U_MOE + 6 * NEXP
OVF = 7
ITEMS = NEXP + OVF

R_NM, R_NF, R_BG, R_CW, R_CB, R_GB, R_GO, R_FQ, R_FK = 0, 8, 16, 40, 64, 70, 72, 73, 74
NROWS = 75

MIB = [4, 5, 6, 7]


def schedule():
    pieces = [("piece", b, kh, s, q) for b in range(NB) for kh in range(2) for s in range(SUBS[b])
              for q in range(2)]
    first = [p for p in pieces if p[1] < 3]
    rest = [p for p in pieces if p[1] >= 3]
    out = [("small",), ("loga", 0), ("loga", 1), ("tokrows",)]
    waiting = [[], []]
    for p in first:
        out.append(p)
        if p[3] == 0 and p[4] == 0:
            out += [("hi", 2 * p[1] + p[2] + 2), ("lo", 2 * p[1] + p[2] + 2)]
        if p[4] == 1:
            out += waiting[0]
            m = [4 * p[1] + p[3]] if p[1] < 2 and p[2] == 1 else []
            waiting = [[("square", q) for q in m] + waiting[1], [("qnorm", q) for q in m]]
    steps = FOX_H * NT
    out += [("cb", 0), ("score", 0), ("score", 1), ("norm", 0)]
    done, convs, los, squash = 0, 0, [], []
    for n in range(steps):
        if n + 2 < steps:
            if (n + 2) % NT == 0:
                out.append(("cb", (n + 2) // NT))
            out.append(("score", n + 2))
        if n + 1 < steps:
            out.append(("norm", n + 1))
        out += los
        out += squash
        squash = []
        if not los and convs < 6 and ("piece", 3 + convs // 4, 1, convs % 4, 1) in rest[:max(done - 1, 0)]:
            out.append(("conv", convs))
            squash = [("squash", convs)]
            convs += 1
        upto = (n + 1) * len(rest) // steps
        taken = rest[done:upto]
        out += taken[:1] + [("turn", n)] + taken[1:] + [("pv", n)]
        out += [("hi", 2 * p[1] + p[2] + 2) for p in taken if p[3] == 0 and p[4] == 0]
        los = [("lo", 2 * p[1] + p[2] + 2) for p in taken if p[3] == 0 and p[4] == 0]
        done = upto
    out += los
    assert convs == 6
    for pr in range(2):
        out += [("gprep", pr), ("kv", pr)]
        for h in (2 * pr, 2 * pr + 1):
            out.append(("ghead", h))
        for h in (2 * pr, 2 * pr + 1):
            out.append(("gout", h))
    out += [("ssdprep",)] + [("ssd", i) for i in range(NT)]
    return out


SCHED = schedule()


def bank_uses():
    uses = {b: [] for b in range(8)}
    uses[0].append("cols")
    for k in range(KD):
        uses[k].append("hT")
    for it in SCHED:
        kind = it[0]
        if kind == "small":
            uses[4].append("small")
        elif kind == "loga":
            uses[5 + it[1]].append(it)
        elif kind == "tokrows":
            uses[7].append(it)
        elif kind == "piece" and it[2] == 0 and it[4] == 0:
            uses[it[3]].append(("block", it[1]))
        elif kind == "qnorm":
            uses[4 + it[1] % 2].append(it)
        elif kind == "cb":
            uses[6].append(it)
        elif kind == "score":
            uses[4 + it[1] % 2].append(it)
        elif kind == "turn":
            uses[6].append(it)
        elif kind == "pv" and it[1] % 8 == 0:
            uses[7].append(("opair", it[1] // 8))
        elif kind == "gprep":
            uses[4].append(it)
        elif kind == "kv":
            uses[5].append(("kv", it[1], 0))
            uses[6].append(("kv", it[1], 1))
        elif kind == "ghead":
            uses[4 + it[1] % 2].append(("gs", it[1]))
            uses[6 + it[1] % 2].append(("go", it[1]))
        elif kind == "gout":
            uses[4 + it[1] % 2].append(it)
        elif kind == "ssd":
            i = it[1]
            uses[4].append(("bca", i))
            uses[5].append(("bcb", i))
            uses[7].append(("xt", i))
            uses[6].append(("sc", i))
            uses[7].append(("yi", i))
            if i:
                uses[6].append(("ye", i))
            if i < NT - 1:
                uses[4].append(("st", i))
            uses[5].append(("yt", i))
    for g in range(6):
        for s in range(4):
            uses[s].append(("gate", g))
            uses[4 + s].append(("proj", g))
    for nh in range(2):
        for s in range(4):
            uses[4 * nh + s].append(("out", nh))
    for k in range(KD):
        uses[k].append("h2T")
    uses[0].append("logits")
    uses[1].append("pos")
    return uses


USES = bank_uses()


def turn(bank, key):
    return USES[bank].index(key)


def unit_source(u, w_in, w_branch, w_out):
    def block(w, r0, c0, n):
        return w[r0:r0 + 512, c0:c0 + n].rearrange("(j p) n -> p j n", p=P)
    if u < U_GATE:
        b, kh = divmod(u, 2)
        return block(w_in, kh * 512, BLOCKS[b][1], BLOCKS[b][2])
    if u < U_OUT:
        g, part = divmod(u - U_GATE, 3)
        dh, r = divmod(g, 3)
        if part < 2:
            return block(w_in, part * 512, C_GATE + r * D + dh * 512, 512)
        return block(w_branch[r], 0, dh * 512, 512)
    nh, kh = divmod(u - U_OUT, 2)
    return block(w_out, kh * 512, nh * 512, 512)


def after(m, per, count):
    return count if m is None else m * per + count


def gslot(h):
    return (0, 2, 1, 3)[h]


class Serial:

    def __init__(self, eng, sem):
        self.eng, self.sem, self.n = eng, sem, 0

    def __call__(self, ins, sem=None, n=None):
        if sem is None:
            self.n += 1
            sem, n = self.sem, self.n
        ins.then_inc(sem, 1)
        self.eng.wait_ge(sem, n)


def build(nc, x, norm_mix, w_in, fox_f_bias, fox_q_norm, fox_k_norm, gla_w_lr, gla_b_gate,
          gla_out_norm, ssm_conv_w, ssm_conv_b, ssm_dt_bias, ssm_a_log, ssm_d, ssm_out_norm,
          w_branch, b_branch_gate, w_out, norm_ffn, w_router_grp, b_router_grp,
          w_router_exp, b_router_exp, w_exp_gate, w_exp_up, w_exp_down, acc):
    with ExitStack() as ctx:
        base = 16512

        def at(name, kb, shape, dt=F32):
            return nc.alloc_sbuf_tensor_at(name, list(shape), dt, offset=base + int(kb * 1024))

        sems = {}

        def sem(name):
            sems[name] = ctx.enter_context(nc.semaphore(name))
            return sems[name]

        stage = at("stage", 0, [P, RING, 4, UW])
        whi = at("whi", 24, [P, RING, 4, UW], F32R)
        wlo = at("wlo", 48, [P, RING, 4, UW], F32R)
        hTh = at("hTh", 72, [P, KD, T], F32R)
        hTl = at("hTl", 88, [P, KD, T], F32R)
        yTh = at("yTh", 72, [P, KD, T], F32R)
        yTl = at("yTl", 88, [P, KD, T], F32R)
        xin = at("xin", 104, [P, NT, D])
        foxq = at("foxq", 104, [P, 4, T])
        foxk = at("foxk", 112, [P, 4, T])
        oAh = at("oAh", 104, [P, 4, T], F32R)
        oAl = at("oAl", 112, [P, 4, T], F32R)
        xn = at("xn", 120, [P, NT, D])
        gqk = at("gqk", 120, [P, 4, T])
        grs = at("grs", 128, [P, 4, T])
        oBh = at("oBh", 120, [P, 4, T], F32R)
        oBl = at("oBl", 128, [P, 4, T], F32R)
        gv = at("gv", 136, [P, NT, MIX])
        oCh = at("oCh", 136, [P, 4, T], F32R)
        zs = at("zs", 144, [P, NT, MIX])
        xbc = at("xbc", 152, [P, 6, T + 3])
        cpos = [164.25]

        def small(name, shape, dt=F32):
            n = int(np.prod(shape[1:])) * (2 if dt == BF16 else 4)
            t = at(name, cpos[0], shape, dt)
            cpos[0] += ((n + 63) // 64) * 64 / 1024
            return t

        ident = small("ident", [P, P])
        identb = small("identb", [P, P], BF16)
        maskq = small("maskq", [P, P], BF16)
        masks = small("masks", [P, P], BF16)
        trib = small("trib", [P, P], BF16)
        onesb = small("onesb", [P, P], BF16)
        blk64 = small("blk64", [P, P])
        ones128 = small("ones128", [P, P])
        sgni = small("sgni", [16, 16])
        sgn16 = small("sgn16", [16, 1])
        cols = small("cols", [P, 80])
        hcol = small("hcol", [P, 56])
        bias16 = small("bias16", [16, 1])
        scale16 = small("scale16", [16, 1])
        wlr = small("wlr", [48, 256])
        nbc = small("nbc", [P, MIX])
        dbc = small("dbc", [P, 8])
        rbias = small("rbias", [P, 20])
        gain1 = small("gain1", [P, 2])
        mhalf = small("mhalf", [P, 8])
        epsc = small("epsc", [P, 1])
        ssq = small("ssq", [P, NT])
        rst = small("rst", [P, NT])
        tokrow = small("tokrow", [P, NT, 32])
        dtok = small("dtok", [P, NT, 8])
        nacs = small("nacs", [P, NT, 8])
        eacs = small("eacs", [P, NT, 8])
        reset16 = small("reset16", [16, T])
        bcum_at = cpos[0]
        bcum = small("bcum", [P, 2, T])
        glam_at = cpos[0]
        glam = small("glam", [P, NT, P])
        cum16 = small("cum16", [16, T])
        tnhb = small("tnhb", [P, T])
        stt = small("stt", [P, MIX])
        top = cpos[0]
        Z0 = 187.75
        sq4 = at("sq4", Z0, [P, D])
        rows = at("rows", Z0 + 4, [NROWS, P])
        wsm = at("wsm", Z0 + 5, [P, KD, P])
        wsmh = at("wsmh", Z0 + 9, [P, KD, P], F32R)
        wsml = at("wsml", Z0 + 13, [P, KD, P], F32R)
        reset64 = at("reset64", Z0 + 17, [P, T])
        sm = at("sm", Z0, [48, T])
        smz = at("smz", Z0 + 2, [P, T])
        sme = at("sme", Z0 + 4, [P, T])
        fv = at("fv", Z0 + 12, [P, NT, MIX])
        qsq = at("qsq", Z0, [P, 2, T])
        qrs = at("qrs", Z0 + 4, [P, 2, T])
        cbt = at("cbt", Z0, [P, 2, T])
        prob = [at("prob0", Z0 + 4, [P, T]), at("prob1", Z0 + 6, [P, T]), at("prob2", glam_at, [P, T])]
        probT = at("probT", Z0 + 8, [P, 2, T])
        nmx = at("nmx", 187.25, [P, 32])
        rsum = at("rsum", 187.375, [P, 32])
        rinv = at("rinv", 187.5, [P, 32])
        assert top <= 187.25, top
        gex = at("gex", Z0, [P, 2, T])
        kend = at("kend", Z0 + 4, [P, T])
        kendT = at("kendT", Z0 + 6, [P, NT, P])
        prev = at("prev", Z0 + 8, [P, 8, P])
        gat = at("gat", Z0 + 12, [P, 2, T])
        oraw = at("oraw", Z0 + 16, [P, 2, T])
        gdec = at("gdec", 187.625, [P, 8])
        dec = at("dec", Z0, [P, 8, P])
        xdt = at("xdt", Z0 + 4, [P, MIX])
        xdt2 = at("xdt2", Z0 + 6, [P, MIX])
        ysd = at("ysd", Z0 + 8, [P, MIX])
        btok = at("btok", Z0 + 10, [P, P])
        toend = at("toend", Z0 + 10.5, [P, 8])
        cdec = at("cdec", Z0 + 10.5625, [P, 8])
        nss = at("nss", Z0 + 10.625, [P, 2])
        nrs = at("nrs", Z0 + 10.6875, [P, 2])
        blast = at("blast", Z0 + 10.75, [P, 8])
        cblk = at("cblk", bcum_at, [P, 2, T])
        oCl = at("oCl", Z0 + 12, [P, 4, T], F32R)
        yacc = at("yacc", 144, [P, KD, T])
        sg = at("sg", Z0, [P, 4, T])
        ytmp = at("ytmp", Z0 + 8, [P, 2, T])
        xr = at("xr", 104, [P, NT, D])
        x1 = at("x1", 120, [P, NT, D])
        h2T = at("h2T", 144, [P, KD, T])
        wr = at("wr", 136, [P, KD, 20])
        rt = 137.0
        rpos = [rt]

        def rout(name, shape, dt=F32):
            n = int(np.prod(shape[1:])) * (2 if dt == BF16 else 4)
            t = at(name, rpos[0], shape, dt)
            rpos[0] += ((n + 63) // 64) * 64 / 1024
            assert rpos[0] <= 144
            return t

        lg = rout("lg", [P, NT, 20])
        gmx = rout("gmx", [P, NT])
        g4 = rout("g4", [P, NT, 4])
        gv4 = rout("gv4", [P, NT, 4])
        goh = rout("goh", [P, NT, 4])
        gsum = rout("gsum", [P, NT])
        gw = rout("gw", [P, NT])
        ein16 = rout("ein16", [P, NT, 16])
        ein = rout("ein", [P, NT, 4])
        m1 = rout("m1", [P, NT])
        m2 = rout("m2", [P, NT])
        oh1 = rout("oh1", [P, NT, 4])
        oh2 = rout("oh2", [P, NT, 4])
        a1 = rout("a1", [P, NT, 16])
        a2 = rout("a2", [P, NT, 16])
        ab = rout("ab", [P, NT, 16], BF16)
        w12 = rout("w12", [P, 2, NT])
        ex2 = rout("ex2", [P, NT])
        nexp = rout("nexp", [P, 16])
        extra = rout("extra", [P, 16])
        incl = rout("incl", [P, 16])
        diff = rout("diff", [P, 16])
        slot = rout("slot", [P, NT, 16])
        over = rout("over", [P, NT, 16])
        sl12 = rout("sl12", [P, 2, NT])
        sli = rout("sli", [P, 2, NT], I32)
        ovm = rout("ovm", [P, OVF, 16])
        ove = rout("ove", [P, 8])
        one16 = rout("one16", [P, 16])
        prio = at("prio", 160, [P, 4])
        e128 = at("e128", 160.0625, [P, 16])
        iota7 = at("iota7", 160.125, [P, OVF])
        tokid = at("tokid", 160.1875, [P, NT], I32)
        entry = at("entry", 160.25, [P, 2, NT, 2], I32)
        tabi = at("tabi", 160.5, [P, ITEMS, 2], I32)
        tab = at("tab", 160.75, [P, ITEMS, 2], I32)
        ovi = at("ovi", 161, [P, 8], I32)
        pad = at("pad", 161.0625, [P, 2])
        zero = at("zero", 192, [P, D])
        gainb = at("gainb", 196, [P, D])
        xg = at("xg", 72, [P, 2, D])
        xTh = at("xTh", 80, [P, 2, KD, P], F32R)
        xTl = at("xTl", 88, [P, 2, KD, P], F32R)
        act1 = at("act1", 96, [P, DE])
        hid = at("hid", 98, [P, DE])
        hdh = at("hdh", 100, [P, 4, P], F32R)
        hdl = at("hdl", 102, [P, 4, P], F32R)
        yrow = at("yrow", 192, [P, 2, D])


        bank = [ctx.enter_context(nc.psum_tensor(f"bank{b}", [P, 512], F32)) for b in range(8)]
        h2d = nc.dram_tensor("h2rows", [T + P, D], F32).ap()
        tabd = nc.dram_tensor("slots", [ITEMS * P, 2], I32).ap()

        full = [sem(f"full{b}") for b in range(8)]
        free = [sem(f"free{b}") for b in range(8)]
        staged = [sem(f"staged{s}") for s in range(RING)]
        hi_ready, lo_ready, unit_used = sem("hi_ready"), sem("lo_ready"), sem("unit_used")
        pool_step, dve_step, act_step, idx_step = sem("pool_step"), sem("dve_step"), sem("act_step"), sem("idx_step")
        x_in = [sem(f"x_in{i}") for i in range(NT)]
        rows_in, wsm_in, par_in, bc_in = sem("rows_in"), sem("wsm_in"), sem("par_in"), sem("bc_in")
        (consts, masks_done, route_consts, ssq_done, rst_done, xn_done, cols_done, hTh_done, wsm_zero, wsmh_done,
         wsml_done, z_done, lnv_done, rows_done, toktr_done, eacs_done) = (sem(n) for n in (
             "consts", "masks_done", "route_consts", "ssq_done", "rst_done", "xn_done", "cols_done", "hTh_done",
             "wsm_zero", "wsmh_done", "wsml_done", "z_done", "lnv_done", "rows_done", "toktr_done", "eacs_done"))
        sq_done, qrs_done, qn_done, exp_done, prob_done, pv_done, oAh_done, tanh_done = (sem(n) for n in (
            "sq_done", "qrs_done", "qn_done", "exp_done", "prob_done", "pv_done", "oAh_done", "tanh_done"))
        (conv_done, ctanh_done, xbc_done, garg_done, gexp_done, kend_done, gpre_done, ors_done, ob_done, oBh_done,
         obl_done) = (sem(n) for n in ("conv_done", "ctanh_done", "xbc_done", "garg_done", "gexp_done", "kend_done",
                                       "gpre_done", "ors_done", "ob_done", "oBh_done", "obl_done"))
        glam_done = sem("glam_done")
        cblk_done, sd_arg, sd_exp, sd_y, sd_sq, sd_rst, sd_norm, oCh_done = (sem(n) for n in (
            "cblk_done", "sd_arg", "sd_exp", "sd_y", "sd_sq", "sd_rst", "sd_norm", "oCh_done"))
        y_added, yh_done, y_done = sem("y_added"), sem("yh_done"), sem("y_done")
        (xr_in, gainb_in, wr_in, x1_sq, r2_done, xn2_done, acc_in, h2_out, pad_out, tab_out, r_arg, r_exp, r_ab, r_slot,
         tab_put, tab_in) = (sem(n) for n in (
             "xr_in", "gainb_in", "wr_in", "x1_sq", "r2_done", "xn2_done", "acc_in", "h2_out", "pad_out", "tab_out", "r_arg",
             "r_exp", "r_ab", "r_slot", "tab_put", "tab_in"))
        xg_in = [sem("xg_in0"), sem("xg_in1")]
        xTh_done, hid_done, hdh_done, added = sem("xTh_done"), sem("hid_done"), sem("hdh_done"), sem("added")
        block = ctx.enter_context(nc.Block())

        B0 = [len(USES[b]) for b in range(8)]

        def whole(b):
            return bank[b][:, :]

        def width_of(u):
            return BLOCKS[u // 2][2] if u < U_GATE else UW

        def wait_unit(eng, u, m=None, ovf=False):
            if u < U_GATE:
                b, kh = divmod(u, 2)
                s = SUBS[b] - 1
                which, n = (full[s], turn(s, ("block", b)) + 1) if kh else (unit_used, b + 1)
            elif u < U_OUT:
                g, part = divmod(u - U_GATE, 3)
                which, n = ((unit_used, NB + g + 1), (full[3], turn(3, ("gate", g)) + 1),
                            (full[7], turn(7, ("proj", g)) + 1))[part]
            elif u < U_MOE:
                nh, kh = divmod(u - U_OUT, 2)
                b = 4 * nh + 3
                which, n = (full[b], turn(b, ("out", nh)) + 1) if kh else (unit_used, NB + 6 + nh + 1)
            elif u < U_MOE + 4:
                k = u - U_MOE
                which, n = ((unit_used, NB + 9), (full[0], B0[0] + 1), (unit_used, NB + 10), (full[1], B0[1] + 1))[k]
            elif u < U_OVF - 2:
                i, k = divmod(u - U_MOE - 4, 6)
                i += 1
                which, n = ((unit_used, NB + 9 + 2 * i), (full[0], B0[0] + i + 1), (full[2], B0[2] + i),
                            (full[3], B0[3] + i), (unit_used, NB + 10 + 2 * i), (full[1], B0[1] + i + 1))[k]
            elif u < U_OVF:
                b = 2 + u - (U_OVF - 2)
                which, n = full[b], B0[b] + NEXP
            else:
                w, k = divmod(u - U_OVF, 6)
                i = NEXP + w
                which, n = ((unit_used, NB + 9 + 2 * i), (full[0], B0[0] + i + 1), (unit_used, NB + 10 + 2 * i),
                            (full[1], B0[1] + i + 1), (full[2], B0[2] + i + 1), (full[3], B0[3] + i + 1))[k]
            items = 1 if ovf else 2
            eng.wait_ge(which, after(m, 2 * items if which is unit_used else items, n))

        def split_hi(act, u, m=None, ovf=False):
            s, n = u % RING, width_of(u)
            units = 6 if ovf else 12
            act.wait_ge(staged[s], after(m, 16 * units // RING, 16 * (u // RING + 1)))
            if U_OVF <= u < U_OVF + RING:
                act.wait_ge(full[u - U_OVF + 1], after(m, 1, B0[u - U_OVF + 1] + NEXP))
            elif u >= RING:
                wait_unit(act, u - RING, m, ovf)
            nc.scalar.activation(whi[:, s, :, 0:n], stage[:, s, :, 0:n], ACT.Copy).then_inc(hi_ready, 1)

        def wait_pv(eng, n):
            if n % 8 == 7:
                eng.wait_ge(full[7], turn(7, ("opair", n // 8)) + 1)
            else:
                eng.wait_ge(pv_done, n + 1 - (n + 1) // 8)

        def split_lo(dve, u, m=None, ovf=False):
            s, n = u % RING, width_of(u)
            dve.wait_ge(hi_ready, after(m, 6 if ovf else 12, u + 1))
            nc.vector.tensor_tensor(wlo[:, s, :, 0:n], stage[:, s, :, 0:n],
                                    whi[:, s, :, 0:n].bitcast(F32), ALU.subtract).then_inc(lo_ready, 1)

        @block.sync
        def _(sp):
            for i in range(NT):
                sp.dma_start(xin[:, i, :], x[i * P:(i + 1) * P, :]).then_inc(x_in[i], 16)
            for u in range(U_MOE):
                if u >= RING:
                    sp.wait_ge(lo_ready, u - RING + 1)
                n = width_of(u)
                sp.dma_start(stage[:, u % RING, :, 0:n], unit_source(u, w_in, w_branch, w_out)).then_inc(
                    staged[u % RING], 16)
                if u == U_OUT:
                    sp.wait_ge(full[7], turn(7, ("proj", 5)) + 1)
                    for i in range(NT):
                        sp.dma_start(xr[:, i, :], x[i * P:(i + 1) * P, :]).then_inc(xr_in, 16)

            def load(u, src, m=None, per=12):
                sp.wait_ge(lo_ready, after(m, per, u - RING + 1))
                sp.dma_start(stage[:, u % RING, :, :], src).then_inc(staged[u % RING], 16)

            def up_src(w, e, kh):
                if isinstance(e, int):
                    return w[e, kh * 512:(kh + 1) * 512, :].rearrange("(j p) n -> p j n", p=P)
                return w[bass.ds(e, 1), kh * 512:(kh + 1) * 512, :].rearrange("o (j p) n -> p (o j) n", p=P)

            def down_src(e, nh):
                if isinstance(e, int):
                    return w_exp_down[e, :, nh * 512:(nh + 1) * 512].rearrange("(j p) n -> p j n", p=P)
                return w_exp_down[bass.ds(e, 1), :, nh * 512:(nh + 1) * 512].rearrange(
                    "o (j p) n -> p (o j) n", p=P)

            def item(u, e, before, m=None):
                load(u, up_src(w_exp_gate, e, 0), m)
                load(u + 1, up_src(w_exp_gate, e, 1), m)
                if before is not None:
                    load(u + 2, down_src(before, 0), m)
                    load(u + 3, down_src(before, 1), m)
                    u += 2
                load(u + 2, up_src(w_exp_up, e, 0), m)
                load(u + 3, up_src(w_exp_up, e, 1), m)

            item(U_MOE, 0, None)
            with sp.Fori(0, 7) as m:
                item(U_MOE + 4, m * 2 + 1, m * 2, m)
                item(U_MOE + 10, m * 2 + 2, m * 2 + 1, m)
            item(U_MOE + 88, 15, 14)
            load(U_MOE + 94, down_src(15, 0))
            load(U_MOE + 95, down_src(15, 1))
            sp.wait_ge(r_slot, 2)
            count = sp.value_load(ovi[0:1, 0:1], min_val=0, max_val=OVF)
            with sp.If(count > 0):
                with sp.Fori(0, count) as m:
                    e = sp.value_load(ovi[0:1, bass.ds(m + 1, 1)], min_val=0, max_val=NEXP - 1)
                    load(U_OVF, up_src(w_exp_gate, e, 0), m, 6)
                    load(U_OVF + 1, up_src(w_exp_gate, e, 1), m, 6)
                    load(U_OVF + 2, up_src(w_exp_up, e, 0), m, 6)
                    load(U_OVF + 3, up_src(w_exp_up, e, 1), m, 6)
                    load(U_OVF + 4, down_src(e, 0), m, 6)
                    load(U_OVF + 5, down_src(e, 1), m, 6)
                sp.nop()

        @block.gpsimd
        def _(pool):
            step = Serial(pool, pool_step)
            g = nc.gpsimd

            def select(out, op, fill, b, pattern, cm, sem=None, n=None):
                step(g.affine_select(out=out, in_=out, compare_op=op, fill=fill, base=b,
                                     pattern=pattern, channel_multiplier=cm), sem, n)

            step(g.memset(wsm[:, :, :], 0.0), wsm_zero, 1)
            step(g.memset(scale16[:, :], 0.0), wsm_zero, 2)
            step(g.memset(ident[:, :], 0.0))
            select(ident[:, :], ALU.not_equal, 1.0, 0, [[-1, P]], 1, consts, 1)
            step(g.memset(mhalf[:, :], -0.5))
            step(g.memset(epsc[:, :], EPS))
            step(g.memset(sgn16[:, :], 1.0))
            select(sgn16[:, :], ALU.is_ge, -1.0, 7, [[0, 1]], -1, consts, 2)
            pool.wait_ge(ssq_done, NT)
            step(g.tensor_scalar(ssq[:, :], ssq[:, :], 1.0 / D, EPS, ALU.mult, ALU.add))
            step(g.tensor_tensor(rst[:, :], ssq[:, :], mhalf[:, 0:NT], ALU.pow), rst_done, 1)
            step(g.memset(reset16[:, :], 1.0))
            select(reset16[:, :].rearrange("p (i t) -> p i t", t=P)[:, :, 0:1], ALU.is_ge, 0.0, 7,
                   [[0, NT], [0, 1]], -1)
            step(g.memset(reset64[:, :], 1.0))
            step(g.memset(reset64[:, :].rearrange("p (c t) -> p c t", t=CHUNK)[:, :, 0:1], 0.0))
            step(g.memset(blk64[:, :], 0.0))
            step(g.memset(blk64[0:64, 0:64], 1.0 / 64))
            step(g.memset(blk64[64:128, 64:128], 1.0 / 64))
            step(g.memset(sgni[:, :], 0.0))
            select(sgni[:, 0:8], ALU.not_equal, -1.0, 0, [[-1, 8]], 1)
            select(sgni[:, 8:16], ALU.not_equal, 1.0, -8, [[-1, 8]], 1)
            step(g.memset(maskq[:, :], 0.0))
            select(maskq[:, :], ALU.is_ge, NEGBIG, 0, [[-1, P]], 1)
            step(g.memset(masks[:, :], 0.0))
            select(masks[:, :], ALU.is_ge, NEGBIG, 0, [[1, P]], -1)
            step(g.memset(ones128[:, :], 1.0 / 128))
            step(g.memset(onesb[:, :], 1.0))
            step(g.memset(trib[:, :], 1.0))
            select(trib[:, :], ALU.is_gt, 0.0, 0, [[1, P]], -1)
            step(g.memset(xbc[:, :, 0:3], 0.0))
            step(g.tensor_copy(identb[:, :], ident[:, :]), masks_done, 1)
            pool.wait_ge(full[6], turn(6, ("turn", FOX_H * NT - 1)) + 1)
            step(g.memset(glam[:, :, :], 1.0))
            select(glam[:, :, :], ALU.is_ge, 0.0, 0, [[0, NT], [1, P]], -1)
            select(glam[:, :, 64:128], ALU.is_ge, 0.0, -64, [[0, NT], [0, 64]], 1, glam_done, 1)
            for i in range(NT):
                pool.wait_ge(sd_sq, i + 1)
                step(g.tensor_scalar(nss[:, :], nss[:, :], 1.0 / 256, EPS, ALU.mult, ALU.add))
                step(g.tensor_tensor(nrs[:, :], nss[:, :], mhalf[:, 0:2], ALU.pow), sd_rst, i + 1)
            pool.wait_ge(free[5], turn(5, ("yt", NT - 1)) + 1)
            for c in range(4):
                step(g.memset(prio[:, c:c + 1], float(4 - c)))
            step(g.iota(e128[:, :], pattern=[[P, 16]], base=0, channel_multiplier=0,
                        allow_small_or_imprecise_dtypes=True))
            step(g.iota(iota7[:, :], pattern=[[1, OVF]], base=0, channel_multiplier=0,
                        allow_small_or_imprecise_dtypes=True))
            step(g.iota(tokid[:, :], pattern=[[P, NT]], base=0, channel_multiplier=1))
            step(g.memset(tabi[:, :, :], 0))
            step(g.iota(tabi[:, :, 0:1], pattern=[[0, ITEMS], [0, 1]], base=T, channel_multiplier=1))
            g.dma_start(tabd.rearrange("(n p) c -> p n c", p=P), tabi[:, :, :]).then_inc(tab_out, 16)
            for k in range(2):
                step(g.tensor_copy(entry[:, k, :, 0:1].rearrange("p i o -> p (i o)"), tokid[:, :]), route_consts, k + 1)
            pool.wait_ge(y_done, KD)
            step(g.memset(zero[:, :], 0.0))
            g.dma_start(h2d[T:T + P, :], zero[:, :]).then_inc(pad_out, 16)
            g.dma_start(acc[T:T + P, :], zero[:, :]).then_inc(pad_out, 16)
            pool.wait_ge(x1_sq, NT)
            step(g.tensor_scalar(ssq[:, :], ssq[:, :], 1.0 / D, EPS, ALU.mult, ALU.add))
            step(g.tensor_tensor(rst[:, :], ssq[:, :], mhalf[:, 0:NT], ALU.pow), r2_done, 1)
            pool.wait_ge(r_slot, 1)
            pool.wait_ge(tab_out, 16)
            for k in range(2):
                for i in range(NT):
                    g.indirect_dma_start(tabd, bass.IndirectOffsetOnAxis(sli[:, k, i:i + 1], 0),
                                         entry[:, k, i, :], None).then_inc(tab_put, 16)
            pool.wait_ge(tab_put, 16 * 8)
            g.dma_start(tab[:, :, :], tabd.rearrange("(n p) c -> p n c", p=P)).then_inc(tab_in, 16)
            pool.wait_ge(tab_in, 16)
            pool.wait_ge(h2_out, 16 * NT)
            pool.wait_ge(pad_out, 32)

            def gather(i, par):
                g.indirect_dma_start(xg[:, par, :], None, h2d,
                                     bass.IndirectOffsetOnAxis(tab[:, i, 0:1], 0)).then_inc(xg_in[par], 16)

            def scatter(i, par):
                pool.wait_ge(free[2], B0[2] + i + 1)
                pool.wait_ge(free[3], B0[3] + i + 1)
                g.indirect_dma_start(acc, bass.IndirectOffsetOnAxis(tab[:, i, 0:1], 0), yrow[:, par, :], None,
                                     compute_op=ALU.add).then_inc(added, 16)

            gather(0, 0)
            gather(1, 1)
            pool.wait_ge(acc_in, 16 * NT)
            for i in range(NEXP):
                if i:
                    pool.wait_ge(added, 16 * i)
                if i + 2 < NEXP:
                    pool.wait_ge(full[5], B0[5] + i + 1)
                    gather(i + 2, i % 2)
                scatter(i, i % 2)
            pool.wait_ge(added, 16 * NEXP)
            pool.wait_ge(r_slot, 2)
            count = pool.value_load(ovi[0:1, 0:1], min_val=0, max_val=OVF)
            for j in range(OVF):
                with pool.If(count > j):
                    pool.wait_ge(full[5], B0[5] + NEXP + j)
                    gather(NEXP + j, 0)
                    scatter(NEXP + j, 0)
                    pool.wait_ge(added, 16 * (NEXP + j + 1))

        @block.scalar
        def _(act):
            a = nc.scalar
            step = Serial(act, act_step)
            for r0, src in ((R_NM, norm_mix.rearrange("(r p) -> r p", p=P)),
                            (R_NF, norm_ffn.rearrange("(r p) -> r p", p=P)),
                            (R_BG, b_branch_gate.rearrange("b (r p) -> (b r) p", p=P)),
                            (R_CW, ssm_conv_w.rearrange("j (r p) -> (j r) p", p=P)),
                            (R_CB, ssm_conv_b.rearrange("(r p) -> r p", p=P)),
                            (R_GB, gla_b_gate.rearrange("(r p) -> r p", p=P)),
                            (R_GO, gla_out_norm.rearrange("(r p) -> r p", p=P))):
                act.dma_start(rows[r0:r0 + src.shape[0], :], src).then_inc(rows_in, 16)
            for r0, src in ((R_FQ, fox_q_norm), (R_FK, fox_k_norm)):
                for half in range(2):
                    act.dma_start(rows[r0:r0 + 1, half * 64:half * 64 + 64],
                                  src.rearrange("(a n) -> a n", a=1)).then_inc(rows_in, 16)
            act.wait_ge(wsm_zero, 2)
            for c0, n, dst in ((C_FF, 8, 0), (C_DT, 8, 8), (C_GLR, 16, 32)):
                act.dma_start(wsm[:, :, dst:dst + n],
                              w_in[:, c0:c0 + n].rearrange("(k p) n -> p k n", p=P)).then_inc(wsm_in, 16)
            act.dma_start(bias16[0:8, :], fox_f_bias.rearrange("(n a) -> n a", a=1)).then_inc(par_in, 16)
            act.dma_start(bias16[8:16, :], ssm_dt_bias.rearrange("(n a) -> n a", a=1)).then_inc(par_in, 16)
            act.dma_start(scale16[8:16, :], ssm_a_log.rearrange("(n a) -> n a", a=1)).then_inc(par_in, 16)
            act.dma_start(wlr[32:48, :], gla_w_lr).then_inc(par_in, 16)
            act.dma_start(nbc[:, :], ssm_out_norm.partition_broadcast(P)).then_inc(bc_in, 16)
            act.dma_start(dbc[:, :], ssm_d.partition_broadcast(P)).then_inc(bc_in, 16)
            act.dma_start(rbias[:, 0:4], b_router_grp.partition_broadcast(P)).then_inc(bc_in, 16)
            act.dma_start(rbias[:, 4:20], b_router_exp.partition_broadcast(P)).then_inc(bc_in, 16)
            for i in range(NT):
                act.wait_ge(x_in[i], 16)
                step(a.activation(sq4[:, :], xin[:, i, :], ACT.Square, accum_out=ssq[:, i:i + 1]), ssq_done, i + 1)
            act.wait_ge(par_in, 16 * 4)
            step(a.activation(scale16[:, :], scale16[:, :], ACT.Exp))
            act.wait_ge(wsm_in, 48)
            a.activation(wsmh[:, :, :], wsm[:, :, :], ACT.Copy).then_inc(wsmh_done, 1)
            split_hi(act, 0)
            split_hi(act, 1)
            act.wait_ge(cols_done, 1)
            for k in range(KD):
                act.wait_ge(full[k], turn(k, "hT") + 1)
                a.activation(hTh[:, k, :], whole(k), ACT.Copy,
                             scale=cols[:, R_NM + k:R_NM + k + 1]).then_inc(hTh_done, 1)

            tanhs = 0
            tanh_read = None
            for it in SCHED:
                kind = it[0]
                if kind == "small":
                    act.wait_ge(z_done, 1)
                    step(a.activation(sme[0:16, :], smz[0:16, :], ACT.Abs))
                    step(a.activation(sme[0:16, :], sme[0:16, :], ACT.Exp, scale=-1.0))
                    step(a.activation(sme[0:16, :], sme[0:16, :], ACT.Ln, bias=1.0), lnv_done, 1)
                elif kind == "loga":
                    pr = it[1]
                    act.wait_ge(free[5 + pr], turn(5 + pr, it) + 1)
                    act.wait_ge(rows_done, 1 + pr)
                    step(a.activation(sme[:, :], smz[:, :], ACT.Abs))
                    step(a.activation(sme[:, :], sme[:, :], ACT.Exp, scale=-1.0))
                    step(a.activation(sme[:, :], sme[:, :], ACT.Ln, bias=1.0), lnv_done, 2 + pr)
                elif kind == "tokrows":
                    act.wait_ge(toktr_done, 1)
                    step(a.activation(eacs[:, :, :], tokrow[:, :, 24:32], ACT.Exp), eacs_done, 1)
                elif kind == "piece":
                    _, b, kh, s, q = it
                    name = BLOCKS[b][0]
                    if q == 0 or kh == 0 or name in ("fq", "fk"):
                        continue
                    n = turn(s, ("block", b)) + 1
                    act.wait_ge(full[s], n)
                    if name in ("gr", "z"):
                        act.wait_ge(*(tanh_read or (xbc_done, 6)))
                        tanhs += 1
                        tanh_read = (free[s], n)
                        step(a.activation(tnhb[:, :], whole(s), ACT.Tanh, scale=0.5), tanh_done, tanhs)
                    elif name in ("xs", "bc"):
                        act.wait_ge(masks_done, 1)
                        dst = xbc[:, s if name == "xs" else 4 + s, 3:3 + T]
                        step(a.activation(dst, whole(s), ACT.Copy), free[s], n)
                    else:
                        dst = {"fv": fv, "gqk": gqk, "gv": gv}[name][:, s, :]
                        scale = GLA_DK ** -0.5 if name == "gqk" and s < 2 else 1.0
                        step(a.activation(dst, whole(s), ACT.Copy, scale=scale), free[s], n)
                elif kind == "square":
                    m = it[1]
                    b = 4 + m % 2
                    act.wait_ge(free[m % 4], turn(m % 4, ("block", m // 4)) + 1)
                    if m >= 2:
                        act.wait_ge(full[b], turn(b, ("qnorm", m - 2)) + 1)
                    step(a.activation(qsq[:, m % 2, :], (foxq if m < 4 else foxk)[:, m % 4, :], ACT.Square),
                         sq_done, m + 1)
                elif kind == "qnorm":
                    m = it[1]
                    b = 4 + m % 2
                    act.wait_ge(full[b], turn(b, it) + 1)
                    if m >= 2:
                        act.wait_ge(qn_done, m - 1)
                    step(a.activation(qrs[:, m % 2, :], whole(b), ACT.Ln, bias=epsc[:, 0:1]), free[b], turn(b, it) + 1)
                    step(a.activation(qrs[:, m % 2, :], qrs[:, m % 2, :], ACT.Exp, scale=-0.5), qrs_done, m + 1)
                elif kind == "score":
                    n = it[1]
                    b = 4 + n % 2
                    w = (n % NT + 1) * P
                    act.wait_ge(free[b], turn(b, it) + 1)
                    step(a.activation(prob[n % 3][:, 0:w], prob[n % 3][:, 0:w], ACT.Exp, scale=-1.0,
                                      bias=nmx[:, n:n + 1], accum_out=rsum[:, n:n + 1]), exp_done, n + 1)
                elif kind == "turn":
                    n = it[1]
                    w = (n % NT + 1) * P
                    act.wait_ge(full[6], turn(6, it) + 1)
                    if n >= 2:
                        wait_pv(act, n - 2)
                    step(a.activation(probT[:, n % 2, 0:w], bank[6][:, 0:w], ACT.Copy), free[6], turn(6, it) + 1)
                elif kind == "pv" and it[1] % 8 == 7:
                    pr = it[1] // 8
                    act.wait_ge(full[7], turn(7, ("opair", pr)) + 1)
                    step(a.activation(oAh[:, pr, :], whole(7), ACT.Copy), oAh_done, pr + 1)
                elif kind == "hi":
                    split_hi(act, it[1])
                elif kind == "squash":
                    s = it[1]
                    act.wait_ge(conv_done, s + 1)
                    if s:
                        act.wait_ge(xbc_done, s)
                    step(a.activation(tnhb[:, :], stt[:, :], ACT.Tanh), ctanh_done, s + 1)
                elif kind == "gprep":
                    pr = it[1]
                    act.wait_ge(xbc_done, 6)
                    if pr:
                        act.wait_ge(obl_done, 2)
                    step(a.activation(gex[:, 0, :], bcum[:, pr, :], ACT.Exp), gexp_done, 3 * pr + 1)
                    step(a.activation(gex[:, 1, :], bcum[:, pr, :], ACT.Exp, scale=-1.0), gexp_done, 3 * pr + 2)
                    act.wait_ge(garg_done, pr + 1)
                    step(a.activation(kend[:, :], kend[:, :], ACT.Exp), gexp_done, 3 * pr + 3)
                    act.wait_ge(full[4], turn(4, it) + 1)
                    if pr:
                        act.wait_ge(full[6], turn(6, ("kv", 0, 1)) + 1)
                        act.wait_ge(full[5], turn(5, ("kv", 0, 0)) + 1)
                    step(a.activation(kendT[:, :, :], whole(4).rearrange("p (i t) -> p i t", t=P), ACT.Copy),
                         free[4], turn(4, it) + 1)
                elif kind == "ghead":
                    h = it[1]
                    b = 6 + h % 2
                    act.wait_ge(full[b], turn(b, ("go", h)) + 1)
                    act.wait_ge(gpre_done, h // 2 + 1)
                    step(a.activation(oraw[:, h % 2, :], whole(b), ACT.Copy))
                    step(a.activation(gex[:, h % 2, :], whole(b), ACT.Square), free[b], turn(b, ("go", h)) + 1)
                elif kind == "gout":
                    h = it[1]
                    b = 4 + h % 2
                    act.wait_ge(full[b], turn(b, it) + 1)
                    step(a.activation(gex[:, h % 2, :], whole(b), ACT.Ln, bias=epsc[:, 0:1]), free[b], turn(b, it) + 1)
                    step(a.activation(gex[:, h % 2, :], gex[:, h % 2, :], ACT.Exp, scale=-0.5), ors_done, h + 1)
                    act.wait_ge(ob_done, h + 1)
                    step(a.activation(oBh[:, gslot(h), :], oraw[:, h % 2, :], ACT.Copy), oBh_done, h + 1)
                elif kind == "ssd":
                    i = it[1]
                    act.wait_ge(sd_arg, i + 1)
                    act.wait_ge(eacs_done, 1)
                    for h in range(SSM_H):
                        b = 4 + h // 4
                        ins = a.activation(dec[:, h, :], bank[b][:, (h % 4) * P:(h % 4) * P + P], ACT.Exp,
                                           bias=nacs[:, i, h:h + 1])
                        if h % 4 == 3:
                            step(ins, free[b], turn(b, ("bca" if b == 4 else "bcb", i)) + 1)
                        else:
                            step(ins)
                    step(a.activation(cdec[:, :], blast[:, :], ACT.Exp))
                    step(a.activation(toend[:, :], toend[:, :], ACT.Exp), sd_exp, i + 1)
                    act.wait_ge(sd_y, i + 1)
                    for gg in range(SSM_G):
                        step(a.activation(xdt[:, 256 * gg:256 * gg + 256], ysd[:, 256 * gg:256 * gg + 256], ACT.Square,
                                          accum_out=nss[:, gg:gg + 1]), *((sd_sq, i + 1) if gg else ()))
                    act.wait_ge(full[5], turn(5, ("yt", i)) + 1)
                    step(a.activation(oCh[:, :, i * P:(i + 1) * P], whole(5).rearrange("p (s t) -> p s t", t=P),
                                      ACT.Copy), oCh_done, i + 1)

            for g in range(6):
                dh, r = divmod(g, 3)
                u = U_GATE + 3 * g
                split_hi(act, u + 2)
                split_hi(act, u + 3)
                for s in range(4):
                    act.wait_ge(full[s], turn(s, ("gate", g)) + 1)
                    if g:
                        act.wait_ge(free[4 + s], turn(4 + s, ("proj", g - 1)) + 1)
                    c = r * 8 + dh * 4 + s
                    step(a.activation(sg[:, s, :], whole(s), ACT.Tanh, scale=0.5, bias=hcol[:, c:c + 1]),
                         free[s], turn(s, ("gate", g)) + 1)
                split_hi(act, u + 4)
            act.wait_ge(full[7], turn(7, ("proj", 5)) + 1)
            for k in range(KD):
                act.wait_ge(y_added, k + 1)
                step(a.activation(yTh[:, k, :], yacc[:, k, :], ACT.Copy, scale=0.5), yh_done, k + 1)
            act.wait_ge(y_added, KD)
            act.dma_start(gainb[:, :], norm_ffn.partition_broadcast(P)).then_inc(gainb_in, 16)
            act.dma_start(wr[:, :, 0:4], w_router_grp.rearrange("(k p) n -> p k n", p=P)).then_inc(wr_in, 16)
            act.dma_start(wr[:, :, 4:20], w_router_exp.rearrange("(k p) n -> p k n", p=P)).then_inc(wr_in, 16)
            for q in range(4):
                split_hi(act, U_OUT + 2 + q)
            for i in range(NT):
                act.wait_ge(free[4 + i], turn(4 + i, ("out", 1)) + 1)
                step(a.activation(sq4[:, :], x1[:, i, :], ACT.Square, accum_out=ssq[:, i:i + 1]), x1_sq, i + 1)
                act.dma_start(acc[i * P:(i + 1) * P, :], x1[:, i, :]).then_inc(acc_in, 16)
            for i in range(NT):
                act.wait_ge(xn2_done, i + 1)
                act.dma_start(h2d[i * P:(i + 1) * P, :], xr[:, i, :]).then_inc(h2_out, 16)
            for k in range(4):
                act.wait_ge(full[k], turn(k, "h2T") + 1)
                step(a.activation(h2T[:, k, :], whole(k), ACT.Copy), free[k], turn(k, "h2T") + 1)
            act.wait_ge(r_arg, 1)
            step(a.activation(g4[:, :, :], g4[:, :, :], ACT.Exp), r_exp, 1)
            act.wait_ge(r_arg, 2)
            step(a.activation(ex2[:, :], ex2[:, :], ACT.Exp), r_exp, 2)
            act.wait_ge(tab_in, 16)
            act.wait_ge(h2_out, 16 * NT)
            act.wait_ge(acc_in, 16 * NT)
            act.wait_ge(pad_out, 32)

            def x_hi(n, par, m=None, per=2):
                for half in range(2):
                    b = 4 + half
                    act.wait_ge(full[b], after(m, per, B0[b] + n + 1))
                    a.activation(xTh[:, par, 4 * half:4 * half + 4, :], whole(b).rearrange("p (j t) -> p j t", t=P),
                                 ACT.Copy).then_inc(xTh_done, 1)

            def hid_hi(n, m=None, per=2):
                act.wait_ge(full[6], after(m, per, B0[6] + n + 1))
                a.activation(hdh[:, :, :], whole(6).rearrange("p (j t) -> p j t", t=P), ACT.Copy).then_inc(hdh_done, 1)

            def silu(n, m=None, per=2):
                act.wait_ge(full[0], after(m, per, B0[0] + n + 1))
                if n:
                    act.wait_ge(free[1], after(m, per, B0[1] + n))
                a.activation(act1[:, :], whole(0), ACT.Silu).then_inc(free[0], 1)

            def rows_out(n, half, par, m=None, per=2, step_of_m=2):
                b = 2 + half
                act.wait_ge(full[b], after(m, per, B0[b] + n + 1))
                if n >= 2:
                    act.wait_ge(added, after(m, 16 * per, 16 * (n - 1 if n < NEXP else n)))
                if m is not None:
                    a.activation(pad[:, half:half + 1], epsc[:, 0:1], ACT.Copy)
                w = tab[:, n, 1:2] if m is None else tab[:, bass.ds(m * step_of_m + n, 1), 1:2].rearrange("p a b -> p (a b)")
                a.activation(yrow[:, par, half * 512:half * 512 + 512], whole(b), ACT.Copy,
                             scale=w.bitcast(F32)).then_inc(free[b], 1)

            def item(n, u, m=None):
                split_hi(act, u + 2, m)
                hid_hi(n - 1, m)
                split_hi(act, u + 3, m)
                silu(n, m)
                split_hi(act, u + 4, m)
                rows_out(n - 1, 0, (n - 1) % 2, m)
                split_hi(act, u + 5, m)
                rows_out(n - 1, 1, (n - 1) % 2, m)
                if n < NEXP - 1:
                    x_hi(n + 1, (n + 1) % 2, m)
                split_hi(act, u + 6, m)
                split_hi(act, u + 7, m)

            x_hi(0, 0)
            u = U_MOE
            split_hi(act, u + 2)
            split_hi(act, u + 3)
            silu(0)
            x_hi(1, 1)
            split_hi(act, u + 4)
            split_hi(act, u + 5)
            item(1, u + 4)
            item(2, u + 10)
            with act.Fori(1, 7) as m:
                item(1 + 2, u + 4 + 12, m - 1)
                item(2 + 2, u + 10 + 12, m - 1)
            item(15, u + 88)
            hid_hi(15)
            rows_out(15, 0, 1)
            rows_out(15, 1, 1)
            act.wait_ge(r_slot, 2)
            count = act.value_load(ovi[0:1, 0:1], min_val=0, max_val=OVF)
            with act.If(count > 0):
                with act.Fori(0, count) as m:
                    u = U_OVF
                    x_hi(NEXP, 0, m, 1)
                    for q in range(4):
                        split_hi(act, u + q, m, True)
                    silu(NEXP, m, 1)
                    split_hi(act, u + 4, m, True)
                    split_hi(act, u + 5, m, True)
                    hid_hi(NEXP, m, 1)
                    rows_out(NEXP, 0, 0, m, 1, 1)
                    rows_out(NEXP, 1, 0, m, 1, 1)
                act.nop()

        @block.vector
        def _(dve):
            v = nc.vector
            step = Serial(dve, dve_step)
            dve.wait_ge(rst_done, 1)
            for i in range(NT):
                dve.wait_ge(x_in[i], 16)
                step(v.tensor_scalar(xn[:, i, :], xin[:, i, :], rst[:, i:i + 1], None, ALU.mult), xn_done, i + 1)
            dve.wait_ge(full[0], 1)
            step(v.tensor_copy(cols[:, 0:NROWS], bank[0][:, 0:NROWS]), free[0], 1)
            step(v.tensor_scalar(hcol[:, 0:54], cols[:, R_BG:R_BG + 54], 0.5, None, ALU.mult))
            step(v.tensor_scalar(gain1[:, 0:1], cols[:, R_GO:R_GO + 1], 0.5, None, ALU.mult))
            step(v.tensor_scalar(gain1[:, 1:2], cols[:, R_FQ:R_FQ + 1], FOX_HD ** -0.5, None, ALU.mult), cols_done, 1)
            dve.wait_ge(wsmh_done, 1)
            step(v.tensor_tensor(wsml[:, :, :], wsm[:, :, :], wsmh[:, :, :].bitcast(F32), ALU.subtract), wsml_done, 1)
            split_lo(dve, 0)
            split_lo(dve, 1)
            for k in range(KD):
                dve.wait_ge(hTh_done, k + 1)
                step(v.scalar_tensor_tensor(out=hTl[:, k, :], in0=whole(k), scalar=cols[:, R_NM + k:R_NM + k + 1],
                                            in1=hTh[:, k, :].bitcast(F32), op0=ALU.mult, op1=ALU.subtract),
                     free[k], turn(k, "hT") + 1)

            def logsig(z, e, n):
                dve.wait_ge(lnv_done, n)
                step(v.scalar_tensor_tensor(out=z, in0=z, scalar=0.0, in1=e, op0=ALU.min, op1=ALU.subtract))

            def per_head(ap):
                return ap.unsqueeze(2).to_broadcast([P, SSM_H, 64])

            def heads(ap):
                return ap.rearrange("p (h d) -> p h d", d=64)

            tanhs = 0
            for it in SCHED:
                kind = it[0]
                if kind == "small":
                    dve.wait_ge(full[4], turn(4, "small") + 1)
                    dve.wait_ge(par_in, 16 * 4)
                    dve.wait_ge(consts, 2)
                    step(v.tensor_scalar(smz[0:16, :], bank[4][0:16, :], bias16[:, 0:1], sgn16[:, 0:1], ALU.add, ALU.mult),
                         z_done, 1)
                    step(v.tensor_copy(sm[32:48, :], bank[4][32:48, :]), free[4], turn(4, "small") + 1)
                    dve.wait_ge(lnv_done, 1)
                    step(v.scalar_tensor_tensor(out=sm[0:16, :], in0=smz[0:16, :], scalar=0.0, in1=sme[0:16, :],
                                                op0=ALU.min, op1=ALU.subtract))
                    dve.wait_ge(masks_done, 1)
                    step(v.tensor_scalar(sme[0:16, :], sm[0:16, :], scale16[:, 0:1], None, ALU.mult))
                    step(v.tensor_tensor_scan(cum16[:, :], reset16[:, :], sme[0:16, :], 0.0, ALU.mult, ALU.add),
                         rows_done, 1)
                elif kind == "loga":
                    pr = it[1]
                    b = 5 + pr
                    dve.wait_ge(full[b], turn(b, it) + 1)
                    step(v.tensor_scalar(smz[:, :], whole(b), cols[:, R_GB + pr:R_GB + pr + 1], None, ALU.add),
                         free[b], turn(b, it) + 1)
                    logsig(smz[:, :], sme[:, :], 2 + pr)
                    step(v.tensor_scalar(smz[:, :], smz[:, :], 1.0 / 16.0, None, ALU.mult))
                    step(v.tensor_tensor_scan(bcum[:, pr, :], reset64[:, :], smz[:, :], 0.0, ALU.mult, ALU.add),
                         rows_done, 2 + pr)
                elif kind == "tokrows":
                    dve.wait_ge(full[7], turn(7, it) + 1)
                    step(v.tensor_copy(tokrow[:, :, :], bank[7][:, 0:128].rearrange("p (i c) -> p i c", c=32)),
                         free[7], turn(7, it) + 1)
                    step(v.tensor_scalar(dtok[:, :, :], tokrow[:, :, 8:16], -1.0, None, ALU.mult))
                    step(v.tensor_scalar(nacs[:, :, :], tokrow[:, :, 24:32], -1.0, None, ALU.mult), toktr_done, 1)
                elif kind == "piece":
                    _, b, kh, s, q = it
                    name = BLOCKS[b][0]
                    if q == 0 or kh == 0 or name not in ("fq", "fk", "gr", "z"):
                        continue
                    n = turn(s, ("block", b)) + 1
                    if name in ("fq", "fk"):
                        dve.wait_ge(full[s], n)
                        step(v.tensor_copy((foxq if name == "fq" else foxk)[:, s, :], whole(s)), free[s], n)
                    else:
                        tanhs += 1
                        dve.wait_ge(tanh_done, tanhs)
                        step(v.scalar_tensor_tensor(out=(grs if name == "gr" else zs)[:, s, :], in0=tnhb[:, :], scalar=1.0,
                                                    in1=whole(s), op0=ALU.add, op1=ALU.mult), free[s], n)
                elif kind == "qnorm":
                    m = it[1]
                    dve.wait_ge(qrs_done, m + 1)
                    q = (foxq if m < 4 else foxk)[:, m % 4, :]
                    gain = gain1[:, 1:2] if m < 4 else cols[:, R_FK:R_FK + 1]
                    step(v.scalar_tensor_tensor(out=q, in0=q, scalar=gain, in1=qrs[:, m % 2, :],
                                                op0=ALU.mult, op1=ALU.mult), qn_done, m + 1)
                elif kind == "cb":
                    h = it[1]
                    dve.wait_ge(full[6], turn(6, it) + 1)
                    step(v.tensor_copy(cbt[:, h % 2, :], whole(6)), free[6], turn(6, it) + 1)
                elif kind == "score":
                    n = it[1]
                    b = 4 + n % 2
                    w = (n % NT + 1) * P
                    dve.wait_ge(full[b], turn(b, it) + 1)
                    if n >= 3:
                        dve.wait_ge(full[6], turn(6, ("turn", n - 3)) + 1)
                    step(v.tensor_tensor_reduce(prob[n % 3][:, 0:w], bank[b][:, 0:w], cbt[:, (n // NT) % 2, 0:w],
                                                -1.0, 3.0e38, ALU.add, ALU.min, nmx[:, n:n + 1]), free[b], turn(b, it) + 1)
                elif kind == "lo":
                    split_lo(dve, it[1])
                elif kind == "norm":
                    n = it[1]
                    w = (n % NT + 1) * P
                    dve.wait_ge(exp_done, n + 1)
                    step(v.reciprocal(rinv[:, n:n + 1], rsum[:, n:n + 1]))
                    step(v.tensor_scalar(prob[n % 3][:, 0:w], prob[n % 3][:, 0:w], rinv[:, n:n + 1], None, ALU.mult),
                         prob_done, n + 1)
                elif kind == "pv" and it[1] % 8 == 7:
                    pr = it[1] // 8
                    dve.wait_ge(oAh_done, pr + 1)
                    step(v.tensor_tensor(oAl[:, pr, :], whole(7), oAh[:, pr, :].bitcast(F32), ALU.subtract),
                         free[7], turn(7, ("opair", pr)) + 1)
                elif kind == "conv":
                    s = it[1]
                    dve.wait_ge(masks_done, 1)
                    dve.wait_ge(free[s % 4], turn(s % 4, ("block", 3 + s // 4)) + 1)
                    c = stt[:, :]
                    step(v.tensor_scalar(c, xbc[:, s, 0:T], hcol[:, 24 + s:25 + s], hcol[:, 48 + s:49 + s],
                                         ALU.mult, ALU.add))
                    for j in range(1, SSM_CONV):
                        w = hcol[:, 24 + 6 * j + s:25 + 6 * j + s]
                        ins = v.scalar_tensor_tensor(out=c, in0=xbc[:, s, j:j + T], scalar=w, in1=c,
                                                     op0=ALU.mult, op1=ALU.add)
                        step(ins, *((conv_done, s + 1) if j == SSM_CONV - 1 else ()))
                elif kind == "squash":
                    s = it[1]
                    dve.wait_ge(ctanh_done, s + 1)
                    step(v.scalar_tensor_tensor(out=xbc[:, s, 3:3 + T], in0=tnhb[:, :], scalar=1.0, in1=stt[:, :],
                                                op0=ALU.add, op1=ALU.mult), xbc_done, s + 1)
                elif kind == "gprep":
                    pr = it[1]
                    q, k = gqk[:, pr, :], gqk[:, 2 + pr, :]
                    bc = bcum[:, pr, :].rearrange("p (c t) -> p c t", t=CHUNK)
                    if pr:
                        dve.wait_ge(full[4], turn(4, ("gprep", 0)) + 1)
                    else:
                        dve.wait_ge(full[7], turn(7, ("opair", 3)) + 1)
                        step(v.memset(gat[:, :, :], 0.0))
                    step(v.tensor_tensor(kend[:, :].rearrange("p (c t) -> p c t", t=CHUNK),
                                         bc[:, :, CHUNK - 1:CHUNK].to_broadcast([P, 8, CHUNK]), bc, ALU.subtract),
                         garg_done, pr + 1)
                    dve.wait_ge(gexp_done, 3 * pr + 3)
                    step(v.tensor_tensor(kend[:, :], kend[:, :], k, ALU.mult), kend_done, pr + 1)
                    step(v.tensor_tensor(k, k, gex[:, 1, :], ALU.mult))
                    step(v.tensor_copy(gdec[:, :].unsqueeze(2),
                                       gex[:, 0, :].rearrange("p (c t) -> p c t", t=CHUNK)[:, :, CHUNK - 1:CHUNK]))
                    step(v.tensor_tensor(q, q, gex[:, 0, :], ALU.mult), gpre_done, pr + 1)
                elif kind == "kv":
                    pr = it[1]
                    dve.wait_ge(full[5], turn(5, ("kv", pr, 0)) + 1)
                    dve.wait_ge(full[6], turn(6, ("kv", pr, 1)) + 1)
                    if pr:
                        for h in range(2):
                            dve.wait_ge(full[6 + h], turn(6 + h, ("go", h)) + 1)
                    for c in range(7):
                        b = 5 + c % 2
                        kv = bank[b][:, (c // 2) * P:(c // 2) * P + P]
                        if c == 0:
                            ins = v.tensor_copy(prev[:, 1, :], kv)
                        else:
                            ins = v.scalar_tensor_tensor(out=prev[:, c + 1, :], in0=prev[:, c, :], scalar=gdec[:, c:c + 1],
                                                         in1=kv, op0=ALU.mult, op1=ALU.add)
                        step(ins, *((free[b], turn(b, ("kv", pr, b - 5)) + 1) if c >= 5 else ()))
                elif kind == "ghead":
                    h = it[1]
                    b = 4 + h % 2
                    dve.wait_ge(full[b], turn(b, ("gs", h)) + 1)
                    if h >= 2:
                        dve.wait_ge(full[6 + h % 2], turn(6 + h % 2, ("go", h - 2)) + 1)
                    dve.wait_ge(glam_done, 1)
                    step(v.copy_predicated(gat[:, h % 2, :], glam[:, :, :].rearrange("p i t -> p (i t)").bitcast(I32),
                                           whole(b)), free[b], turn(b, ("gs", h)) + 1)
                elif kind == "gout":
                    h = it[1]
                    o = oraw[:, h % 2, :]
                    dve.wait_ge(ors_done, h + 1)
                    step(v.scalar_tensor_tensor(out=o, in0=o, scalar=gain1[:, 0:1], in1=gex[:, h % 2, :],
                                                op0=ALU.mult, op1=ALU.mult))
                    step(v.tensor_tensor(o, o, grs[:, h, :], ALU.mult), ob_done, h + 1)
                    dve.wait_ge(oBh_done, h + 1)
                    step(v.tensor_tensor(oBl[:, h, :], o, oBh[:, gslot(h), :].bitcast(F32), ALU.subtract), obl_done, h + 1)
                elif kind == "ssdprep":
                    step(v.memset(stt[:, :], 0.0))
                    step(v.memset(cblk[:, :, :], 0.0))
                    step(v.tensor_copy(cblk[0:64, 0, :], xbc[0:64, 5, 3:3 + T]))
                    step(v.tensor_copy(cblk[64:128, 1, :], xbc[64:128, 5, 3:3 + T]), cblk_done, 1)
                    dve.wait_ge(bc_in, 64)
                    dve.wait_ge(eacs_done, 1)
                elif kind == "ssd":
                    i = it[1]
                    dve.wait_ge(full[4], turn(4, ("bca", i)) + 1)
                    dve.wait_ge(full[5], turn(5, ("bcb", i)) + 1)
                    for q in range(2):
                        step(v.tensor_copy(blast[:, 4 * q:4 * q + 4].unsqueeze(2),
                                           whole(4 + q).rearrange("p (h t) -> p h t", t=P)[:, :, P - 1:P]))
                    step(v.tensor_tensor(toend[:, :], blast[:, :], nacs[:, i, :], ALU.add), sd_arg, i + 1)
                    n = turn(7, ("xt", i)) + 1
                    dve.wait_ge(full[7], n)
                    step(v.tensor_tensor(heads(xdt[:, :]), heads(whole(7)), per_head(dtok[:, i, :]), ALU.mult))
                    step(v.tensor_tensor(heads(ysd[:, :]), heads(whole(7)), per_head(dbc[:, :]), ALU.mult), free[7], n)
                    dve.wait_ge(sd_exp, i + 1)
                    step(v.tensor_tensor(heads(xdt2[:, :]), heads(xdt[:, :]), per_head(toend[:, :]), ALU.mult))
                    n = turn(6, ("sc", i)) + 1
                    dve.wait_ge(full[6], n)
                    step(v.tensor_copy(btok[:, :], bank[6][:, 256:384]))
                    for q in range(SSM_G):
                        ins = v.tensor_tensor(dec[:, 4 * q:4 * q + 4, :], dec[:, 4 * q:4 * q + 4, :],
                                              bank[6][:, q * P:q * P + P].unsqueeze(1).to_broadcast([P, 4, P]), ALU.mult)
                        step(ins, *((free[6], n) if q else ()))
                    n = turn(7, ("yi", i)) + 1
                    dve.wait_ge(full[7], n)
                    step(v.tensor_tensor(ysd[:, :], ysd[:, :], whole(7), ALU.add), free[7], n)
                    if i:
                        n = turn(6, ("ye", i)) + 1
                        dve.wait_ge(full[6], n)
                        step(v.tensor_tensor(heads(xdt[:, :]), heads(whole(6)), per_head(eacs[:, i, :]), ALU.mult), free[6], n)
                        step(v.tensor_tensor(ysd[:, :], ysd[:, :], xdt[:, :], ALU.add))
                    step(v.scalar_tensor_tensor(out=ysd[:, :], in0=ysd[:, :], scalar=0.5, in1=zs[:, i, :],
                                                op0=ALU.mult, op1=ALU.mult), sd_y, i + 1)
                    if i < NT - 1:
                        n = turn(4, ("st", i)) + 1
                        dve.wait_ge(full[4], n)
                        for q in range(SSM_G):
                            r = slice(64 * q, 64 * q + 64)
                            state = stt[r, 256 * q:256 * q + 256]
                            if i:
                                step(v.tensor_tensor(state.rearrange("p (h d) -> p h d", d=64),
                                                     state.rearrange("p (h d) -> p h d", d=64),
                                                     cdec[r, 4 * q:4 * q + 4].unsqueeze(2).to_broadcast([64, 4, 64]), ALU.mult))
                            step(v.tensor_tensor(state, state, bank[4][r, 256 * q:256 * q + 256], ALU.add),
                                 *((free[4], n) if q else ()))
                    dve.wait_ge(sd_rst, i + 1)
                    for q in range(SSM_G):
                        c = slice(256 * q, 256 * q + 256)
                        step(v.scalar_tensor_tensor(out=ysd[:, c], in0=ysd[:, c], scalar=nrs[:, q:q + 1], in1=nbc[:, c],
                                                    op0=ALU.mult, op1=ALU.mult), *((sd_norm, i + 1) if q else ()))
                    dve.wait_ge(oCh_done, i + 1)
                    step(v.tensor_tensor(oCl[:, :, i * P:(i + 1) * P], whole(5).rearrange("p (s t) -> p s t", t=P),
                                         oCh[:, :, i * P:(i + 1) * P].bitcast(F32), ALU.subtract),
                         free[5], turn(5, ("yt", i)) + 1)

            for g in range(6):
                dh, r = divmod(g, 3)
                u = U_GATE + 3 * g
                split_lo(dve, u + 2)
                split_lo(dve, u + 3)
                split_lo(dve, u + 4)
                for s in range(4):
                    n = turn(4 + s, ("proj", g)) + 1
                    dve.wait_ge(full[4 + s], n)
                    dve.wait_ge(free[s], turn(s, ("gate", g)) + 1)
                    y = yacc[:, dh * 4 + s, :]
                    dst = y if r == 0 else ytmp[:, s % 2, :]
                    step(v.scalar_tensor_tensor(out=dst, in0=sg[:, s, :], scalar=1.0, in1=whole(4 + s),
                                                op0=ALU.add, op1=ALU.mult), free[4 + s], n)
                    if r:
                        step(v.tensor_tensor(y, y, dst, ALU.add), *((y_added, dh * 4 + s + 1) if r == 2 else ()))
            for k in range(KD):
                dve.wait_ge(yh_done, k + 1)
                step(v.scalar_tensor_tensor(out=yTl[:, k, :], in0=yacc[:, k, :], scalar=0.5,
                                            in1=yTh[:, k, :].bitcast(F32), op0=ALU.mult, op1=ALU.subtract), y_done, k + 1)
            dve.wait_ge(xr_in, 16 * NT)
            for nh in range(2):
                split_lo(dve, U_OUT + 2 * nh + 2)
                split_lo(dve, U_OUT + 2 * nh + 3)
                for i in range(NT):
                    b = 4 * nh + i
                    n = turn(b, ("out", nh)) + 1
                    c = slice(nh * 512, nh * 512 + 512)
                    dve.wait_ge(full[b], n)
                    step(v.tensor_tensor(x1[:, i, c], xr[:, i, c], whole(b), ALU.add), free[b], n)
            dve.wait_ge(r2_done, 1)
            dve.wait_ge(gainb_in, 16)
            for i in range(NT):
                step(v.scalar_tensor_tensor(out=xr[:, i, :], in0=x1[:, i, :], scalar=rst[:, i:i + 1], in1=gainb[:, :],
                                            op0=ALU.mult, op1=ALU.mult), xn2_done, i + 1)
            for k in range(4, KD):
                n = turn(k, "h2T") + 1
                dve.wait_ge(full[k], n)
                step(v.tensor_copy(h2T[:, k, :], whole(k)), free[k], n)

            def b4(ap):
                return ap.unsqueeze(2).to_broadcast([P, NT, 4])

            def best(values, high, onehot):
                step(v.tensor_reduce(high, values, AX, ALU.max))
                step(v.tensor_tensor(onehot, values, b4(high), ALU.is_equal))
                step(v.tensor_tensor(gv4[:, :, :], onehot, prio[:, :].unsqueeze(1).to_broadcast([P, NT, 4]), ALU.mult))
                step(v.tensor_reduce(gsum[:, :], gv4[:, :, :], AX, ALU.max))
                step(v.tensor_tensor(onehot, gv4[:, :, :], b4(gsum[:, :]), ALU.is_equal))

            dve.wait_ge(route_consts, 2)
            dve.wait_ge(full[0], turn(0, "logits") + 1)
            step(v.tensor_tensor(lg[:, :, :], bank[0][:, 0:80].rearrange("p (i c) -> p i c", c=20),
                                 rbias[:, :].unsqueeze(1).to_broadcast([P, NT, 20]), ALU.add),
                 free[0], turn(0, "logits") + 1)
            best(lg[:, :, 0:4], gmx[:, :], goh[:, :, :])
            step(v.tensor_tensor(g4[:, :, :], lg[:, :, 0:4], b4(gmx[:, :]), ALU.subtract), r_arg, 1)
            for q in range(NEG):
                step(v.tensor_tensor(ein16[:, :, 4 * q:4 * q + 4], lg[:, :, 4 + 4 * q:8 + 4 * q],
                                     goh[:, :, q:q + 1].to_broadcast([P, NT, 4]), ALU.mult))
            step(v.tensor_tensor(ein[:, :, :], ein16[:, :, 0:4], ein16[:, :, 4:8], ALU.add))
            step(v.tensor_tensor(ein[:, :, :], ein[:, :, :], ein16[:, :, 8:12], ALU.add))
            step(v.tensor_tensor(ein[:, :, :], ein[:, :, :], ein16[:, :, 12:16], ALU.add))
            best(ein[:, :, :], m1[:, :], oh1[:, :, :])
            step(v.scalar_tensor_tensor(out=ein[:, :, :], in0=oh1[:, :, :], scalar=NEGBIG, in1=ein[:, :, :],
                                        op0=ALU.mult, op1=ALU.add))
            best(ein[:, :, :], m2[:, :], oh2[:, :, :])
            step(v.tensor_tensor(ex2[:, :], m2[:, :], m1[:, :], ALU.subtract), r_arg, 2)
            for a16, oh in ((a1, oh1), (a2, oh2)):
                for q in range(NEG):
                    step(v.tensor_tensor(a16[:, :, 4 * q:4 * q + 4], oh[:, :, :],
                                         goh[:, :, q:q + 1].to_broadcast([P, NT, 4]), ALU.mult))
            step(v.tensor_tensor(ab[:, :, :], a1[:, :, :], a2[:, :, :], ALU.add), r_ab, 1)
            dve.wait_ge(r_exp, 2)
            step(v.tensor_reduce(gsum[:, :], g4[:, :, :], AX, ALU.add))
            step(v.tensor_scalar(m1[:, :], ex2[:, :], 1.0, None, ALU.add))
            step(v.tensor_tensor(m1[:, :], m1[:, :], gsum[:, :], ALU.mult))
            step(v.reciprocal(w12[:, 0, :], m1[:, :]))
            step(v.tensor_tensor(w12[:, 1, :], w12[:, 0, :], ex2[:, :], ALU.mult))
            for k in range(2):
                step(v.tensor_copy(entry[:, k, :, 1:2].bitcast(F32), w12[:, k, :].unsqueeze(2)))
            dve.wait_ge(full[1], turn(1, "pos") + 1)
            step(v.tensor_copy(nexp[:, :], bank[1][:, 64:80]))
            step(v.tensor_scalar(extra[:, :], nexp[:, :], 128.0, None, ALU.is_gt))
            for lim in (256.0, 384.0):
                step(v.scalar_tensor_tensor(out=extra[:, :], in0=nexp[:, :], scalar=lim, in1=extra[:, :],
                                            op0=ALU.is_gt, op1=ALU.add))
            step(v.memset(one16[:, :], 1.0))
            step(v.tensor_tensor_scan(incl[:, :], one16[:, :], extra[:, :], 0.0, ALU.mult, ALU.add))
            step(v.tensor_tensor(diff[:, :], incl[:, :], extra[:, :], ALU.subtract))
            step(v.tensor_scalar(diff[:, :], diff[:, :], 128.0, 128.0 * (NEXP - 1), ALU.mult, ALU.add))
            step(v.tensor_tensor(diff[:, :], diff[:, :], e128[:, :], ALU.subtract))
            place = bank[1][:, 0:64].rearrange("p (i e) -> p i e", e=16)

            def over_tokens(ap):
                return ap.unsqueeze(1).to_broadcast([P, NT, 16])
            step(v.tensor_scalar(over[:, :, :], place, 128.0, None, ALU.is_ge))
            step(v.tensor_tensor(over[:, :, :], over[:, :, :], over_tokens(diff[:, :]), ALU.mult))
            step(v.tensor_tensor(slot[:, :, :], over[:, :, :], place, ALU.add), free[1], turn(1, "pos") + 1)
            step(v.tensor_tensor(slot[:, :, :], slot[:, :, :], over_tokens(e128[:, :]), ALU.add))
            for k, a16 in enumerate((a1, a2)):
                step(v.tensor_tensor(a16[:, :, :], a16[:, :, :], slot[:, :, :], ALU.mult))
                step(v.tensor_reduce(sl12[:, k, :], a16[:, :, :], AX, ALU.add))
            step(v.tensor_copy(sli[:, :, :], sl12[:, :, :]), r_slot, 1)
            step(v.tensor_tensor(ovm[:, :, :], incl[:, :].unsqueeze(1).to_broadcast([P, OVF, 16]),
                                 iota7[:, :].unsqueeze(2).to_broadcast([P, OVF, 16]), ALU.is_le))
            step(v.tensor_reduce(ove[:, 1:8], ovm[:, :, :], AX, ALU.add))
            step(v.tensor_copy(ove[:, 0:1], incl[:, 15:16]))
            step(v.tensor_scalar(ove[:, :], ove[:, :], 15.0, None, ALU.min))
            step(v.tensor_copy(ovi[:, :], ove[:, :]), r_slot, 2)

            def x_lo(n, par, m=None, per=2):
                for half in range(2):
                    dve.wait_ge(xTh_done, after(m, 2 * per, 2 * n + half + 1))
                    b = 4 + half
                    v.tensor_tensor(xTl[:, par, 4 * half:4 * half + 4, :], whole(b).rearrange("p (j t) -> p j t", t=P),
                                    xTh[:, par, 4 * half:4 * half + 4, :].bitcast(F32), ALU.subtract).then_inc(free[b], 1)

            def hid_lo(n, m=None, per=2):
                dve.wait_ge(hdh_done, after(m, per, n + 1))
                v.tensor_tensor(hdl[:, :, :], whole(6).rearrange("p (j t) -> p j t", t=P), hdh[:, :, :].bitcast(F32),
                                ALU.subtract).then_inc(free[6], 1)

            def gated(n, m=None, per=2):
                dve.wait_ge(full[1], after(m, per, B0[1] + n + 1))
                dve.wait_ge(free[0], after(m, per, B0[0] + n + 1))
                v.tensor_tensor(hid[:, :], act1[:, :], whole(1), ALU.mult).then_inc(free[1], 1)

            def item(n, u, m=None):
                split_lo(dve, u + 2, m)
                hid_lo(n - 1, m)
                split_lo(dve, u + 3, m)
                split_lo(dve, u + 4, m)
                split_lo(dve, u + 5, m)
                if n < NEXP - 1:
                    x_lo(n + 1, (n + 1) % 2, m)
                split_lo(dve, u + 6, m)
                split_lo(dve, u + 7, m)
                gated(n, m)

            x_lo(0, 0)
            u = U_MOE
            split_lo(dve, u + 2)
            split_lo(dve, u + 3)
            x_lo(1, 1)
            split_lo(dve, u + 4)
            split_lo(dve, u + 5)
            gated(0)
            with dve.Fori(0, 7) as m:
                item(1, u + 4, m)
                item(2, u + 10, m)
            item(15, u + 88)
            hid_lo(15)
            count = dve.value_load(ovi[0:1, 0:1], min_val=0, max_val=OVF)
            with dve.If(count > 0):
                with dve.Fori(0, count) as m:
                    u = U_OVF
                    x_lo(NEXP, 0, m, 1)
                    for q in range(6):
                        if q == 4:
                            gated(NEXP, m, 1)
                        split_lo(dve, u + q, m, True)
                    hid_lo(NEXP, m, 1)
                dve.nop()

        @block.tensor
        def _(pe):
            t = nc.tensor

            def passes(out, lhs, rhs, start, stop):
                t.matmul(out, lhs[0], rhs[0], start=start, stop=False)
                t.matmul(out, lhs[0], rhs[1], start=False, stop=False)
                return t.matmul(out, lhs[1], rhs[0], start=False, stop=stop)

            def take(b, key):
                n = turn(b, key)
                if n:
                    pe.wait_ge(free[b], n)

            pe.wait_ge(consts, 1)
            pe.wait_ge(rows_in, 16 * 11)
            t.transpose(bank[0][:, 0:NROWS], rows[:, :], ident[0:NROWS, 0:NROWS]).then_inc(full[0], 1)
            take(0, "hT")
            for i in range(NT):
                pe.wait_ge(xn_done, i + 1)
                for k in range(KD):
                    ins = t.transpose(bank[k][:, i * P:(i + 1) * P], xn[:, i, k * P:(k + 1) * P], ident[:, :])
                    if i == NT - 1:
                        ins.then_inc(full[k], 1)

            for it in SCHED:
                kind = it[0]
                if kind == "small":
                    pe.wait_ge(wsml_done, 1)
                    for k in range(KD):
                        pe.wait_ge(free[k], turn(k, "hT") + 1)
                    for k in range(KD):
                        ins = passes(whole(4), (wsmh[:, k, :], wsml[:, k, :]), (hTh[:, k, :], hTl[:, k, :]),
                                     k == 0, k == KD - 1)
                    ins.then_inc(full[4], 1)
                elif kind == "loga":
                    pr = it[1]
                    take(5 + pr, it)
                    pe.wait_ge(free[4], turn(4, "small") + 1)
                    pe.wait_ge(par_in, 16 * 4)
                    t.matmul(whole(5 + pr), wlr[32:48, pr * P:(pr + 1) * P], sm[32:48, :], start=True,
                             stop=True).then_inc(full[5 + pr], 1)
                elif kind == "tokrows":
                    take(7, it)
                    pe.wait_ge(rows_done, 1)
                    for i in range(NT):
                        for q, src in enumerate((sm, cum16)):
                            ins = t.transpose(bank[7][:, 32 * i + 16 * q:32 * i + 16 * q + 16],
                                              src[0:16, i * P:(i + 1) * P], ident[0:16, 0:16])
                    ins.then_inc(full[7], 1)
                elif kind == "piece":
                    _, b, kh, s, q = it
                    u = 2 * b + kh
                    slot_u = u % RING
                    if s == 0 and q == 0:
                        pe.wait_ge(lo_ready, u + 1)
                    if kh == 0 and q == 0:
                        take(s, ("block", b))
                    for j in (2 * q, 2 * q + 1):
                        k = 4 * kh + j
                        if BLOCKS[b][3] == "T":
                            c = slice(s * P, (s + 1) * P)
                            lhs = whi[:, slot_u, j, c], wlo[:, slot_u, j, c]
                            rhs = hTh[:, k, :], hTl[:, k, :]
                        else:
                            c = slice(s * P, (s + 1) * P)
                            lhs = hTh[:, k, c], hTl[:, k, c]
                            rhs = whi[:, slot_u, j, :], wlo[:, slot_u, j, :]
                        ins = passes(whole(s), lhs, rhs, k == 0, k == KD - 1)
                    if q == 1 and kh == 1:
                        ins.then_inc(full[s], 1)
                    elif q == 1 and s == SUBS[b] - 1:
                        ins.then_inc(unit_used, 1)
                elif kind == "qnorm":
                    m = it[1]
                    b = 4 + m % 2
                    take(b, it)
                    pe.wait_ge(masks_done, 1)
                    pe.wait_ge(sq_done, m + 1)
                    t.matmul(whole(b), blk64[:, :], qsq[:, m % 2, :], start=True, stop=True).then_inc(full[b], 1)
                elif kind == "cb":
                    h = it[1]
                    take(6, it)
                    t.matmul(whole(6), sgni[:, h:h + 1].to_broadcast([16, P]), cum16[:, :], start=True,
                             stop=True).then_inc(full[6], 1)
                elif kind == "score":
                    n = it[1]
                    h, i = divmod(n, NT)
                    b = 4 + n % 2
                    r = slice((h % 2) * 64, (h % 2) * 64 + 64)
                    take(b, it)
                    if n == 0:
                        pe.wait_ge(qn_done, 8)
                    t.matmul(bank[b][:, 0:(i + 1) * P], foxq[r, h // 2, i * P:(i + 1) * P],
                             foxk[r, h // 2, 0:(i + 1) * P], start=True, stop=True)
                    t.matmul(bank[b][:, i * P:(i + 1) * P], identb[:, :], maskq[:, :], start=False, stop=True,
                             skip_group_check=True).then_inc(full[b], 1)
                elif kind == "turn":
                    n = it[1]
                    take(6, it)
                    pe.wait_ge(prob_done, n + 1)
                    for k in range(n % NT + 1):
                        ins = t.transpose(bank[6][:, k * P:(k + 1) * P], prob[n % 3][:, k * P:(k + 1) * P], ident[:, :])
                    ins.then_inc(full[6], 1)
                elif kind == "pv":
                    n = it[1]
                    h, i = divmod(n, NT)
                    pe.wait_ge(free[6], turn(6, ("turn", n)) + 1)
                    if n == 0:
                        for q in range(NT):
                            pe.wait_ge(free[q], turn(q, ("block", 2)) + 1)
                    if n % 8 == 0:
                        take(7, ("opair", n // 8))
                    out = bank[7][(h % 2) * 64:(h % 2) * 64 + 64, i * P:(i + 1) * P]
                    for k in range(i + 1):
                        ins = t.matmul(out, fv[:, k, h * 64:h * 64 + 64], probT[:, n % 2, k * P:(k + 1) * P],
                                       start=k == 0, stop=k == i)
                    ins.then_inc(full[7] if n % 8 == 7 else pv_done, 1)
                elif kind == "gprep":
                    take(4, it)
                    pe.wait_ge(kend_done, it[1] + 1)
                    for i in range(NT):
                        ins = t.transpose(bank[4][:, i * P:(i + 1) * P], kend[:, i * P:(i + 1) * P], ident[:, :])
                    ins.then_inc(full[4], 1)
                elif kind == "kv":
                    pr = it[1]
                    take(5, ("kv", pr, 0))
                    take(6, ("kv", pr, 1))
                    pe.wait_ge(free[4], turn(4, ("gprep", pr)) + 1)
                    for par in range(2):
                        rows_c = slice(par * 64, par * 64 + 64)
                        for c in range(par, 7, 2):
                            for hh in range(2):
                                h = 2 * pr + hh
                                ins = t.matmul(bank[5 + par][hh * 64:hh * 64 + 64, (c // 2) * P:(c // 2) * P + P],
                                               kendT[rows_c, c // 2, hh * 64:hh * 64 + 64],
                                               gv[rows_c, c // 2, h * P:(h + 1) * P], start=True, stop=True)
                        ins.then_inc(full[5 + par], 1)
                elif kind == "ghead":
                    h = it[1]
                    pr, hh = divmod(h, 2)
                    r = slice(hh * 64, hh * 64 + 64)
                    q, k = gqk[r, pr, :], gqk[r, 2 + pr, :]
                    b = 4 + hh
                    take(b, ("gs", h))
                    pe.wait_ge(gpre_done, pr + 1)
                    for i in range(NT):
                        c = slice(i * P, (i + 1) * P)
                        ins = t.matmul(bank[b][:, c], k[:, c], q[:, c], start=True, stop=True)
                    ins.then_inc(full[b], 1)
                    take(6 + hh, ("go", h))
                    pe.wait_ge(free[b], turn(b, ("gs", h)) + 1)
                    pe.wait_ge(free[5], turn(5, ("kv", pr, 0)) + 1)
                    for i in range(NT):
                        c = slice(i * P, (i + 1) * P)
                        t.matmul(bank[6 + hh][:, c], gv[:, i, h * P:(h + 1) * P], gat[:, hh, c], start=True,
                                 stop=True, skip_group_check=True)
                        for ch in (2 * i, 2 * i + 1):
                            if ch:
                                cc = slice(ch * CHUNK, (ch + 1) * CHUNK)
                                ins = t.matmul(bank[6 + hh][:, cc], prev[r, ch, :], q[:, cc], start=False,
                                               stop=True, skip_group_check=True)
                    ins.then_inc(full[6 + hh], 1)
                elif kind == "gout":
                    h = it[1]
                    b = 4 + h % 2
                    take(b, it)
                    pe.wait_ge(free[6 + h % 2], turn(6 + h % 2, ("go", h)) + 1)
                    t.matmul(whole(b), ones128[:, :], gex[:, h % 2, :], start=True, stop=True).then_inc(full[b], 1)
                elif kind == "ssdprep":
                    pe.wait_ge(xbc_done, 6)
                    pe.wait_ge(cblk_done, 1)
                elif kind == "ssd":
                    i = it[1]
                    c = slice(i * P, (i + 1) * P)
                    c3 = slice(3 + i * P, 3 + (i + 1) * P)
                    for q, name in enumerate(("bca", "bcb")):
                        take(4 + q, (name, i))
                        for h in range(4):
                            out = bank[4 + q][:, h * P:(h + 1) * P]
                            t.matmul(out, sgni[:, 8 + 4 * q + h:9 + 4 * q + h].to_broadcast([16, P]), cum16[:, c],
                                     start=True, stop=False)
                            ins = t.matmul(out, identb[:, :], masks[:, :], start=False, stop=True)
                        ins.then_inc(full[4 + q], 1)
                    take(7, ("xt", i))
                    for s in range(4):
                        ins = t.transpose(bank[7][:, s * P:(s + 1) * P], xbc[:, s, c3], ident[:, :])
                    ins.then_inc(full[7], 1)
                    take(6, ("sc", i))
                    t.matmul(bank[6][:, 0:256].rearrange("p (g t) -> p g t", t=P), xbc[:, 4, c3], cblk[:, :, c],
                             start=True, stop=True)
                    t.transpose(bank[6][:, 256:384], xbc[:, 4, c3], ident[:, :]).then_inc(full[6], 1)
                    take(7, ("yi", i))
                    pe.wait_ge(free[6], turn(6, ("sc", i)) + 1)
                    for h in range(SSM_H):
                        ins = t.matmul(bank[7][:, h * 64:h * 64 + 64], dec[:, h, :], xdt[:, h * 64:h * 64 + 64],
                                       start=True, stop=True)
                    ins.then_inc(full[7], 1)
                    if i:
                        pe.wait_ge(free[4], turn(4, ("st", i - 1)) + 1)
                        take(6, ("ye", i))
                        t.matmul(whole(6), xbc[:, 5, c3], stt[:, :], start=True, stop=True).then_inc(full[6], 1)
                    if i < NT - 1:
                        take(4, ("st", i))
                        t.matmul(whole(4), btok[:, :], xdt2[:, :], start=True, stop=True).then_inc(full[4], 1)
                    take(5, ("yt", i))
                    pe.wait_ge(sd_norm, i + 1)
                    for s in range(4):
                        ins = t.transpose(bank[5][:, s * P:(s + 1) * P], ysd[:, s * P:(s + 1) * P], ident[:, :])
                    ins.then_inc(full[5], 1)

            branches = ((oAh, oAl), (oBh, oBl), (oCh, oCl))
            pe.wait_ge(obl_done, GLA_H)
            for g in range(6):
                dh, r = divmod(g, 3)
                u = U_GATE + 3 * g
                for kh in range(2):
                    su = (u + kh) % RING
                    pe.wait_ge(lo_ready, u + kh + 1)
                    for s in range(4):
                        c = slice(s * P, (s + 1) * P)
                        if kh == 0:
                            take(s, ("gate", g))
                        for j in range(4):
                            k = 4 * kh + j
                            ins = passes(whole(s), (whi[:, su, j, c], wlo[:, su, j, c]), (hTh[:, k, :], hTl[:, k, :]),
                                         k == 0, k == KD - 1)
                        if kh == 1:
                            ins.then_inc(full[s], 1)
                        elif s == 3:
                            ins.then_inc(unit_used, 1)
                su = (u + 2) % RING
                pe.wait_ge(lo_ready, u + 3)
                for s in range(4):
                    c = slice(s * P, (s + 1) * P)
                    take(4 + s, ("proj", g))
                    for j in range(4):
                        jh = gslot(j) if r == 1 else j
                        ins = passes(whole(4 + s), (whi[:, su, j, c], wlo[:, su, j, c]),
                                     (branches[r][0][:, jh, :], branches[r][1][:, j, :]), j == 0, j == 3)
                    ins.then_inc(full[4 + s], 1)
            pe.wait_ge(y_done, KD)
            for nh in range(2):
                for kh in range(2):
                    u = U_OUT + 2 * nh + kh
                    pe.wait_ge(lo_ready, u + 1)
                    for i in range(NT):
                        c = slice(i * P, (i + 1) * P)
                        if kh == 0:
                            take(4 * nh + i, ("out", nh))
                        for j in range(4):
                            k = 4 * kh + j
                            ins = passes(whole(4 * nh + i), (yTh[:, k, c], yTl[:, k, c]),
                                         (whi[:, u % RING, j, :], wlo[:, u % RING, j, :]), k == 0, k == KD - 1)
                        if kh == 1:
                            ins.then_inc(full[4 * nh + i], 1)
                        elif i == NT - 1:
                            ins.then_inc(unit_used, 1)
            for k in range(KD):
                take(k, "h2T")
            for i in range(NT):
                pe.wait_ge(xn2_done, i + 1)
                for k in range(KD):
                    ins = t.transpose(bank[k][:, i * P:(i + 1) * P], xr[:, i, k * P:(k + 1) * P], ident[:, :])
                    if i == NT - 1:
                        ins.then_inc(full[k], 1)
            pe.wait_ge(wr_in, 32)
            for k in range(KD):
                pe.wait_ge(free[k], turn(k, "h2T") + 1)
            for i in range(NT):
                for k in range(KD):
                    ins = t.matmul(bank[0][:, i * 20:i * 20 + 20], h2T[:, k, i * P:(i + 1) * P], wr[:, k, :],
                                   start=k == 0, stop=k == KD - 1)
            ins.then_inc(full[0], 1)
            pe.wait_ge(r_ab, 1)
            for i in range(NT):
                for j in range(i + 1):
                    t.matmul(bank[1][:, 16 * i:16 * i + 16], (trib if j == i else onesb)[:, :], ab[:, j, :],
                             start=j == 0, stop=j == i)
            for j in range(NT):
                ins = t.matmul(bank[1][:, 64:80], onesb[:, :], ab[:, j, :], start=j == 0, stop=j == NT - 1)
            ins.then_inc(full[1], 1)

            def expert_unit(u, out, lhs, first, last, b=None, m=None, per=12):
                su = u % RING
                pe.wait_ge(lo_ready, after(m, per, u + 1))
                for j in range(4):
                    ins = passes(out, (lhs[0][:, j, :], lhs[1][:, j, :]), (whi[:, su, j, :], wlo[:, su, j, :]),
                                 first and j == 0, last and j == 3)
                return ins

            def up_product(n, u, b, par, m=None, per=2, uper=12, between=None):
                for kh in range(2):
                    if kh == 0:
                        pe.wait_ge(free[b], after(m, per, B0[b] + n))
                        if b == 0:
                            for q in (4, 5):
                                pe.wait_ge(free[q], after(m, per, B0[q] + n + 1))
                    k = slice(4 * kh, 4 * kh + 4)
                    ins = expert_unit(u + kh, whole(b), (xTh[:, par, k, :], xTl[:, par, k, :]), kh == 0, kh == 1,
                                      m=m, per=uper)
                    if kh == 0:
                        ins.then_inc(unit_used, 1)
                        if between:
                            between()
                    else:
                        ins.then_inc(full[b], 1)

            def down_product(n, u, m=None, per=2, uper=12):
                pe.wait_ge(free[6], after(m, per, B0[6] + n + 1))
                for nh in range(2):
                    pe.wait_ge(free[2 + nh], after(m, per, B0[2 + nh] + n))
                    ins = expert_unit(u + nh, whole(2 + nh), (hdh, hdl), True, True, m=m, per=uper)
                    ins.then_inc(full[2 + nh], 1)

            def turn_rows(n, par, landed, m=None, per=2, lper=16):
                pe.wait_ge(xg_in[par], after(m, lper, landed))
                for half in range(2):
                    b = 4 + half
                    pe.wait_ge(free[b], after(m, per, B0[b] + n))
                    for q in range(4):
                        k = 4 * half + q
                        ins = t.transpose(bank[b][:, q * P:(q + 1) * P], xg[:, par, k * P:(k + 1) * P], ident[:, :])
                    ins.then_inc(full[b], 1)

            def turn_hid(n, m=None, per=2):
                pe.wait_ge(free[1], after(m, per, B0[1] + n + 1))
                pe.wait_ge(free[6], after(m, per, B0[6] + n))
                for j in range(4):
                    ins = t.transpose(bank[6][:, j * P:(j + 1) * P], hid[:, j * P:(j + 1) * P], ident[:, :])
                ins.then_inc(full[6], 1)

            def item(n, u, landed, m=None):
                up_product(n, u, 0, n % 2, m, between=lambda: turn_hid(n - 1, m))
                down_product(n - 1, u + 2, m)
                if n < NEXP - 1:
                    turn_rows(n + 1, (n + 1) % 2, landed, m)
                up_product(n, u + 4, 1, n % 2, m)

            turn_rows(0, 0, 16)
            u = U_MOE
            up_product(0, u, 0, 0)
            turn_rows(1, 1, 16)
            up_product(0, u + 2, 1, 0)
            with pe.Fori(0, 7) as m:
                item(1, u + 4, 32, m)
                item(2, u + 10, 32, m)
            item(15, u + 88, 0)
            turn_hid(15)
            down_product(15, u + 94)
            pe.wait_ge(r_slot, 2)
            count = pe.value_load(ovi[0:1, 0:1], min_val=0, max_val=OVF)
            with pe.If(count > 0):
                with pe.Fori(0, count) as m:
                    u = U_OVF
                    turn_rows(NEXP, 0, 16 * (NEXP // 2 + 1), m, 1, 16)
                    up_product(NEXP, u, 0, 0, m, 1, 6)
                    up_product(NEXP, u + 2, 1, 0, m, 1, 6)
                    turn_hid(NEXP, m, 1)
                    down_product(NEXP, u + 4, m, 1, 6)
                pe.nop()


_OUT = "out_dram"


def kernel(**inputs):
    from concourse import bacc
    from concourse.bass_utils import run_bass_kernel_spmd

    nc = bacc.Bacc("TRN2", target_bir_lowering=False, num_devices=1)
    arrays, args = {}, {}
    for name, value in inputs.items():
        a = np.ascontiguousarray(value)[0]
        arrays[f"in_{name}"] = a
        args[name] = nc.dram_tensor(f"in_{name}", a.shape, mybir.dt.from_np(a.dtype), kind="ExternalInput").ap()
    acc = nc.dram_tensor(_OUT, (T + P, D), F32, kind="ExternalOutput").ap()
    build(nc, acc=acc, **args)
    out = run_bass_kernel_spmd(nc, [arrays], core_ids=[0]).results[0][_OUT]
    return out[:T].reshape(1, T, D)
```

```python
from contextlib import ExitStack

import numpy as np

import concourse.bass as bass
from concourse import mybir

F32 = mybir.dt.float32
F32R = mybir.dt.float32r
BF16 = mybir.dt.bfloat16
I32 = mybir.dt.int32
ALU = mybir.AluOpType
ACT = mybir.ActivationFunctionType
AX = mybir.AxisListType.X

P = 128
T, D = 512, 1024
NT, KD = T // P, D // P
MIX = 512
CHUNK = 64
EPS = 1e-6
FOX_H, FOX_HD = 8, 64
GLA_H, GLA_DK, GLA_RANK = 4, 64, 16
SSM_H, SSM_G, SSM_CONV = 8, 2, 4
NEG, NEXP, EPG, DE = 4, 16, 4, 512
NEGBIG = -1e30

C_FQ, C_FK, C_FV, C_FF = 0, 512, 1024, 1536
C_GQK, C_GV, C_GR, C_GLR = 1544, 2056, 2568, 3080
C_Z, C_XBC, C_DT, C_GATE = 3096, 3608, 4376, 4384

KORDER = [4, 0, 1, 2, 3, 5, 6, 7]
RING = 3
UW = 512

BLOCKS = [("fq", C_FQ, 512, "T"), ("fk", C_FK, 512, "T"), ("fv", C_FV, 512, "tok"),
          ("xs", C_XBC, 512, "T"), ("bc", C_XBC + 512, 256, "T"), ("gqk", C_GQK, 512, "T"),
          ("gv", C_GV, 512, "tok"), ("gr", C_GR, 512, "T"), ("z", C_Z, 512, "tok")]
NB = len(BLOCKS)
SUBS = [4 if b[3] == "tok" else b[2] // P for b in BLOCKS]

U_GATE = 2 * NB
GATES = [(0, 0), (1, 0), (0, 1), (0, 2), (1, 1), (1, 2)]
U_OUT = U_GATE + 18
U_MOE = U_OUT + 4
U_OVF = U_MOE + 6 * NEXP
OVF = 7
ITEMS = NEXP + OVF

R_NM, R_NF, R_BG, R_CW, R_CB, R_GB, R_GO, R_FQ, R_FK = 0, 8, 16, 40, 64, 70, 72, 73, 74
NROWS = 75



def schedule():
    pieces = [("piece", b, kh, s, q) for b in range(NB) for kh in range(2) for s in range(SUBS[b])
              for q in range(2)]
    first = [p for p in pieces if p[1] < 3]
    rest = [p for p in pieces if 3 <= p[1] < NB - 2]
    last = [p for p in pieces if p[1] >= NB - 2]
    out = [("small",)]
    early = {(0, 0, 3): [("loga", 0)], (1, 1, 1): [("loga", 1)], (2, 0, 2): [("tokrows",)]}
    waiting = [[], [], []]
    for p in first:
        out.append(p)
        if p[3] == 0 and p[4] == 0:
            out += [("hi", 2 * p[1] + p[2] + 2), ("lo", 2 * p[1] + p[2] + 2)]
        if p[4] == 1:
            out += early.get(p[1:4], [])
        if p[4] == 1:
            out += waiting[0]
            m = [4 * p[1] + p[3]] if p[1] < 2 and p[2] == 1 else []
            waiting = [[("square", q) for q in m] + waiting[1], waiting[2], [("qnorm", q) for q in m]]
    steps = FOX_H * NT
    out += [("cb", 0), ("score", 0), ("score", 1), ("norm", 0)]
    done, convs, los, squash = 0, 0, [], []
    for n in range(steps):
        if n + 2 < steps:
            if (n + 2) % NT == 0:
                out.append(("cb", (n + 2) // NT))
            out.append(("score", n + 2))
        if n + 1 < steps:
            out.append(("norm", n + 1))
        out += los
        out += squash
        squash = []
        if not los and convs < 6 and ("piece", 3 + convs // 4, 1, convs % 4, 1) in rest[:max(done - 1, 0)]:
            out.append(("conv", convs))
            squash = [("squash", convs)]
            convs += 1
        upto = (n + 1) * len(rest) // steps
        taken = rest[done:upto]
        out += taken[:-1] + [("turn", n)] + taken[-1:] + [("pv", n)]
        out += [("hi", 2 * p[1] + p[2] + 2) for p in taken if p[3] == 0 and p[4] == 0]
        los = [("lo", 2 * p[1] + p[2] + 2) for p in taken if p[3] == 0 and p[4] == 0]
        done = upto
    out += squash + los
    assert convs == 6
    def fill(n, queue):
        for _ in range(min(n, len(queue))):
            p = queue.pop(0)
            out.append(p)
            if p[0] == "piece" and p[3] == p[4] == 0:
                out.extend([("hi", 2 * p[1] + p[2] + 2), ("lo", 2 * p[1] + p[2] + 2)])
            elif p[0] == "gpiece" and p[2] == p[3] == 0:
                out.extend([("hi", U_GATE + p[1] + 2), ("lo", U_GATE + p[1] + 2)])
    out += [("gdecay", 0)]
    fill(4, last)
    out += [("gprep", 0)]
    fill(3, last)
    out += [("kv", 0), ("gs", 0), ("gs", 1), ("gdecay", 1)]
    fill(3, last)
    out += [("go", 0), ("go", 1)]
    fill(5, last)
    out += [("gprep", 1), ("gout", 0)]
    fill(5, last)
    out += [("kv", 1), ("gs", 2), ("gs", 3), ("ssdprep",)]
    fill(4, last)
    out += [("go", 2), ("go", 3)]
    fill(4, last)
    out += [("gout", 1)]
    fill(2, last)
    gates = [("gpiece", part, s, q) for part in range(3) for s in range(4) for q in range(2)]
    for i, (a_fill, b_fill) in enumerate(((3, 3), (3, 3), (3, 3), (3, 3))):
        out.append(("ssdA", i))
        fill(len(last), last)
        fill(a_fill, gates)
        out.append(("ssdB", i))
        fill(b_fill, gates)
        out.append(("ssdC", i))
    assert not gates
    return out


SCHED = schedule()


def bank_uses():
    uses = {b: [] for b in range(8)}
    uses[0].append("cols")
    for k in range(KD):
        uses[k].append("hT")
    for it in SCHED:
        kind = it[0]
        if kind == "small":
            uses[4].append("small")
        elif kind == "loga":
            uses[5 + it[1]].append(it)
        elif kind == "tokrows":
            uses[7].append(it)
        elif kind == "piece" and it[2] == 0 and it[4] == 0:
            uses[it[3]].append(("block", it[1]))
        elif kind == "qnorm":
            uses[4 + it[1] % 2].append(it)
        elif kind == "cb":
            uses[6].append(it)
        elif kind == "score":
            uses[4 + it[1] % 2].append(it)
        elif kind == "turn":
            uses[6].append(it)
        elif kind == "pv" and it[1] % 8 == 0:
            uses[7].append(("opair", it[1] // 8))
        elif kind == "gprep":
            uses[4].append(it)
        elif kind == "kv":
            uses[6].append(("kv", it[1], 0))
            uses[7].append(("kv", it[1], 1))
        elif kind == "gs":
            uses[4 + it[1] % 2].append(it)
        elif kind == "go":
            uses[6 + it[1] % 2].append(it)
        elif kind == "gout":
            for hh in range(2):
                uses[4 + hh].append(("gout", 2 * it[1] + hh))
        elif kind == "gpiece" and it[3] == 0 and it[1] != 1:
            uses[it[2]].append(("gate" if it[1] == 0 else "proj", 0))
        elif kind == "ssdA":
            i = it[1]
            uses[4].append(("bca", i))
            uses[5].append(("bcb", i))
            uses[7].append(("xt", i))
            uses[6].append(("sc", i))
        elif kind == "ssdB":
            i = it[1]
            uses[7].append(("yi", i))
            if i:
                uses[6].append(("ye", i))
            if i < NT - 1:
                uses[4].append(("st", i))
        elif kind == "ssdC":
            uses[5].append(("yt", it[1]))
    for g in range(1, 6):
        for s in range(4):
            uses[s].append(("gate", g))
            uses[4 + s].append(("proj", g))
    for nh in range(2):
        for s in range(4):
            uses[4 * nh + s].append(("out", nh))
    for k in range(KD):
        uses[k].append("h2T")
    uses[0].append("logitsT")
    uses[2].append("logits")
    uses[1].append("pos")
    return uses


USES = bank_uses()


def turn(bank, key):
    return USES[bank].index(key)


def unit_source(u, w_in, w_branch, w_out):
    def block(w, r0, c0, n):
        return w[r0:r0 + 512, c0:c0 + n].rearrange("(j p) n -> p j n", p=P)
    if u < U_GATE:
        b, kh = divmod(u, 2)
        return block(w_in, kh * 512, BLOCKS[b][1], BLOCKS[b][2])
    if u < U_OUT:
        g, part = divmod(u - U_GATE, 3)
        dh, r = GATES[g]
        if part < 2:
            return block(w_in, part * 512, C_GATE + r * D + dh * 512, 512)
        return block(w_branch[r], 0, dh * 512, 512)
    kh, nh = divmod(u - U_OUT, 2)
    return block(w_out, kh * 512, nh * 512, 512)


def after(m, per, count):
    return count if m is None else m * per + count


def gslot(h):
    return (0, 2, 1, 3)[h]


class Serial:

    def __init__(self, eng, sem):
        self.eng, self.sem, self.n = eng, sem, 0

    def __call__(self, ins, sem=None, n=None):
        if sem is None:
            self.n += 1
            sem, n = self.sem, self.n
        ins.then_inc(sem, 1)
        self.eng.wait_ge(sem, n)


def build(nc, x, norm_mix, w_in, fox_f_bias, fox_q_norm, fox_k_norm, gla_w_lr, gla_b_gate,
          gla_out_norm, ssm_conv_w, ssm_conv_b, ssm_dt_bias, ssm_a_log, ssm_d, ssm_out_norm,
          w_branch, b_branch_gate, w_out, norm_ffn, w_router_grp, b_router_grp,
          w_router_exp, b_router_exp, w_exp_gate, w_exp_up, w_exp_down, acc):
    with ExitStack() as ctx:
        base = 16512

        def at(name, kb, shape, dt=F32):
            return nc.alloc_sbuf_tensor_at(name, list(shape), dt, offset=base + int(kb * 1024))

        sems = {}

        def sem(name):
            sems[name] = ctx.enter_context(nc.semaphore(name))
            return sems[name]

        stage = at("stage", 0, [P, RING, 4, UW])
        whi = at("whi", 24, [P, RING, 4, UW], F32R)
        wlo = at("wlo", 48, [P, RING, 4, UW], F32R)
        hTh = at("hTh", 72, [P, KD, T], F32R)
        hTl = at("hTl", 88, [P, KD, T], F32R)
        xin = at("xin", 104, [P, NT, D])
        foxq = at("foxq", 104, [P, 4, T])
        foxk = at("foxk", 112, [P, 4, T])
        oAh = at("oAh", 104, [P, 4, T], F32R)
        oAl = at("oAl", 112, [P, 4, T], F32R)
        xn = at("xn", 120, [P, NT, D])
        gqk = at("gqk", 120, [P, 4, T])
        grs = at("grs", 128, [P, 4, T])
        oBh = at("oBh", 120, [P, 4, T], F32R)
        oBl = at("oBl", 128, [P, 4, T], F32R)
        gv = at("gv", 136, [P, NT, MIX])
        oCh = at("oCh", 136, [P, 4, T], F32R)
        zs = at("zs", 144, [P, NT, MIX])
        xbc = at("xbc", 152, [P, 6, T + 3])
        cpos = [164.25]

        def small(name, shape, dt=F32):
            n = int(np.prod(shape[1:])) * (2 if dt == BF16 else 4)
            t = at(name, cpos[0], shape, dt)
            cpos[0] += ((n + 63) // 64) * 64 / 1024
            return t

        ident = small("ident", [P, P])
        identb = small("identb", [P, P], BF16)
        trib = small("trib", [P, P], BF16)
        onesb = small("onesb", [P, P], BF16)
        cols = small("cols", [P, 80])
        hcol = small("hcol", [P, 56])
        rbias = small("rbias", [P, 20])
        mhalf = small("mhalf", [P, 8])
        epsc = small("epsc", [P, 1])
        ssq = small("ssq", [P, NT])
        rst = small("rst", [P, NT])
        kept_to = cpos[0]
        maskq = small("maskq", [P, P], BF16)
        masks = small("masks", [P, P], BF16)
        sgni = small("sgni", [16, 16])
        sgn16 = small("sgn16", [16, 1])
        bias16 = small("bias16", [16, 1])
        scale16 = small("scale16", [16, 1])
        gain1 = small("gain1", [P, 2])
        nbc = small("nbc", [P, MIX])
        dbc = small("dbc", [P, 8])
        tokrow = small("tokrow", [P, NT, 32])
        dtok = small("dtok", [P, NT, 8])
        nacs = small("nacs", [P, NT, 8])
        eacs = small("eacs", [P, NT, 8])
        blk64_at = cpos[0]
        blk64 = small("blk64", [P, P])
        ones128 = small("ones128", [P, P])
        wlr = small("wlr", [48, 256])
        reset16_at = cpos[0]
        reset16 = small("reset16", [16, T])
        bcum_at = cpos[0]
        bcum = small("bcum", [P, 2, T])
        glam_at = cpos[0]
        glam = small("glam", [P, NT, P])
        cum16 = small("cum16", [16, T])
        tnhb_at = cpos[0]
        tnhb = small("tnhb", [P, T])
        stt_at = cpos[0]
        stt = small("stt", [P, MIX])
        top = cpos[0]
        Z0 = 187.75
        sq4 = at("sq4", Z0, [P, D])
        rows = at("rows", Z0 + 4, [NROWS, P])
        wsm = at("wsm", Z0 + 5, [P, KD, P])
        wsmh = at("wsmh", Z0 + 9, [P, KD, P], F32R)
        wsml = at("wsml", Z0 + 13, [P, KD, P], F32R)
        reset64 = at("reset64", 150, [P, T])
        sm = at("sm", 144, [48, T])
        smz = at("smz", 146, [P, T])
        sme = at("sme", 148, [P, T])
        fv = at("fv", Z0 + 12, [P, NT, MIX])
        qsq = at("qsq", Z0, [P, 2, T])
        qrs = at("qrs", Z0 + 4, [P, 2, T])
        cbt = at("cbt", Z0, [P, 2, T])
        prob = [at("prob0", Z0 + 4, [P, T]), at("prob1", Z0 + 6, [P, T]), at("prob2", glam_at, [P, T])]
        probT = at("probT", Z0 + 8, [P, 2, T])
        nmx = at("nmx", 187.25, [P, 32])
        rsum = at("rsum", 187.375, [P, 32])
        rinv = at("rinv", 187.5, [P, 32])
        assert top <= 187.25, top
        gex = at("gex", Z0, [P, 2, T])
        kend = at("kend", Z0 + 4, [P, T])
        kendT = at("kendT", Z0 + 6, [P, NT, P])
        prev = at("prev", Z0 + 8, [P, 8, P])
        gat = at("gat", Z0 + 12, [P, 2, T])
        oraw = at("oraw", Z0 + 16, [P, 2, T])
        osq = [at("osq0", reset16_at, [P, T]), at("osq1", stt_at, [P, T])]
        gdec = at("gdec", 187.625, [P, 8])
        dec = at("dec", Z0, [P, 8, P])
        xdt = at("xdt", Z0 + 4, [P, MIX])
        xdt2 = at("xdt2", Z0 + 6, [P, MIX])
        ysd = at("ysd", Z0 + 8, [P, MIX])
        btok = at("btok", Z0 + 10, [P, P])
        toend = at("toend", Z0 + 10.5, [P, 8])
        cdec = at("cdec", Z0 + 10.5625, [P, 8])
        nss = at("nss", Z0 + 10.625, [P, 2])
        nrs = at("nrs", Z0 + 10.6875, [P, 2])
        blast = at("blast", Z0 + 10.75, [P, 8])
        cblk = at("cblk", bcum_at, [P, 2, T])
        oCl = at("oCl", Z0 + 12, [P, 4, T], F32R)
        yacc = [at("y0", glam_at, [P, T]), at("y1", reset16_at, [P, T]), at("y2", tnhb_at, [P, T]),
                at("y3", blk64_at, [P, T])] + [at(f"y{k}", 144 + 2 * k, [P, T]) for k in range(4, KD)]
        sg = at("sg", 144, [P, 4, T])
        ytmp = at("ytmp", Z0, [P, 2, T])
        yTh = [at("yTh0", 104, [P, 4, T], F32R), at("yTh1", 72, [P, 4, T], F32R)]
        yTl = [at("yTl0", 112, [P, 4, T], F32R), at("yTl1", 80, [P, 4, T], F32R)]
        x1 = at("x1", 120, [P, NT, D])
        xn2 = at("xn2", 88, [P, NT, D])
        h2T = at("h2T", 144, [P, KD, T])
        lgT = at("lgT", 162, [20, T])
        wr = at("wr", 161.25, [P, KD, 20])
        rpos = [Z0]

        def rout(name, shape, dt=F32):
            n = int(np.prod(shape[1:])) * (2 if dt == BF16 else 4)
            t = at(name, rpos[0], shape, dt)
            rpos[0] += ((n + 63) // 64) * 64 / 1024
            assert rpos[0] <= Z0 + 8
            return t

        lg = rout("lg", [P, NT, 20])
        gmx = rout("gmx", [P, NT])
        g4 = rout("g4", [P, NT, 4])
        gv4 = rout("gv4", [P, NT, 4])
        goh = rout("goh", [P, NT, 4])
        gsum = rout("gsum", [P, NT])
        gw = rout("gw", [P, NT])
        ein16 = rout("ein16", [P, NT, 16])
        ein = rout("ein", [P, NT, 4])
        m1 = rout("m1", [P, NT])
        m2 = rout("m2", [P, NT])
        oh1 = rout("oh1", [P, NT, 4])
        oh2 = rout("oh2", [P, NT, 4])
        a1 = rout("a1", [P, NT, 16])
        a2 = rout("a2", [P, NT, 16])
        ab = rout("ab", [P, NT, 16], BF16)
        w12 = rout("w12", [P, 2, NT])
        ex2 = rout("ex2", [P, NT])
        nexp = rout("nexp", [P, 16])
        extra = rout("extra", [P, 16])
        incl = rout("incl", [P, 16])
        diff = rout("diff", [P, 16])
        slot = rout("slot", [P, NT, 16])
        over = rout("over", [P, NT, 16])
        sl12 = rout("sl12", [P, 2, NT])
        sli = rout("sli", [P, 2, NT], I32)
        ovm = rout("ovm", [P, OVF, 16])
        ove = rout("ove", [P, 8])
        one16 = rout("one16", [P, 16])
        prio = at("prio", 160, [P, 4])
        e128 = at("e128", 160.0625, [P, 16])
        iota7 = at("iota7", 160.125, [P, OVF])
        tokid = at("tokid", 160.1875, [P, NT], I32)
        entry = at("entry", 160.25, [P, 2, NT, 2], I32)
        tabi = at("tabi", 160.5, [P, ITEMS, 2], I32)
        tab = at("tab", 160.75, [P, ITEMS, 2], I32)
        ovi = at("ovi", 161, [P, 8], I32)
        pad = at("pad", 161.0625, [P, 2])
        zero = at("zero", Z0 + 4, [P, D])
        gainb = at("gainb", Z0 + 8, [P, D])
        xg = at("xg", 72, [P, 2, D])
        xTh = at("xTh", 80, [P, 2, KD, P], F32R)
        xTl = at("xTl", 88, [P, 2, KD, P], F32R)
        act1 = at("act1", 96, [P, DE])
        hid = at("hid", 98, [P, DE])
        hdh = at("hdh", 100, [P, 4, P], F32R)
        hdl = at("hdl", 102, [P, 4, P], F32R)
        yrow = at("yrow", Z0 + 4, [P, 2, D])
        assert kept_to <= 170
        mstage = [at(f"mstage{k}", kb, [P, 4, UW]) for k, kb in enumerate(
            (8, 16, 0, 178, Z0 + 12, 136, 104, 112, 120, 128, 144, 152))]


        bank = [ctx.enter_context(nc.psum_tensor(f"bank{b}", [P, 512], F32)) for b in range(8)]
        h2d = nc.dram_tensor("h2rows", [T + P, D], F32).ap()
        tabd = nc.dram_tensor("slots", [ITEMS * P, 2], I32).ap()

        full = [sem(f"full{b}") for b in range(8)]
        free = [sem(f"free{b}") for b in range(8)]
        staged = [sem(f"staged{s}") for s in range(RING)]
        mstaged = [sem(f"mstaged{k}") for k in range(12)]
        hi_ready, lo_ready, unit_used = sem("hi_ready"), sem("lo_ready"), sem("unit_used")
        pool_step, dve_step, act_step, idx_step = sem("pool_step"), sem("dve_step"), sem("act_step"), sem("idx_step")
        x_in = [sem(f"x_in{i}") for i in range(NT)]
        rows_in, wsm_in, par_in, bc_in = sem("rows_in"), sem("wsm_in"), sem("par_in"), sem("bc_in")
        (consts, masks_done, route_consts, ssq_done, rst_done, xn_done, cols_done, hTh_done, wsm_zero, wsmh_done,
         wsml_done, z_done, lnv_done, rows_done, toktr_done, eacs_done) = (sem(n) for n in (
             "consts", "masks_done", "route_consts", "ssq_done", "rst_done", "xn_done", "cols_done", "hTh_done",
             "wsm_zero", "wsmh_done", "wsml_done", "z_done", "lnv_done", "rows_done", "toktr_done", "eacs_done"))
        sq_done, qrs_done, qn_done, exp_done, prob_done, pv_done, oAh_done, tanh_done = (sem(n) for n in (
            "sq_done", "qrs_done", "qn_done", "exp_done", "prob_done", "pv_done", "oAh_done", "tanh_done"))
        (conv_done, ctanh_done, xbc_done, garg_done, gexp_done, kend_done, gpre_done, ors_done, ob_done, oBh_done,
         obl_done) = (sem(n) for n in ("conv_done", "ctanh_done", "xbc_done", "garg_done", "gexp_done", "kend_done",
                                       "gpre_done", "ors_done", "ob_done", "oBh_done", "obl_done"))
        glam_done = sem("glam_done")
        cblk_done, sd_last, sd_arg, sd_exp, sd_y, sd_sq, sd_rst, sd_norm, oCh_done = (sem(n) for n in (
            "cblk_done", "sd_last", "sd_arg", "sd_exp", "sd_y", "sd_sq", "sd_rst", "sd_norm", "oCh_done"))
        y_added, yh_done, y_done = sem("y_added"), sem("yh_done"), sem("y_done")
        (xr_in, gainb_in, wr_in, x1_sq, r2_done, xn2_done, wr_done, acc_in, h2_out, pad_out, tab_out, r_arg, r_exp, r_ab, r_slot,
         tab_put, tab_in) = (sem(n) for n in (
             "xr_in", "gainb_in", "wr_in", "x1_sq", "r2_done", "xn2_done", "wr_done", "acc_in", "h2_out", "pad_out", "tab_out", "r_arg",
             "r_exp", "r_ab", "r_slot", "tab_put", "tab_in"))
        xg_in = [sem("xg_in0"), sem("xg_in1")]
        xTh_done, hid_done, hdh_done, added = sem("xTh_done"), sem("hid_done"), sem("hdh_done"), sem("added")
        ssq_dve = sem("ssq_dve")
        block = ctx.enter_context(nc.Block())

        B0 = [len(USES[b]) for b in range(8)]

        def whole(b):
            return bank[b][:, :]

        def width_of(u):
            return BLOCKS[u // 2][2] if u < U_GATE else UW

        def source_of(u):
            return stage[:, u % RING] if u < U_MOE else mstage[(u - U_MOE) % 12]

        def wait_unit(eng, u, m=None, ovf=False):
            if u < U_GATE:
                b, kh = divmod(u, 2)
                s = SUBS[b] - 1
                which, n = (full[s], turn(s, ("block", b)) + 1) if kh else (unit_used, b + 1)
            elif u < U_OUT:
                g, part = divmod(u - U_GATE, 3)
                which, n = ((unit_used, NB + g + 1), (full[3], turn(3, ("gate", g)) + 1),
                            (full[7 if g else 3], turn(7 if g else 3, ("proj", g)) + 1))[part]
            elif u < U_MOE:
                kh, nh = divmod(u - U_OUT, 2)
                b = 4 * nh + 3
                which, n = (full[b], turn(b, ("out", nh)) + 1) if kh else (unit_used, NB + 6 + nh + 1)
            elif u < U_MOE + 4:
                k = u - U_MOE
                which, n = ((unit_used, NB + 9), (full[0], B0[0] + 1), (unit_used, NB + 10), (full[1], B0[1] + 1))[k]
            elif u < U_OVF - 2:
                i, k = divmod(u - U_MOE - 4, 6)
                i += 1
                which, n = ((unit_used, NB + 9 + 2 * i), (full[0], B0[0] + i + 1), (full[2], B0[2] + i),
                            (full[3], B0[3] + i), (unit_used, NB + 10 + 2 * i), (full[1], B0[1] + i + 1))[k]
            elif u < U_OVF:
                b = 2 + u - (U_OVF - 2)
                which, n = full[b], B0[b] + NEXP
            else:
                w, k = divmod(u - U_OVF, 6)
                i = NEXP + w
                which, n = ((unit_used, NB + 9 + 2 * i), (full[0], B0[0] + i + 1), (unit_used, NB + 10 + 2 * i),
                            (full[1], B0[1] + i + 1), (full[2], B0[2] + i + 1), (full[3], B0[3] + i + 1))[k]
            items = 1 if ovf else 2
            eng.wait_ge(which, after(m, 2 * items if which is unit_used else items, n))

        def split_hi(act, u, m=None, ovf=False):
            s, n = u % RING, width_of(u)
            if u < U_MOE:
                act.wait_ge(staged[s], 16 * (u // RING + 1))
            else:
                act.wait_ge(mstaged[(u - U_MOE) % 12], after(m, 16, 16 * ((u - U_MOE) // 12 + 1)))
            if U_OVF <= u < U_OVF + RING:
                act.wait_ge(full[u - U_OVF + 1], after(m, 1, B0[u - U_OVF + 1] + NEXP))
            elif u >= RING:
                wait_unit(act, u - RING, m, ovf)
            nc.scalar.activation(whi[:, s, :, 0:n], source_of(u)[:, :, 0:n], ACT.Copy).then_inc(hi_ready, 1)

        def wait_pv(eng, n):
            if n % 8 == 7:
                eng.wait_ge(full[7], turn(7, ("opair", n // 8)) + 1)
            else:
                eng.wait_ge(pv_done, n + 1 - (n + 1) // 8)

        def split_lo(dve, u, m=None, ovf=False):
            s, n = u % RING, width_of(u)
            dve.wait_ge(hi_ready, after(m, 6 if ovf else 12, u + 1))
            nc.vector.tensor_tensor(wlo[:, s, :, 0:n], source_of(u)[:, :, 0:n],
                                    whi[:, s, :, 0:n].bitcast(F32), ALU.subtract).then_inc(lo_ready, 1)

        @block.sync
        def _(sp):
            for i in range(NT):
                sp.dma_start(xin[:, i, :], x[i * P:(i + 1) * P, :]).then_inc(x_in[i], 16)
            sp.wait_ge(wsm_zero, 2)
            for c0, n, dst in ((C_FF, 8, 0), (C_DT, 8, 8), (C_GLR, 16, 32)):
                sp.dma_start(wsm[:, :, dst:dst + n],
                             w_in[:, c0:c0 + n].rearrange("(k p) n -> p k n", p=P)).then_inc(wsm_in, 16)
            for u in range(U_MOE):
                if u >= RING:
                    sp.wait_ge(lo_ready, u - RING + 1)
                n = width_of(u)
                sp.dma_start(stage[:, u % RING, :, 0:n], unit_source(u, w_in, w_branch, w_out)).then_inc(
                    staged[u % RING], 16)
                if u == U_OUT + 1:
                    sp.wait_ge(full[7], turn(7, ("proj", 4)) + 1)
                    for i in range(NT):
                        sp.dma_start(x1[:, i, :], x[i * P:(i + 1) * P, :]).then_inc(xr_in, 16)

            def load(u, src, m=None, ovf=False):
                k = (u - U_MOE) % 12
                if ovf:
                    sp.wait_ge(lo_ready, after(m, 6, u - 6 + 1))
                elif u >= U_MOE + 12:
                    sp.wait_ge(lo_ready, after(m, 12, u - 12 + 1))
                elif k < 3:
                    sp.wait_ge(lo_ready, u - RING + 1)
                elif k == 3:
                    sp.wait_ge(y_done, 4)
                elif k == 4:
                    sp.wait_ge(full[7], turn(7, ("proj", 5)) + 1)
                elif k == 6:
                    sp.wait_ge(unit_used, NB + 8)
                elif k == 8:
                    sp.wait_ge(acc_in, 16 * NT)
                    sp.wait_ge(xn2_done, NT)
                    sp.wait_ge(full[7], turn(7, "h2T") + 1)
                elif k == 10:
                    sp.wait_ge(full[0], turn(0, "logitsT") + 1)
                if not ovf and u >= U_MOE + 4:
                    sp.wait_ge(mstaged[(u - 4 - U_MOE) % 12], after(m, 16, 16 * ((u - 4 - U_MOE) // 12 + 1)))
                sp.dma_start(mstage[k][:, :, :], src).then_inc(mstaged[k], 16)

            def up_src(w, e, kh):
                if isinstance(e, int):
                    return w[e, kh * 512:(kh + 1) * 512, :].rearrange("(j p) n -> p j n", p=P)
                return w[bass.ds(e, 1), kh * 512:(kh + 1) * 512, :].rearrange("o (j p) n -> p (o j) n", p=P)

            def down_src(e, nh):
                if isinstance(e, int):
                    return w_exp_down[e, :, nh * 512:(nh + 1) * 512].rearrange("(j p) n -> p j n", p=P)
                return w_exp_down[bass.ds(e, 1), :, nh * 512:(nh + 1) * 512].rearrange(
                    "o (j p) n -> p (o j) n", p=P)

            def item(u, e, before, m=None):
                load(u, up_src(w_exp_gate, e, 0), m)
                load(u + 1, up_src(w_exp_gate, e, 1), m)
                if before is not None:
                    load(u + 2, down_src(before, 0), m)
                    load(u + 3, down_src(before, 1), m)
                    u += 2
                load(u + 2, up_src(w_exp_up, e, 0), m)
                load(u + 3, up_src(w_exp_up, e, 1), m)

            item(U_MOE, 0, None)
            item(U_MOE + 4, 1, 0)
            item(U_MOE + 10, 2, 1)
            with sp.Fori(1, 7) as m:
                item(U_MOE + 16, m * 2 + 1, m * 2, m - 1)
                item(U_MOE + 22, m * 2 + 2, m * 2 + 1, m - 1)
            item(U_MOE + 88, 15, 14)
            load(U_MOE + 94, down_src(15, 0))
            load(U_MOE + 95, down_src(15, 1))
            sp.wait_ge(r_slot, 2)
            count = sp.value_load(ovi[0:1, 0:1], min_val=0, max_val=OVF)
            with sp.If(count > 0):
                with sp.Fori(0, count) as m:
                    e = sp.value_load(ovi[0:1, bass.ds(m + 1, 1)], min_val=0, max_val=NEXP - 1)
                    load(U_OVF, up_src(w_exp_gate, e, 0), m, True)
                    load(U_OVF + 1, up_src(w_exp_gate, e, 1), m, True)
                    load(U_OVF + 2, up_src(w_exp_up, e, 0), m, True)
                    load(U_OVF + 3, up_src(w_exp_up, e, 1), m, True)
                    load(U_OVF + 4, down_src(e, 0), m, True)
                    load(U_OVF + 5, down_src(e, 1), m, True)
                sp.nop()

        @block.gpsimd
        def _(pool):
            step = Serial(pool, pool_step)
            g = nc.gpsimd

            def select(out, op, fill, b, pattern, cm, sem=None, n=None):
                step(g.affine_select(out=out, in_=out, compare_op=op, fill=fill, base=b,
                                     pattern=pattern, channel_multiplier=cm), sem, n)

            step(g.memset(wsm[:, :, :], 0.0), wsm_zero, 1)
            step(g.memset(scale16[:, :], 0.0), wsm_zero, 2)
            step(g.memset(ident[:, :], 0.0))
            select(ident[:, :], ALU.not_equal, 1.0, 0, [[-1, P]], 1, consts, 1)
            step(g.memset(mhalf[:, :], -0.5))
            step(g.memset(epsc[:, :], EPS))
            step(g.memset(sgn16[:, :], 1.0))
            select(sgn16[:, :], ALU.is_ge, -1.0, 7, [[0, 1]], -1, consts, 2)
            pool.wait_ge(ssq_done, 2)
            pool.wait_ge(ssq_dve, 2)
            step(g.tensor_scalar(ssq[:, :], ssq[:, :], 1.0 / D, EPS, ALU.mult, ALU.add))
            step(g.tensor_tensor(rst[:, :], ssq[:, :], mhalf[:, 0:NT], ALU.pow), rst_done, 1)
            step(g.memset(reset16[:, :], 1.0))
            select(reset16[:, :].rearrange("p (i t) -> p i t", t=P)[:, :, 0:1], ALU.is_ge, 0.0, 7,
                   [[0, NT], [0, 1]], -1)
            step(g.memset(reset64[:, :], 1.0))
            step(g.memset(reset64[:, :].rearrange("p (c t) -> p c t", t=CHUNK)[:, :, 0:1], 0.0))
            step(g.memset(blk64[:, :], 0.0))
            step(g.memset(blk64[0:64, 0:64], 1.0 / 64))
            step(g.memset(blk64[64:128, 64:128], 1.0 / 64))
            step(g.memset(sgni[:, :], 0.0))
            select(sgni[:, 0:8], ALU.not_equal, -1.0, 0, [[-1, 8]], 1)
            select(sgni[:, 8:16], ALU.not_equal, 1.0, -8, [[-1, 8]], 1)
            step(g.memset(maskq[:, :], 0.0))
            select(maskq[:, :], ALU.is_ge, NEGBIG, 0, [[-1, P]], 1)
            step(g.memset(masks[:, :], 0.0))
            select(masks[:, :], ALU.is_ge, NEGBIG, 0, [[1, P]], -1)
            step(g.memset(ones128[:, :], 1.0 / 128))
            step(g.memset(onesb[:, :], 1.0))
            step(g.memset(trib[:, :], 1.0))
            select(trib[:, :], ALU.is_gt, 0.0, 0, [[1, P]], -1)
            step(g.memset(xbc[:, :, 0:3], 0.0))
            step(g.tensor_copy(identb[:, :], ident[:, :]), masks_done, 1)
            pool.wait_ge(full[6], turn(6, ("turn", FOX_H * NT - 1)) + 1)
            step(g.memset(glam[:, :, :], 1.0))
            select(glam[:, :, :], ALU.is_ge, 0.0, 0, [[0, NT], [1, P]], -1)
            select(glam[:, :, 64:128], ALU.is_ge, 0.0, -64, [[0, NT], [0, 64]], 1, glam_done, 1)
            for i in range(NT):
                pool.wait_ge(sd_sq, i + 1)
                step(g.tensor_scalar(nss[:, :], nss[:, :], 1.0 / 256, EPS, ALU.mult, ALU.add))
                step(g.tensor_tensor(nrs[:, :], nss[:, :], mhalf[:, 0:2], ALU.pow), sd_rst, i + 1)
            pool.wait_ge(free[5], turn(5, ("yt", NT - 1)) + 1)
            for c in range(4):
                step(g.memset(prio[:, c:c + 1], float(4 - c)))
            step(g.iota(e128[:, :], pattern=[[P, 16]], base=0, channel_multiplier=0,
                        allow_small_or_imprecise_dtypes=True))
            step(g.iota(iota7[:, :], pattern=[[1, OVF]], base=0, channel_multiplier=0,
                        allow_small_or_imprecise_dtypes=True))
            step(g.iota(tokid[:, :], pattern=[[P, NT]], base=0, channel_multiplier=1))
            step(g.memset(tabi[:, :, :], 0))
            step(g.iota(tabi[:, :, 0:1], pattern=[[0, ITEMS], [0, 1]], base=T, channel_multiplier=1))
            g.dma_start(tabd.rearrange("(n p) c -> p n c", p=P), tabi[:, :, :]).then_inc(tab_out, 16)
            for k in range(2):
                step(g.tensor_copy(entry[:, k, :, 0:1].rearrange("p i o -> p (i o)"), tokid[:, :]), route_consts, k + 1)
            pool.wait_ge(y_done, KD)
            step(g.memset(zero[:, :], 0.0))
            g.dma_start(h2d[T:T + P, :], zero[:, :]).then_inc(pad_out, 16)
            g.dma_start(acc[T:T + P, :], zero[:, :]).then_inc(pad_out, 16)
            pool.wait_ge(x1_sq, NT)
            step(g.tensor_scalar(ssq[:, :], ssq[:, :], 1.0 / D, EPS, ALU.mult, ALU.add))
            step(g.tensor_tensor(rst[:, :], ssq[:, :], mhalf[:, 0:NT], ALU.pow), r2_done, 1)
            pool.wait_ge(r_slot, 1)
            pool.wait_ge(tab_out, 16)
            for k in range(2):
                for i in range(NT):
                    g.indirect_dma_start(tabd, bass.IndirectOffsetOnAxis(sli[:, k, i:i + 1], 0),
                                         entry[:, k, i, :], None).then_inc(tab_put, 16)
            pool.wait_ge(tab_put, 16 * 8)
            g.dma_start(tab[:, :, :], tabd.rearrange("(n p) c -> p n c", p=P)).then_inc(tab_in, 16)
            pool.wait_ge(tab_in, 16)
            pool.wait_ge(h2_out, 16 * NT)
            pool.wait_ge(pad_out, 32)

            def gather(i, par):
                g.indirect_dma_start(xg[:, par, :], None, h2d,
                                     bass.IndirectOffsetOnAxis(tab[:, i, 0:1], 0)).then_inc(xg_in[par], 16)

            def scatter(i, par):
                pool.wait_ge(free[2], B0[2] + i + 1)
                pool.wait_ge(free[3], B0[3] + i + 1)
                g.indirect_dma_start(acc, bass.IndirectOffsetOnAxis(tab[:, i, 0:1], 0), yrow[:, par, :], None,
                                     compute_op=ALU.add).then_inc(added, 16)

            gather(0, 0)
            gather(1, 1)
            pool.wait_ge(full[5], B0[5] + 1)
            gather(2, 0)
            pool.wait_ge(acc_in, 16 * NT)
            for i in range(NEXP):
                if i + 3 < NEXP:
                    pool.wait_ge(full[5], B0[5] + i + 2)
                    gather(i + 3, (i + 1) % 2)
                if i:
                    pool.wait_ge(added, 16 * i)
                scatter(i, i % 2)
            pool.wait_ge(added, 16 * NEXP)
            pool.wait_ge(r_slot, 2)
            count = pool.value_load(ovi[0:1, 0:1], min_val=0, max_val=OVF)
            for j in range(OVF):
                with pool.If(count > j):
                    pool.wait_ge(full[5], B0[5] + NEXP + j)
                    gather(NEXP + j, 0)
                    scatter(NEXP + j, 0)
                    pool.wait_ge(added, 16 * (NEXP + j + 1))

        @block.scalar
        def _(act):
            a = nc.scalar
            step = Serial(act, act_step)
            for r0, src in ((R_NM, norm_mix.rearrange("(r p) -> r p", p=P)),
                            (R_NF, norm_ffn.rearrange("(r p) -> r p", p=P)),
                            (R_BG, b_branch_gate.rearrange("b (r p) -> (b r) p", p=P)),
                            (R_CW, ssm_conv_w.rearrange("j (r p) -> (j r) p", p=P)),
                            (R_CB, ssm_conv_b.rearrange("(r p) -> r p", p=P)),
                            (R_GB, gla_b_gate.rearrange("(r p) -> r p", p=P)),
                            (R_GO, gla_out_norm.rearrange("(r p) -> r p", p=P))):
                act.dma_start(rows[r0:r0 + src.shape[0], :], src).then_inc(rows_in, 16)
            for r0, src in ((R_FQ, fox_q_norm), (R_FK, fox_k_norm)):
                act.dma_start(rows[r0:r0 + 1, :].rearrange("a (h n) -> a h n", h=2),
                              src.rearrange("(a n) -> a n", a=1).unsqueeze(1).to_broadcast([1, 2, FOX_HD])).then_inc(
                                  rows_in, 16)
            for i in (2, 3):
                act.wait_ge(x_in[i], 16)
                step(a.activation(sq4[:, :], xin[:, i, :], ACT.Square, accum_out=ssq[:, i:i + 1]), ssq_done, i - 1)
            act.wait_ge(wsm_in, 48)
            a.activation(wsmh[:, :, :], wsm[:, :, :], ACT.Copy).then_inc(wsmh_done, 1)
            split_hi(act, 0)
            split_hi(act, 1)
            act.wait_ge(cols_done, 1)
            for k in KORDER:
                act.wait_ge(full[k], turn(k, "hT") + 1)
                a.activation(hTh[:, k, :], whole(k), ACT.Copy,
                             scale=cols[:, R_NM + k:R_NM + k + 1]).then_inc(hTh_done, 1)

            act.wait_ge(wsm_zero, 2)
            act.dma_start(bias16[0:8, :], fox_f_bias.rearrange("(n a) -> n a", a=1)).then_inc(par_in, 16)
            act.dma_start(bias16[8:16, :], ssm_dt_bias.rearrange("(n a) -> n a", a=1)).then_inc(par_in, 16)
            act.dma_start(scale16[8:16, :], ssm_a_log.rearrange("(n a) -> n a", a=1)).then_inc(par_in, 16)
            act.dma_start(wlr[32:48, :], gla_w_lr).then_inc(par_in, 16)
            act.dma_start(nbc[:, :], ssm_out_norm.partition_broadcast(P)).then_inc(bc_in, 16)
            act.dma_start(dbc[:, :], ssm_d.partition_broadcast(P)).then_inc(bc_in, 16)
            act.dma_start(rbias[:, 0:4], b_router_grp.partition_broadcast(P)).then_inc(bc_in, 16)
            act.dma_start(rbias[:, 4:20], b_router_exp.partition_broadcast(P)).then_inc(bc_in, 16)
            act.wait_ge(par_in, 16 * 4)
            step(a.activation(scale16[:, :], scale16[:, :], ACT.Exp))

            tanhs = 0
            tanh_read = None
            for it in SCHED:
                kind = it[0]
                if kind == "small":
                    act.wait_ge(z_done, 1)
                    step(a.activation(sme[0:16, :], smz[0:16, :], ACT.Abs))
                    step(a.activation(sme[0:16, :], sme[0:16, :], ACT.Exp, scale=-1.0))
                    step(a.activation(sme[0:16, :], sme[0:16, :], ACT.Ln, bias=1.0), lnv_done, 1)
                elif kind == "loga":
                    pr = it[1]
                    act.wait_ge(free[5 + pr], turn(5 + pr, it) + 1)
                    act.wait_ge(rows_done, 1 + pr)
                    step(a.activation(sme[:, :], smz[:, :], ACT.Abs))
                    step(a.activation(sme[:, :], sme[:, :], ACT.Exp, scale=-1.0))
                    step(a.activation(sme[:, :], sme[:, :], ACT.Ln, bias=1.0), lnv_done, 2 + pr)
                elif kind == "tokrows":
                    act.wait_ge(toktr_done, 1)
                    step(a.activation(eacs[:, :, :], tokrow[:, :, 24:32], ACT.Exp), eacs_done, 1)
                elif kind == "piece":
                    _, b, kh, s, q = it
                    name = BLOCKS[b][0]
                    if q == 0 or kh == 0 or name in ("fq", "fk"):
                        continue
                    n = turn(s, ("block", b)) + 1
                    act.wait_ge(full[s], n)
                    if name in ("gr", "z"):
                        act.wait_ge(*(tanh_read or (xbc_done, 6)))
                        tanhs += 1
                        tanh_read = (free[s], n)
                        step(a.activation(tnhb[:, :], whole(s), ACT.Tanh, scale=0.5), tanh_done, tanhs)
                    elif name in ("xs", "bc"):
                        act.wait_ge(masks_done, 1)
                        dst = xbc[:, s if name == "xs" else 4 + s, 3:3 + T]
                        step(a.activation(dst, whole(s), ACT.Copy), free[s], n)
                    else:
                        dst = {"fv": fv, "gqk": gqk, "gv": gv}[name][:, s, :]
                        scale = GLA_DK ** -0.5 if name == "gqk" and s < 2 else 1.0
                        step(a.activation(dst, whole(s), ACT.Copy, scale=scale), free[s], n)
                elif kind == "square":
                    m = it[1]
                    b = 4 + m % 2
                    act.wait_ge(free[m % 4], turn(m % 4, ("block", m // 4)) + 1)
                    if m >= 2:
                        act.wait_ge(full[b], turn(b, ("qnorm", m - 2)) + 1)
                    step(a.activation(qsq[:, m % 2, :], (foxq if m < 4 else foxk)[:, m % 4, :], ACT.Square),
                         sq_done, m + 1)
                elif kind == "qnorm":
                    m = it[1]
                    b = 4 + m % 2
                    act.wait_ge(full[b], turn(b, it) + 1)
                    if m >= 2:
                        act.wait_ge(qn_done, m - 1)
                    step(a.activation(qrs[:, m % 2, :], whole(b), ACT.Ln, bias=epsc[:, 0:1]), free[b], turn(b, it) + 1)
                    step(a.activation(qrs[:, m % 2, :], qrs[:, m % 2, :], ACT.Exp, scale=-0.5), qrs_done, m + 1)
                elif kind == "score":
                    n = it[1]
                    b = 4 + n % 2
                    w = (n % NT + 1) * P
                    act.wait_ge(free[b], turn(b, it) + 1)
                    step(a.activation(prob[n % 3][:, 0:w], prob[n % 3][:, 0:w], ACT.Exp, scale=-1.0,
                                      bias=nmx[:, n:n + 1], accum_out=rsum[:, n:n + 1]), exp_done, n + 1)
                elif kind == "turn":
                    n = it[1]
                    w = (n % NT + 1) * P
                    act.wait_ge(full[6], turn(6, it) + 1)
                    if n >= 2:
                        wait_pv(act, n - 2)
                    step(a.activation(probT[:, n % 2, 0:w], bank[6][:, 0:w], ACT.Copy), free[6], turn(6, it) + 1)
                elif kind == "pv" and it[1] % 8 == 7:
                    pr = it[1] // 8
                    act.wait_ge(full[7], turn(7, ("opair", pr)) + 1)
                    step(a.activation(oAh[:, pr, :], whole(7), ACT.Copy), oAh_done, pr + 1)
                elif kind == "hi":
                    split_hi(act, it[1])
                elif kind == "gpiece":
                    _, part, s, q = it
                    if part == 1 and q == 1:
                        n = turn(s, ("gate", 0)) + 1
                        act.wait_ge(full[s], n)
                        act.wait_ge(obl_done, GLA_H)
                        step(a.activation(yacc[s][:, :], whole(s), ACT.Tanh, scale=0.5, bias=hcol[:, s:s + 1]),
                             free[s], n)
                elif kind == "squash":
                    s = it[1]
                    act.wait_ge(conv_done, s + 1)
                    if s:
                        act.wait_ge(xbc_done, s)
                    step(a.activation(tnhb[:, :], stt[:, :], ACT.Tanh), ctanh_done, s + 1)
                elif kind == "gdecay":
                    pr = it[1]
                    act.wait_ge(xbc_done, 6)
                    if pr:
                        act.wait_ge(gpre_done, pr)
                    step(a.activation(gex[:, 0, :], bcum[:, pr, :], ACT.Exp), gexp_done, 3 * pr + 1)
                    step(a.activation(gex[:, 1, :], bcum[:, pr, :], ACT.Exp, scale=-1.0), gexp_done, 3 * pr + 2)
                    act.wait_ge(garg_done, pr + 1)
                    step(a.activation(kend[:, :], kend[:, :], ACT.Exp), gexp_done, 3 * pr + 3)
                elif kind == "gprep":
                    pr = it[1]
                    act.wait_ge(full[4], turn(4, it) + 1)
                    if pr:
                        for par in range(2):
                            act.wait_ge(full[6 + par], turn(6 + par, ("kv", 0, par)) + 1)
                    step(a.activation(kendT[:, :, :], whole(4).rearrange("p (i t) -> p i t", t=P), ACT.Copy),
                         free[4], turn(4, it) + 1)
                elif kind == "go":
                    h = it[1]
                    b = 6 + h % 2
                    act.wait_ge(full[b], turn(b, ("go", h)) + 1)
                    if h >= 2:
                        act.wait_ge(obl_done, h - 1)
                    step(a.activation(oraw[:, h % 2, :], whole(b), ACT.Copy))
                    step(a.activation(osq[h % 2][:, :], whole(b), ACT.Square), free[b], turn(b, ("go", h)) + 1)
                elif kind == "gout":
                    pair = (2 * it[1], 2 * it[1] + 1)
                    for h in pair:
                        b = 4 + h % 2
                        n = turn(b, ("gout", h)) + 1
                        act.wait_ge(full[b], n)
                        step(a.activation(osq[h % 2][:, :], whole(b), ACT.Ln, bias=epsc[:, 0:1]), free[b], n)
                    for h in pair:
                        step(a.activation(osq[h % 2][:, :], osq[h % 2][:, :], ACT.Exp, scale=-0.5), ors_done, h + 1)
                    for h in pair:
                        act.wait_ge(ob_done, h + 1)
                        step(a.activation(oBh[:, gslot(h), :], oraw[:, h % 2, :], ACT.Copy), oBh_done, h + 1)
                elif kind == "ssdA":
                    i = it[1]
                    act.wait_ge(eacs_done, 1)
                    for h in range(SSM_H):
                        b = 4 + h // 4
                        if h % 4 == 0:
                            act.wait_ge(sd_last, 2 * i + 1 + h // 4)
                        ins = a.activation(dec[:, h, :], bank[b][:, (h % 4) * P:(h % 4) * P + P], ACT.Exp,
                                           bias=nacs[:, i, h:h + 1])
                        if h % 4 == 3:
                            step(ins, free[b], turn(b, ("bca" if b == 4 else "bcb", i)) + 1)
                        else:
                            step(ins)
                    act.wait_ge(sd_arg, i + 1)
                    step(a.activation(cdec[:, :], blast[:, :], ACT.Exp))
                    step(a.activation(toend[:, :], toend[:, :], ACT.Exp), sd_exp, i + 1)
                elif kind == "ssdB":
                    i = it[1]
                    act.wait_ge(sd_y, i + 1)
                    for gg in range(SSM_G):
                        step(a.activation(xdt[:, 256 * gg:256 * gg + 256], ysd[:, 256 * gg:256 * gg + 256], ACT.Square,
                                          accum_out=nss[:, gg:gg + 1]), *((sd_sq, i + 1) if gg else ()))
                elif kind == "ssdC":
                    i = it[1]
                    act.wait_ge(full[5], turn(5, ("yt", i)) + 1)
                    step(a.activation(oCh[:, :, i * P:(i + 1) * P], whole(5).rearrange("p (s t) -> p s t", t=P),
                                      ACT.Copy), oCh_done, i + 1)

            def y_hi(k):
                step(a.activation(yTh[k // 4][:, k % 4, :], yacc[k][:, :], ACT.Copy, scale=0.5), yh_done, k + 1)

            for g in range(1, 6):
                dh, r = GATES[g]
                u = U_GATE + 3 * g
                split_hi(act, u + 2)
                if g == 4:
                    act.wait_ge(y_added, 4)
                    for k in range(4):
                        y_hi(k)
                split_hi(act, u + 3)
                for s in range(4):
                    act.wait_ge(full[s], turn(s, ("gate", g)) + 1)
                    if g > 1:
                        act.wait_ge(free[4 + s], turn(4 + s, ("proj", g - 1)) + 1)
                    c = r * 8 + dh * 4 + s
                    step(a.activation(sg[:, s, :], whole(s), ACT.Tanh, scale=0.5, bias=hcol[:, c:c + 1]),
                         free[s], turn(s, ("gate", g)) + 1)
                split_hi(act, u + 4)
            for k in range(4, KD):
                act.wait_ge(y_added, k + 1)
                y_hi(k)
            act.dma_start(gainb[:, :], norm_ffn.partition_broadcast(P)).then_inc(gainb_in, 16)
            act.dma_start(wr[:, :, 0:4], w_router_grp.rearrange("(k p) n -> p k n", p=P)).then_inc(wr_in, 16)
            act.dma_start(wr[:, :, 4:20], w_router_exp.rearrange("(k p) n -> p k n", p=P)).then_inc(wr_in, 16)
            for q in range(4):
                split_hi(act, U_OUT + 2 + q)
            for i in range(NT):
                act.wait_ge(free[4 + i], turn(4 + i, ("out", 1)) + 1)
                step(a.activation(sq4[:, :], x1[:, i, :], ACT.Square, accum_out=ssq[:, i:i + 1]), x1_sq, i + 1)
                act.dma_start(acc[i * P:(i + 1) * P, :], x1[:, i, :]).then_inc(acc_in, 16)
            for k in range(4):
                act.wait_ge(full[k], turn(k, "h2T") + 1)
                step(a.activation(h2T[:, k, :], whole(k), ACT.Copy), free[k], turn(k, "h2T") + 1)
            for i in range(NT):
                act.wait_ge(xn2_done, i + 1)
                act.dma_start(h2d[i * P:(i + 1) * P, :], xn2[:, i, :]).then_inc(h2_out, 16)
            act.wait_ge(r_arg, 1)
            step(a.activation(g4[:, :, :], g4[:, :, :], ACT.Exp), r_exp, 1)
            act.wait_ge(r_arg, 2)
            step(a.activation(ex2[:, :], ex2[:, :], ACT.Exp), r_exp, 2)
            act.wait_ge(tab_in, 16)
            act.wait_ge(h2_out, 16 * NT)
            act.wait_ge(acc_in, 16 * NT)
            act.wait_ge(pad_out, 32)

            def x_hi(n, par, m=None, per=2):
                for half in range(2):
                    b = 4 + half
                    act.wait_ge(full[b], after(m, per, B0[b] + n + 1))
                    a.activation(xTh[:, par, 4 * half:4 * half + 4, :], whole(b).rearrange("p (j t) -> p j t", t=P),
                                 ACT.Copy).then_inc(xTh_done, 1)

            def hid_hi(n, m=None, per=2):
                act.wait_ge(full[6], after(m, per, B0[6] + n + 1))
                a.activation(hdh[:, :, :], whole(6).rearrange("p (j t) -> p j t", t=P), ACT.Copy).then_inc(hdh_done, 1)

            def silu(n, m=None, per=2):
                act.wait_ge(full[0], after(m, per, B0[0] + n + 1))
                if n:
                    act.wait_ge(free[1], after(m, per, B0[1] + n))
                a.activation(act1[:, :], whole(0), ACT.Silu).then_inc(free[0], 1)

            def rows_out(n, half, par, m=None, per=2, step_of_m=2):
                b = 2 + half
                act.wait_ge(full[b], after(m, per, B0[b] + n + 1))
                if n >= 2:
                    act.wait_ge(added, after(m, 16 * per, 16 * (n - 1 if n < NEXP else n)))
                if m is not None:
                    a.activation(pad[:, half:half + 1], epsc[:, 0:1], ACT.Copy)
                w = tab[:, n, 1:2] if m is None else tab[:, bass.ds(m * step_of_m + n, 1), 1:2].rearrange("p a b -> p (a b)")
                a.activation(yrow[:, par, half * 512:half * 512 + 512], whole(b), ACT.Copy,
                             scale=w.bitcast(F32)).then_inc(free[b], 1)

            def item(n, u, m=None):
                split_hi(act, u + 2, m)
                hid_hi(n - 1, m)
                split_hi(act, u + 3, m)
                silu(n, m)
                split_hi(act, u + 4, m)
                rows_out(n - 1, 0, (n - 1) % 2, m)
                split_hi(act, u + 5, m)
                rows_out(n - 1, 1, (n - 1) % 2, m)
                if n < NEXP - 1:
                    x_hi(n + 1, (n + 1) % 2, m)
                split_hi(act, u + 6, m)
                split_hi(act, u + 7, m)

            x_hi(0, 0)
            u = U_MOE
            split_hi(act, u + 2)
            split_hi(act, u + 3)
            silu(0)
            x_hi(1, 1)
            split_hi(act, u + 4)
            split_hi(act, u + 5)
            item(1, u + 4)
            item(2, u + 10)
            with act.Fori(1, 7) as m:
                item(1 + 2, u + 4 + 12, m - 1)
                item(2 + 2, u + 10 + 12, m - 1)
            item(15, u + 88)
            hid_hi(15)
            rows_out(15, 0, 1)
            rows_out(15, 1, 1)
            act.wait_ge(r_slot, 2)
            count = act.value_load(ovi[0:1, 0:1], min_val=0, max_val=OVF)
            with act.If(count > 0):
                with act.Fori(0, count) as m:
                    u = U_OVF
                    x_hi(NEXP, 0, m, 1)
                    for q in range(4):
                        split_hi(act, u + q, m, True)
                    silu(NEXP, m, 1)
                    split_hi(act, u + 4, m, True)
                    split_hi(act, u + 5, m, True)
                    hid_hi(NEXP, m, 1)
                    rows_out(NEXP, 0, 0, m, 1, 1)
                    rows_out(NEXP, 1, 0, m, 1, 1)
                act.nop()

        @block.vector
        def _(dve):
            v = nc.vector
            step = Serial(dve, dve_step)
            for i in range(2):
                dve.wait_ge(x_in[i], 16)
                step(v.tensor_tensor_reduce(xn[:, i, :], xin[:, i, :], xin[:, i, :], 1.0, 0.0, ALU.mult, ALU.add,
                                            ssq[:, i:i + 1]), ssq_dve, i + 1)
            dve.wait_ge(rst_done, 1)
            for i in range(NT):
                dve.wait_ge(x_in[i], 16)
                step(v.tensor_scalar(xn[:, i, :], xin[:, i, :], rst[:, i:i + 1], None, ALU.mult), xn_done, i + 1)
            dve.wait_ge(full[0], 1)
            step(v.tensor_copy(cols[:, 0:NROWS], bank[0][:, 0:NROWS]), free[0], 1)
            step(v.tensor_scalar(hcol[:, 0:54], cols[:, R_BG:R_BG + 54], 0.5, None, ALU.mult))
            step(v.tensor_scalar(gain1[:, 0:1], cols[:, R_GO:R_GO + 1], 0.5, None, ALU.mult))
            step(v.tensor_scalar(gain1[:, 1:2], cols[:, R_FQ:R_FQ + 1], FOX_HD ** -0.5, None, ALU.mult), cols_done, 1)
            dve.wait_ge(wsmh_done, 1)
            step(v.tensor_tensor(wsml[:, :, :], wsm[:, :, :], wsmh[:, :, :].bitcast(F32), ALU.subtract), wsml_done, 1)
            split_lo(dve, 0)
            split_lo(dve, 1)
            for n, k in enumerate(KORDER):
                dve.wait_ge(hTh_done, n + 1)
                step(v.scalar_tensor_tensor(out=hTl[:, k, :], in0=whole(k), scalar=cols[:, R_NM + k:R_NM + k + 1],
                                            in1=hTh[:, k, :].bitcast(F32), op0=ALU.mult, op1=ALU.subtract),
                     free[k], turn(k, "hT") + 1)

            def logsig(z, e, n):
                dve.wait_ge(lnv_done, n)
                step(v.scalar_tensor_tensor(out=z, in0=z, scalar=0.0, in1=e, op0=ALU.min, op1=ALU.subtract))

            def per_head(ap):
                return ap.unsqueeze(2).to_broadcast([P, SSM_H, 64])

            def heads(ap):
                return ap.rearrange("p (h d) -> p h d", d=64)

            tanhs = 0
            for it in SCHED:
                kind = it[0]
                if kind == "small":
                    dve.wait_ge(full[4], turn(4, "small") + 1)
                    dve.wait_ge(par_in, 16 * 4)
                    dve.wait_ge(consts, 2)
                    step(v.tensor_scalar(smz[0:16, :], bank[4][0:16, :], bias16[:, 0:1], sgn16[:, 0:1], ALU.add, ALU.mult),
                         z_done, 1)
                    step(v.tensor_copy(sm[32:48, :], bank[4][32:48, :]), free[4], turn(4, "small") + 1)
                    dve.wait_ge(lnv_done, 1)
                    step(v.scalar_tensor_tensor(out=sm[0:16, :], in0=smz[0:16, :], scalar=0.0, in1=sme[0:16, :],
                                                op0=ALU.min, op1=ALU.subtract))
                    dve.wait_ge(masks_done, 1)
                    step(v.tensor_scalar(sme[0:16, :], sm[0:16, :], scale16[:, 0:1], None, ALU.mult))
                    step(v.tensor_tensor_scan(cum16[:, :], reset16[:, :], sme[0:16, :], 0.0, ALU.mult, ALU.add),
                         rows_done, 1)
                elif kind == "loga":
                    pr = it[1]
                    b = 5 + pr
                    dve.wait_ge(full[b], turn(b, it) + 1)
                    step(v.tensor_scalar(smz[:, :], whole(b), cols[:, R_GB + pr:R_GB + pr + 1], None, ALU.add),
                         free[b], turn(b, it) + 1)
                    logsig(smz[:, :], sme[:, :], 2 + pr)
                    step(v.tensor_scalar(smz[:, :], smz[:, :], 1.0 / 16.0, None, ALU.mult))
                    step(v.tensor_tensor_scan(bcum[:, pr, :], reset64[:, :], smz[:, :], 0.0, ALU.mult, ALU.add),
                         rows_done, 2 + pr)
                elif kind == "tokrows":
                    dve.wait_ge(full[7], turn(7, it) + 1)
                    step(v.tensor_copy(tokrow[:, :, :], bank[7][:, 0:128].rearrange("p (i c) -> p i c", c=32)),
                         free[7], turn(7, it) + 1)
                    step(v.tensor_scalar(dtok[:, :, :], tokrow[:, :, 8:16], -1.0, None, ALU.mult))
                    step(v.tensor_scalar(nacs[:, :, :], tokrow[:, :, 24:32], -1.0, None, ALU.mult), toktr_done, 1)
                elif kind == "piece":
                    _, b, kh, s, q = it
                    name = BLOCKS[b][0]
                    if q == 0 or kh == 0 or name not in ("fq", "fk", "gr", "z"):
                        continue
                    n = turn(s, ("block", b)) + 1
                    if name in ("fq", "fk"):
                        dve.wait_ge(full[s], n)
                        step(v.tensor_copy((foxq if name == "fq" else foxk)[:, s, :], whole(s)), free[s], n)
                    else:
                        tanhs += 1
                        dve.wait_ge(tanh_done, tanhs)
                        step(v.scalar_tensor_tensor(out=(grs if name == "gr" else zs)[:, s, :], in0=tnhb[:, :], scalar=1.0,
                                                    in1=whole(s), op0=ALU.add, op1=ALU.mult), free[s], n)
                elif kind == "qnorm":
                    m = it[1]
                    dve.wait_ge(qrs_done, m + 1)
                    q = (foxq if m < 4 else foxk)[:, m % 4, :]
                    gain = gain1[:, 1:2] if m < 4 else cols[:, R_FK:R_FK + 1]
                    step(v.scalar_tensor_tensor(out=q, in0=q, scalar=gain, in1=qrs[:, m % 2, :],
                                                op0=ALU.mult, op1=ALU.mult), qn_done, m + 1)
                elif kind == "cb":
                    h = it[1]
                    dve.wait_ge(full[6], turn(6, it) + 1)
                    step(v.tensor_copy(cbt[:, h % 2, :], whole(6)), free[6], turn(6, it) + 1)
                elif kind == "score":
                    n = it[1]
                    b = 4 + n % 2
                    w = (n % NT + 1) * P
                    dve.wait_ge(full[b], turn(b, it) + 1)
                    if n >= 3:
                        dve.wait_ge(full[6], turn(6, ("turn", n - 3)) + 1)
                    step(v.tensor_tensor_reduce(prob[n % 3][:, 0:w], bank[b][:, 0:w], cbt[:, (n // NT) % 2, 0:w],
                                                -1.0, 3.0e38, ALU.add, ALU.min, nmx[:, n:n + 1]), free[b], turn(b, it) + 1)
                elif kind == "lo":
                    split_lo(dve, it[1])
                elif kind == "norm":
                    n = it[1]
                    w = (n % NT + 1) * P
                    dve.wait_ge(exp_done, n + 1)
                    step(v.reciprocal(rinv[:, n:n + 1], rsum[:, n:n + 1]))
                    step(v.tensor_scalar(prob[n % 3][:, 0:w], prob[n % 3][:, 0:w], rinv[:, n:n + 1], None, ALU.mult),
                         prob_done, n + 1)
                elif kind == "pv" and it[1] % 8 == 7:
                    pr = it[1] // 8
                    dve.wait_ge(oAh_done, pr + 1)
                    step(v.tensor_tensor(oAl[:, pr, :], whole(7), oAh[:, pr, :].bitcast(F32), ALU.subtract),
                         free[7], turn(7, ("opair", pr)) + 1)
                elif kind == "gpiece":
                    _, part, s, q = it
                    if part == 2 and q == 1:
                        n = turn(s, ("proj", 0)) + 1
                        dve.wait_ge(full[s], n)
                        step(v.scalar_tensor_tensor(out=yacc[s][:, :], in0=yacc[s][:, :], scalar=1.0, in1=whole(s),
                                                    op0=ALU.add, op1=ALU.mult), free[s], n)
                elif kind == "conv":
                    s = it[1]
                    dve.wait_ge(masks_done, 1)
                    dve.wait_ge(free[s % 4], turn(s % 4, ("block", 3 + s // 4)) + 1)
                    c = stt[:, :]
                    step(v.tensor_scalar(c, xbc[:, s, 0:T], hcol[:, 24 + s:25 + s], hcol[:, 48 + s:49 + s],
                                         ALU.mult, ALU.add))
                    for j in range(1, SSM_CONV):
                        w = hcol[:, 24 + 6 * j + s:25 + 6 * j + s]
                        ins = v.scalar_tensor_tensor(out=c, in0=xbc[:, s, j:j + T], scalar=w, in1=c,
                                                     op0=ALU.mult, op1=ALU.add)
                        step(ins, *((conv_done, s + 1) if j == SSM_CONV - 1 else ()))
                elif kind == "squash":
                    s = it[1]
                    dve.wait_ge(ctanh_done, s + 1)
                    step(v.scalar_tensor_tensor(out=xbc[:, s, 3:3 + T], in0=tnhb[:, :], scalar=1.0, in1=stt[:, :],
                                                op0=ALU.add, op1=ALU.mult), xbc_done, s + 1)
                elif kind == "gdecay":
                    pr = it[1]
                    q, k = gqk[:, pr, :], gqk[:, 2 + pr, :]
                    bc = bcum[:, pr, :].rearrange("p (c t) -> p c t", t=CHUNK)
                    if pr:
                        dve.wait_ge(full[4], turn(4, ("gprep", 0)) + 1)
                    else:
                        dve.wait_ge(full[7], turn(7, ("opair", 3)) + 1)
                        step(v.memset(gat[:, :, :], 0.0))
                    step(v.tensor_tensor(kend[:, :].rearrange("p (c t) -> p c t", t=CHUNK),
                                         bc[:, :, CHUNK - 1:CHUNK].to_broadcast([P, 8, CHUNK]), bc, ALU.subtract),
                         garg_done, pr + 1)
                    dve.wait_ge(gexp_done, 3 * pr + 3)
                    step(v.tensor_tensor(kend[:, :], kend[:, :], k, ALU.mult), kend_done, pr + 1)
                    step(v.tensor_tensor(k, k, gex[:, 1, :], ALU.mult))
                    step(v.tensor_copy(gdec[:, :].unsqueeze(2),
                                       gex[:, 0, :].rearrange("p (c t) -> p c t", t=CHUNK)[:, :, CHUNK - 1:CHUNK]))
                    step(v.tensor_tensor(q, q, gex[:, 0, :], ALU.mult), gpre_done, pr + 1)
                elif kind == "kv":
                    pr = it[1]
                    dve.wait_ge(full[6], turn(6, ("kv", pr, 0)) + 1)
                    dve.wait_ge(full[7], turn(7, ("kv", pr, 1)) + 1)
                    if pr:
                        for h in range(2):
                            dve.wait_ge(full[6 + h], turn(6 + h, ("go", h)) + 1)
                    for c in range(7):
                        b = 6 + c % 2
                        kv = bank[b][:, (c // 2) * P:(c // 2) * P + P]
                        if c == 0:
                            ins = v.tensor_copy(prev[:, 1, :], kv)
                        else:
                            ins = v.scalar_tensor_tensor(out=prev[:, c + 1, :], in0=prev[:, c, :], scalar=gdec[:, c:c + 1],
                                                         in1=kv, op0=ALU.mult, op1=ALU.add)
                        step(ins, *((free[b], turn(b, ("kv", pr, b - 6)) + 1) if c >= 5 else ()))
                elif kind == "gs":
                    h = it[1]
                    b = 4 + h % 2
                    dve.wait_ge(full[b], turn(b, ("gs", h)) + 1)
                    if h >= 2:
                        dve.wait_ge(full[6 + h % 2], turn(6 + h % 2, ("go", h - 2)) + 1)
                    dve.wait_ge(glam_done, 1)
                    step(v.copy_predicated(gat[:, h % 2, :], glam[:, :, :].rearrange("p i t -> p (i t)").bitcast(I32),
                                           whole(b)), free[b], turn(b, ("gs", h)) + 1)
                elif kind == "gout":
                    pair = (2 * it[1], 2 * it[1] + 1)
                    for h in pair:
                        o = oraw[:, h % 2, :]
                        dve.wait_ge(ors_done, h + 1)
                        step(v.scalar_tensor_tensor(out=o, in0=o, scalar=gain1[:, 0:1], in1=osq[h % 2][:, :],
                                                    op0=ALU.mult, op1=ALU.mult))
                        step(v.tensor_tensor(o, o, grs[:, h, :], ALU.mult), ob_done, h + 1)
                    for h in pair:
                        dve.wait_ge(oBh_done, h + 1)
                        step(v.tensor_tensor(oBl[:, h, :], oraw[:, h % 2, :], oBh[:, gslot(h), :].bitcast(F32),
                                             ALU.subtract), obl_done, h + 1)
                elif kind == "ssdprep":
                    step(v.memset(cblk[:, :, :], 0.0))
                    step(v.tensor_copy(cblk[0:64, 0, :], xbc[0:64, 5, 3:3 + T]))
                    step(v.tensor_copy(cblk[64:128, 1, :], xbc[64:128, 5, 3:3 + T]), cblk_done, 1)
                    dve.wait_ge(bc_in, 64)
                    dve.wait_ge(eacs_done, 1)
                elif kind == "ssdA":
                    i = it[1]
                    for q, name in enumerate(("bca", "bcb")):
                        dve.wait_ge(full[4 + q], turn(4 + q, (name, i)) + 1)
                        step(v.tensor_copy(blast[:, 4 * q:4 * q + 4].unsqueeze(2),
                                           whole(4 + q).rearrange("p (h t) -> p h t", t=P)[:, :, P - 1:P]),
                             sd_last, 2 * i + 1 + q)
                    step(v.tensor_tensor(toend[:, :], blast[:, :], nacs[:, i, :], ALU.add), sd_arg, i + 1)
                    n = turn(7, ("xt", i)) + 1
                    dve.wait_ge(full[7], n)
                    step(v.tensor_tensor(heads(xdt[:, :]), heads(whole(7)), per_head(dtok[:, i, :]), ALU.mult))
                    step(v.tensor_tensor(heads(ysd[:, :]), heads(whole(7)), per_head(dbc[:, :]), ALU.mult), free[7], n)
                    dve.wait_ge(sd_exp, i + 1)
                    step(v.tensor_tensor(heads(xdt2[:, :]), heads(xdt[:, :]), per_head(toend[:, :]), ALU.mult))
                    n = turn(6, ("sc", i)) + 1
                    dve.wait_ge(full[6], n)
                    step(v.tensor_copy(btok[:, :], bank[6][:, 256:384]))
                    for q in range(SSM_G):
                        ins = v.tensor_tensor(dec[:, 4 * q:4 * q + 4, :], dec[:, 4 * q:4 * q + 4, :],
                                              bank[6][:, q * P:q * P + P].unsqueeze(1).to_broadcast([P, 4, P]), ALU.mult)
                        step(ins, *((free[6], n) if q else ()))
                elif kind == "ssdB":
                    i = it[1]
                    n = turn(7, ("yi", i)) + 1
                    dve.wait_ge(full[7], n)
                    step(v.tensor_tensor(ysd[:, :], ysd[:, :], whole(7), ALU.add), free[7], n)
                    if i:
                        n = turn(6, ("ye", i)) + 1
                        dve.wait_ge(full[6], n)
                        step(v.tensor_tensor(heads(xdt[:, :]), heads(whole(6)), per_head(eacs[:, i, :]), ALU.mult), free[6], n)
                        step(v.tensor_tensor(ysd[:, :], ysd[:, :], xdt[:, :], ALU.add))
                    step(v.scalar_tensor_tensor(out=ysd[:, :], in0=ysd[:, :], scalar=0.5, in1=zs[:, i, :],
                                                op0=ALU.mult, op1=ALU.mult), sd_y, i + 1)
                    if i == 0:
                        step(v.memset(stt[:, :], 0.0))
                    if i < NT - 1:
                        n = turn(4, ("st", i)) + 1
                        dve.wait_ge(full[4], n)
                        for q in range(SSM_G):
                            r = slice(64 * q, 64 * q + 64)
                            state = stt[r, 256 * q:256 * q + 256]
                            if i:
                                step(v.tensor_tensor(state.rearrange("p (h d) -> p h d", d=64),
                                                     state.rearrange("p (h d) -> p h d", d=64),
                                                     cdec[r, 4 * q:4 * q + 4].unsqueeze(2).to_broadcast([64, 4, 64]), ALU.mult))
                            step(v.tensor_tensor(state, state, bank[4][r, 256 * q:256 * q + 256], ALU.add),
                                 *((free[4], n) if q else ()))
                    dve.wait_ge(sd_rst, i + 1)
                    for q in range(SSM_G):
                        c = slice(256 * q, 256 * q + 256)
                        step(v.scalar_tensor_tensor(out=ysd[:, c], in0=ysd[:, c], scalar=nrs[:, q:q + 1], in1=nbc[:, c],
                                                    op0=ALU.mult, op1=ALU.mult), *((sd_norm, i + 1) if q else ()))
                elif kind == "ssdC":
                    i = it[1]
                    dve.wait_ge(oCh_done, i + 1)
                    step(v.tensor_tensor(oCl[:, :, i * P:(i + 1) * P], whole(5).rearrange("p (s t) -> p s t", t=P),
                                         oCh[:, :, i * P:(i + 1) * P].bitcast(F32), ALU.subtract),
                         free[5], turn(5, ("yt", i)) + 1)

            def y_lo(k):
                dve.wait_ge(yh_done, k + 1)
                step(v.scalar_tensor_tensor(out=yTl[k // 4][:, k % 4, :], in0=yacc[k][:, :], scalar=0.5,
                                            in1=yTh[k // 4][:, k % 4, :].bitcast(F32), op0=ALU.mult, op1=ALU.subtract),
                     y_done, k + 1)

            for g in range(1, 6):
                dh, r = GATES[g]
                u = U_GATE + 3 * g
                split_lo(dve, u + 2)
                if g == 4:
                    for k in range(4):
                        y_lo(k)
                split_lo(dve, u + 3)
                split_lo(dve, u + 4)
                for s in range(4):
                    n = turn(4 + s, ("proj", g)) + 1
                    dve.wait_ge(full[4 + s], n)
                    dve.wait_ge(free[s], turn(s, ("gate", g)) + 1)
                    y = yacc[dh * 4 + s][:, :]
                    dst = y if r == 0 else ytmp[:, s % 2, :]
                    step(v.scalar_tensor_tensor(out=dst, in0=sg[:, s, :], scalar=1.0, in1=whole(4 + s),
                                                op0=ALU.add, op1=ALU.mult), free[4 + s], n)
                    if r:
                        step(v.tensor_tensor(y, y, dst, ALU.add), *((y_added, dh * 4 + s + 1) if r == 2 else ()))
                    if g == 5 and s:
                        y_lo(3 + s)
            y_lo(KD - 1)
            dve.wait_ge(xr_in, 16 * NT)
            for nh in range(2):
                split_lo(dve, U_OUT + 2 * nh + 2)
                split_lo(dve, U_OUT + 2 * nh + 3)
                for i in range(NT):
                    b = 4 * nh + i
                    n = turn(b, ("out", nh)) + 1
                    c = slice(nh * 512, nh * 512 + 512)
                    dve.wait_ge(full[b], n)
                    step(v.tensor_tensor(x1[:, i, c], x1[:, i, c], whole(b), ALU.add), free[b], n)
            dve.wait_ge(wr_in, 32)
            step(v.tensor_tensor(wr[:, :, :], wr[:, :, :], cols[:, R_NF:R_NF + KD].unsqueeze(2).to_broadcast([P, KD, 20]),
                                 ALU.mult), wr_done, 1)
            for k in range(4, KD):
                n = turn(k, "h2T") + 1
                dve.wait_ge(full[k], n)
                step(v.tensor_copy(h2T[:, k, :], whole(k)), free[k], n)
            dve.wait_ge(r2_done, 1)
            dve.wait_ge(gainb_in, 16)
            for i in range(NT):
                step(v.scalar_tensor_tensor(out=xn2[:, i, :], in0=x1[:, i, :], scalar=rst[:, i:i + 1], in1=gainb[:, :],
                                            op0=ALU.mult, op1=ALU.mult), xn2_done, i + 1)

            def b4(ap):
                return ap.unsqueeze(2).to_broadcast([P, NT, 4])

            def best(values, high, onehot):
                step(v.tensor_reduce(high, values, AX, ALU.max))
                step(v.tensor_tensor(onehot, values, b4(high), ALU.is_equal))
                step(v.tensor_tensor(gv4[:, :, :], onehot, prio[:, :].unsqueeze(1).to_broadcast([P, NT, 4]), ALU.mult))
                step(v.tensor_reduce(gsum[:, :], gv4[:, :, :], AX, ALU.max))
                step(v.tensor_tensor(onehot, gv4[:, :, :], b4(gsum[:, :]), ALU.is_equal))

            dve.wait_ge(route_consts, 2)
            dve.wait_ge(pad_out, 32)
            dve.wait_ge(full[0], turn(0, "logitsT") + 1)
            step(v.tensor_copy(lgT[:, :], bank[0][0:20, :]), free[0], turn(0, "logitsT") + 1)
            dve.wait_ge(full[2], turn(2, "logits") + 1)
            step(v.tensor_tensor(lg[:, :, :], bank[2][:, 0:80].rearrange("p (i c) -> p i c", c=20),
                                 rst[:, :].unsqueeze(2).to_broadcast([P, NT, 20]), ALU.mult),
                 free[2], turn(2, "logits") + 1)
            step(v.tensor_tensor(lg[:, :, :], lg[:, :, :], rbias[:, :].unsqueeze(1).to_broadcast([P, NT, 20]), ALU.add))
            best(lg[:, :, 0:4], gmx[:, :], goh[:, :, :])
            step(v.tensor_tensor(g4[:, :, :], lg[:, :, 0:4], b4(gmx[:, :]), ALU.subtract), r_arg, 1)
            def grouped(ap):
                return ap.rearrange("p i (g e) -> p i g e", e=EPG)

            group_of = goh[:, :, :].unsqueeze(3).to_broadcast([P, NT, NEG, EPG])
            step(v.tensor_tensor(grouped(ein16[:, :, :]), grouped(lg[:, :, 4:20]), group_of, ALU.mult))
            step(v.tensor_reduce(ein[:, :, :], ein16[:, :, :].rearrange("p i (g e) -> p i e g", e=EPG), AX, ALU.add))
            best(ein[:, :, :], m1[:, :], oh1[:, :, :])
            step(v.scalar_tensor_tensor(out=ein[:, :, :], in0=oh1[:, :, :], scalar=NEGBIG, in1=ein[:, :, :],
                                        op0=ALU.mult, op1=ALU.add))
            best(ein[:, :, :], m2[:, :], oh2[:, :, :])
            step(v.tensor_tensor(ex2[:, :], m2[:, :], m1[:, :], ALU.subtract), r_arg, 2)
            for a16, oh in ((a1, oh1), (a2, oh2)):
                step(v.tensor_tensor(grouped(a16[:, :, :]), oh[:, :, :].unsqueeze(2).to_broadcast([P, NT, NEG, EPG]),
                                     group_of, ALU.mult))
            step(v.tensor_tensor(ab[:, :, :], a1[:, :, :], a2[:, :, :], ALU.add), r_ab, 1)
            dve.wait_ge(r_exp, 2)
            step(v.tensor_reduce(gsum[:, :], g4[:, :, :], AX, ALU.add))
            step(v.tensor_scalar(m1[:, :], ex2[:, :], 1.0, None, ALU.add))
            step(v.tensor_tensor(m1[:, :], m1[:, :], gsum[:, :], ALU.mult))
            step(v.reciprocal(w12[:, 0, :], m1[:, :]))
            step(v.tensor_tensor(w12[:, 1, :], w12[:, 0, :], ex2[:, :], ALU.mult))
            for k in range(2):
                step(v.tensor_copy(entry[:, k, :, 1:2].bitcast(F32), w12[:, k, :].unsqueeze(2)))
            dve.wait_ge(full[1], turn(1, "pos") + 1)
            step(v.tensor_copy(nexp[:, :], bank[1][:, 64:80]))
            step(v.tensor_scalar(extra[:, :], nexp[:, :], 128.0, None, ALU.is_gt))
            for lim in (256.0, 384.0):
                step(v.scalar_tensor_tensor(out=extra[:, :], in0=nexp[:, :], scalar=lim, in1=extra[:, :],
                                            op0=ALU.is_gt, op1=ALU.add))
            step(v.memset(one16[:, :], 1.0))
            step(v.tensor_tensor_scan(incl[:, :], one16[:, :], extra[:, :], 0.0, ALU.mult, ALU.add))
            step(v.tensor_tensor(diff[:, :], incl[:, :], extra[:, :], ALU.subtract))
            step(v.tensor_scalar(diff[:, :], diff[:, :], 128.0, 128.0 * (NEXP - 1), ALU.mult, ALU.add))
            step(v.tensor_tensor(diff[:, :], diff[:, :], e128[:, :], ALU.subtract))
            place = bank[1][:, 0:64].rearrange("p (i e) -> p i e", e=16)

            def over_tokens(ap):
                return ap.unsqueeze(1).to_broadcast([P, NT, 16])
            step(v.tensor_scalar(over[:, :, :], place, 128.0, None, ALU.is_ge))
            step(v.tensor_tensor(over[:, :, :], over[:, :, :], over_tokens(diff[:, :]), ALU.mult))
            step(v.tensor_tensor(slot[:, :, :], over[:, :, :], place, ALU.add), free[1], turn(1, "pos") + 1)
            step(v.tensor_tensor(slot[:, :, :], slot[:, :, :], over_tokens(e128[:, :]), ALU.add))
            for k, a16 in enumerate((a1, a2)):
                step(v.tensor_tensor(a16[:, :, :], a16[:, :, :], slot[:, :, :], ALU.mult))
                step(v.tensor_reduce(sl12[:, k, :], a16[:, :, :], AX, ALU.add))
            step(v.tensor_copy(sli[:, :, :], sl12[:, :, :]), r_slot, 1)
            step(v.tensor_tensor(ovm[:, :, :], incl[:, :].unsqueeze(1).to_broadcast([P, OVF, 16]),
                                 iota7[:, :].unsqueeze(2).to_broadcast([P, OVF, 16]), ALU.is_le))
            step(v.tensor_reduce(ove[:, 1:8], ovm[:, :, :], AX, ALU.add))
            step(v.tensor_copy(ove[:, 0:1], incl[:, 15:16]))
            step(v.tensor_scalar(ove[:, :], ove[:, :], 15.0, None, ALU.min))
            step(v.tensor_copy(ovi[:, :], ove[:, :]), r_slot, 2)

            def x_lo(n, par, m=None, per=2):
                for half in range(2):
                    dve.wait_ge(xTh_done, after(m, 2 * per, 2 * n + half + 1))
                    b = 4 + half
                    v.tensor_tensor(xTl[:, par, 4 * half:4 * half + 4, :], whole(b).rearrange("p (j t) -> p j t", t=P),
                                    xTh[:, par, 4 * half:4 * half + 4, :].bitcast(F32), ALU.subtract).then_inc(free[b], 1)

            def hid_lo(n, m=None, per=2):
                dve.wait_ge(hdh_done, after(m, per, n + 1))
                v.tensor_tensor(hdl[:, :, :], whole(6).rearrange("p (j t) -> p j t", t=P), hdh[:, :, :].bitcast(F32),
                                ALU.subtract).then_inc(free[6], 1)

            def gated(n, m=None, per=2):
                dve.wait_ge(full[1], after(m, per, B0[1] + n + 1))
                dve.wait_ge(free[0], after(m, per, B0[0] + n + 1))
                v.tensor_tensor(hid[:, :], act1[:, :], whole(1), ALU.mult).then_inc(free[1], 1)

            def item(n, u, m=None):
                split_lo(dve, u + 2, m)
                hid_lo(n - 1, m)
                split_lo(dve, u + 3, m)
                split_lo(dve, u + 4, m)
                split_lo(dve, u + 5, m)
                if n < NEXP - 1:
                    x_lo(n + 1, (n + 1) % 2, m)
                split_lo(dve, u + 6, m)
                split_lo(dve, u + 7, m)
                gated(n, m)

            x_lo(0, 0)
            u = U_MOE
            split_lo(dve, u + 2)
            split_lo(dve, u + 3)
            x_lo(1, 1)
            split_lo(dve, u + 4)
            split_lo(dve, u + 5)
            gated(0)
            with dve.Fori(0, 7) as m:
                item(1, u + 4, m)
                item(2, u + 10, m)
            item(15, u + 88)
            hid_lo(15)
            count = dve.value_load(ovi[0:1, 0:1], min_val=0, max_val=OVF)
            with dve.If(count > 0):
                with dve.Fori(0, count) as m:
                    u = U_OVF
                    x_lo(NEXP, 0, m, 1)
                    for q in range(6):
                        if q == 4:
                            gated(NEXP, m, 1)
                        split_lo(dve, u + q, m, True)
                    hid_lo(NEXP, m, 1)
                dve.nop()

        @block.tensor
        def _(pe):
            t = nc.tensor

            def passes(out, lhs, rhs, start, stop):
                t.matmul(out, lhs[0], rhs[0], start=start, stop=False)
                t.matmul(out, lhs[0], rhs[1], start=False, stop=False)
                return t.matmul(out, lhs[1], rhs[0], start=False, stop=stop)

            def take(b, key):
                n = turn(b, key)
                if n:
                    pe.wait_ge(free[b], n)

            pe.wait_ge(consts, 1)
            pe.wait_ge(rows_in, 16 * 9)
            t.transpose(bank[0][:, 0:NROWS], rows[:, :], ident[0:NROWS, 0:NROWS]).then_inc(full[0], 1)
            pe.wait_ge(xn_done, NT)
            for k in KORDER:
                if k == 0:
                    take(0, "hT")
                for i in range(NT):
                    ins = t.transpose(bank[k][:, i * P:(i + 1) * P], xn[:, i, k * P:(k + 1) * P], ident[:, :])
                ins.then_inc(full[k], 1)

            for it in SCHED:
                kind = it[0]
                if kind == "small":
                    pe.wait_ge(wsml_done, 1)
                    for k in KORDER:
                        pe.wait_ge(free[k], turn(k, "hT") + 1)
                        ins = passes(whole(4), (wsmh[:, k, :], wsml[:, k, :]), (hTh[:, k, :], hTl[:, k, :]),
                                     k == KORDER[0], k == KORDER[-1])
                    ins.then_inc(full[4], 1)
                elif kind == "loga":
                    pr = it[1]
                    take(5 + pr, it)
                    pe.wait_ge(free[4], turn(4, "small") + 1)
                    pe.wait_ge(par_in, 16 * 4)
                    t.matmul(whole(5 + pr), wlr[32:48, pr * P:(pr + 1) * P], sm[32:48, :], start=True,
                             stop=True).then_inc(full[5 + pr], 1)
                elif kind == "tokrows":
                    take(7, it)
                    pe.wait_ge(rows_done, 1)
                    for i in range(NT):
                        for q, src in enumerate((sm, cum16)):
                            ins = t.transpose(bank[7][:, 32 * i + 16 * q:32 * i + 16 * q + 16],
                                              src[0:16, i * P:(i + 1) * P], ident[0:16, 0:16])
                    ins.then_inc(full[7], 1)
                elif kind == "piece":
                    _, b, kh, s, q = it
                    u = 2 * b + kh
                    slot_u = u % RING
                    if s == 0 and q == 0:
                        pe.wait_ge(lo_ready, u + 1)
                    if kh == 0 and q == 0:
                        take(s, ("block", b))
                    for j in (2 * q, 2 * q + 1):
                        k = 4 * kh + j
                        if BLOCKS[b][3] == "T":
                            c = slice(s * P, (s + 1) * P)
                            lhs = whi[:, slot_u, j, c], wlo[:, slot_u, j, c]
                            rhs = hTh[:, k, :], hTl[:, k, :]
                        else:
                            c = slice(s * P, (s + 1) * P)
                            lhs = hTh[:, k, c], hTl[:, k, c]
                            rhs = whi[:, slot_u, j, :], wlo[:, slot_u, j, :]
                        ins = passes(whole(s), lhs, rhs, k == 0, k == KD - 1)
                    if q == 1 and kh == 1:
                        ins.then_inc(full[s], 1)
                    elif q == 1 and s == SUBS[b] - 1:
                        ins.then_inc(unit_used, 1)
                elif kind == "gpiece":
                    _, part, s, q = it
                    u = U_GATE + part
                    c = slice(s * P, (s + 1) * P)
                    if s == 0 and q == 0:
                        pe.wait_ge(lo_ready, u + 1)
                    if part != 1 and q == 0:
                        take(s, ("gate" if part == 0 else "proj", 0))
                    for j in (2 * q, 2 * q + 1):
                        k = 4 * part + j
                        rhs = (oAh[:, j, :], oAl[:, j, :]) if part == 2 else (hTh[:, k, :], hTl[:, k, :])
                        ins = passes(whole(s), (whi[:, u % RING, j, c], wlo[:, u % RING, j, c]), rhs,
                                     part != 1 and j == 0, part != 0 and j == 3)
                    if q == 1 and part > 0:
                        ins.then_inc(full[s], 1)
                    elif q == 1 and s == 3:
                        ins.then_inc(unit_used, 1)
                elif kind == "qnorm":
                    m = it[1]
                    b = 4 + m % 2
                    take(b, it)
                    pe.wait_ge(masks_done, 1)
                    pe.wait_ge(sq_done, m + 1)
                    t.matmul(whole(b), blk64[:, :], qsq[:, m % 2, :], start=True, stop=True).then_inc(full[b], 1)
                elif kind == "cb":
                    h = it[1]
                    take(6, it)
                    t.matmul(whole(6), sgni[:, h:h + 1].to_broadcast([16, P]), cum16[:, :], start=True,
                             stop=True).then_inc(full[6], 1)
                elif kind == "score":
                    n = it[1]
                    h, i = divmod(n, NT)
                    b = 4 + n % 2
                    r = slice((h % 2) * 64, (h % 2) * 64 + 64)
                    take(b, it)
                    if n == 0:
                        pe.wait_ge(qn_done, 8)
                    t.matmul(bank[b][:, 0:(i + 1) * P], foxq[r, h // 2, i * P:(i + 1) * P],
                             foxk[r, h // 2, 0:(i + 1) * P], start=True, stop=True)
                    t.matmul(bank[b][:, i * P:(i + 1) * P], identb[:, :], maskq[:, :], start=False, stop=True,
                             skip_group_check=True).then_inc(full[b], 1)
                elif kind == "turn":
                    n = it[1]
                    take(6, it)
                    pe.wait_ge(prob_done, n + 1)
                    for k in range(n % NT + 1):
                        ins = t.transpose(bank[6][:, k * P:(k + 1) * P], prob[n % 3][:, k * P:(k + 1) * P], ident[:, :])
                    ins.then_inc(full[6], 1)
                elif kind == "pv":
                    n = it[1]
                    h, i = divmod(n, NT)
                    pe.wait_ge(free[6], turn(6, ("turn", n)) + 1)
                    if n == 0:
                        for q in range(NT):
                            pe.wait_ge(free[q], turn(q, ("block", 2)) + 1)
                    if n % 8 == 0:
                        take(7, ("opair", n // 8))
                    out = bank[7][(h % 2) * 64:(h % 2) * 64 + 64, i * P:(i + 1) * P]
                    for k in range(i + 1):
                        ins = t.matmul(out, fv[:, k, h * 64:h * 64 + 64], probT[:, n % 2, k * P:(k + 1) * P],
                                       start=k == 0, stop=k == i)
                    ins.then_inc(full[7] if n % 8 == 7 else pv_done, 1)
                elif kind == "gprep":
                    take(4, it)
                    pe.wait_ge(kend_done, it[1] + 1)
                    for i in range(NT):
                        ins = t.transpose(bank[4][:, i * P:(i + 1) * P], kend[:, i * P:(i + 1) * P], ident[:, :])
                    ins.then_inc(full[4], 1)
                elif kind == "kv":
                    pr = it[1]
                    take(6, ("kv", pr, 0))
                    take(7, ("kv", pr, 1))
                    pe.wait_ge(free[4], turn(4, ("gprep", pr)) + 1)
                    for par in range(2):
                        rows_c = slice(par * 64, par * 64 + 64)
                        for c in range(par, 7, 2):
                            for hh in range(2):
                                h = 2 * pr + hh
                                ins = t.matmul(bank[6 + par][hh * 64:hh * 64 + 64, (c // 2) * P:(c // 2) * P + P],
                                               kendT[rows_c, c // 2, hh * 64:hh * 64 + 64],
                                               gv[rows_c, c // 2, h * P:(h + 1) * P], start=True, stop=True)
                        ins.then_inc(full[6 + par], 1)
                elif kind in ("gs", "go"):
                    h = it[1]
                    pr, hh = divmod(h, 2)
                    r = slice(hh * 64, hh * 64 + 64)
                    q, k = gqk[r, pr, :], gqk[r, 2 + pr, :]
                    b = 4 + hh
                    if kind == "gs":
                        take(b, it)
                        pe.wait_ge(gpre_done, pr + 1)
                        for i in range(NT):
                            c = slice(i * P, (i + 1) * P)
                            ins = t.matmul(bank[b][:, c], k[:, c], q[:, c], start=True, stop=True)
                        ins.then_inc(full[b], 1)
                        continue
                    take(6 + hh, ("go", h))
                    pe.wait_ge(free[b], turn(b, ("gs", h)) + 1)
                    pe.wait_ge(free[6], turn(6, ("kv", pr, 0)) + 1)
                    for i in range(NT):
                        c = slice(i * P, (i + 1) * P)
                        t.matmul(bank[6 + hh][:, c], gv[:, i, h * P:(h + 1) * P], gat[:, hh, c], start=True,
                                 stop=True, skip_group_check=True)
                        for ch in (2 * i, 2 * i + 1):
                            if ch:
                                cc = slice(ch * CHUNK, (ch + 1) * CHUNK)
                                ins = t.matmul(bank[6 + hh][:, cc], prev[r, ch, :], q[:, cc], start=False,
                                               stop=True, skip_group_check=True)
                    ins.then_inc(full[6 + hh], 1)
                elif kind == "gout":
                    for h in (2 * it[1], 2 * it[1] + 1):
                        b = 4 + h % 2
                        take(b, ("gout", h))
                        pe.wait_ge(free[6 + h % 2], turn(6 + h % 2, ("go", h)) + 1)
                        t.matmul(whole(b), ones128[:, :], osq[h % 2][:, :], start=True, stop=True).then_inc(full[b], 1)
                elif kind == "ssdA":
                    i = it[1]
                    if i == 0:
                        pe.wait_ge(xbc_done, 6)
                        pe.wait_ge(cblk_done, 1)
                    c = slice(i * P, (i + 1) * P)
                    c3 = slice(3 + i * P, 3 + (i + 1) * P)
                    def decay_rows(q, name):
                        take(4 + q, (name, i))
                        for h in range(4):
                            out = bank[4 + q][:, h * P:(h + 1) * P]
                            t.matmul(out, sgni[:, 8 + 4 * q + h:9 + 4 * q + h].to_broadcast([16, P]), cum16[:, c],
                                     start=True, stop=False)
                            ins = t.matmul(out, identb[:, :], masks[:, :], start=False, stop=True)
                        ins.then_inc(full[4 + q], 1)

                    decay_rows(0, "bca")
                    take(7, ("xt", i))
                    for s in range(4):
                        ins = t.transpose(bank[7][:, s * P:(s + 1) * P], xbc[:, s, c3], ident[:, :])
                    ins.then_inc(full[7], 1)
                    take(6, ("sc", i))
                    t.matmul(bank[6][:, 0:256].rearrange("p (g t) -> p g t", t=P), xbc[:, 4, c3], cblk[:, :, c],
                             start=True, stop=True)
                    t.transpose(bank[6][:, 256:384], xbc[:, 4, c3], ident[:, :]).then_inc(full[6], 1)
                    decay_rows(1, "bcb")
                elif kind == "ssdB":
                    i = it[1]
                    c3 = slice(3 + i * P, 3 + (i + 1) * P)
                    take(7, ("yi", i))
                    pe.wait_ge(free[6], turn(6, ("sc", i)) + 1)
                    for h in range(SSM_H):
                        ins = t.matmul(bank[7][:, h * 64:h * 64 + 64], dec[:, h, :], xdt[:, h * 64:h * 64 + 64],
                                       start=True, stop=True)
                    ins.then_inc(full[7], 1)
                    if i:
                        pe.wait_ge(free[4], turn(4, ("st", i - 1)) + 1)
                        take(6, ("ye", i))
                        t.matmul(whole(6), xbc[:, 5, c3], stt[:, :], start=True, stop=True).then_inc(full[6], 1)
                    if i < NT - 1:
                        take(4, ("st", i))
                        t.matmul(whole(4), btok[:, :], xdt2[:, :], start=True, stop=True).then_inc(full[4], 1)
                elif kind == "ssdC":
                    i = it[1]
                    take(5, ("yt", i))
                    pe.wait_ge(sd_norm, i + 1)
                    for s in range(4):
                        ins = t.transpose(bank[5][:, s * P:(s + 1) * P], ysd[:, s * P:(s + 1) * P], ident[:, :])
                    ins.then_inc(full[5], 1)

            branches = ((oAh, oAl), (oBh, oBl), (oCh, oCl))
            for g in range(1, 6):
                dh, r = GATES[g]
                u = U_GATE + 3 * g
                for kh in range(2):
                    su = (u + kh) % RING
                    pe.wait_ge(lo_ready, u + kh + 1)
                    for s in range(4):
                        c = slice(s * P, (s + 1) * P)
                        if kh == 0:
                            take(s, ("gate", g))
                        for j in range(4):
                            k = 4 * kh + j
                            ins = passes(whole(s), (whi[:, su, j, c], wlo[:, su, j, c]), (hTh[:, k, :], hTl[:, k, :]),
                                         k == 0, k == KD - 1)
                        if kh == 1:
                            ins.then_inc(full[s], 1)
                        elif s == 3:
                            ins.then_inc(unit_used, 1)
                su = (u + 2) % RING
                pe.wait_ge(lo_ready, u + 3)
                for s in range(4):
                    c = slice(s * P, (s + 1) * P)
                    take(4 + s, ("proj", g))
                    for j in range(4):
                        jh = gslot(j) if r == 1 else j
                        ins = passes(whole(4 + s), (whi[:, su, j, c], wlo[:, su, j, c]),
                                     (branches[r][0][:, jh, :], branches[r][1][:, j, :]), j == 0, j == 3)
                    ins.then_inc(full[4 + s], 1)
            for kh in range(2):
                for nh in range(2):
                    u = U_OUT + 2 * kh + nh
                    pe.wait_ge(y_done, 4 * kh + 4)
                    pe.wait_ge(lo_ready, u + 1)
                    for i in range(NT):
                        c = slice(i * P, (i + 1) * P)
                        if kh == 0:
                            take(4 * nh + i, ("out", nh))
                        for j in range(4):
                            k = 4 * kh + j
                            ins = passes(whole(4 * nh + i), (yTh[kh][:, j, c], yTl[kh][:, j, c]),
                                         (whi[:, u % RING, j, :], wlo[:, u % RING, j, :]), k == 0, k == KD - 1)
                        if kh == 1:
                            ins.then_inc(full[4 * nh + i], 1)
                        elif i == NT - 1:
                            ins.then_inc(unit_used, 1)
            for i in range(NT):
                pe.wait_ge(free[4 + i], turn(4 + i, ("out", 1)) + 1)
                for k in range(KD):
                    if i == 0:
                        take(k, "h2T")
                    ins = t.transpose(bank[k][:, i * P:(i + 1) * P], x1[:, i, k * P:(k + 1) * P], ident[:, :])
                    if i == NT - 1:
                        ins.then_inc(full[k], 1)
            pe.wait_ge(wr_done, 1)
            for k in range(KD):
                pe.wait_ge(free[k], turn(k, "h2T") + 1)
            for k in range(KD):
                ins = t.matmul(bank[0][0:20, :], wr[:, k, :], h2T[:, k, :], start=k == 0, stop=k == KD - 1)
            ins.then_inc(full[0], 1)
            take(2, "logits")
            pe.wait_ge(free[0], turn(0, "logitsT") + 1)
            for i in range(NT):
                ins = t.transpose(bank[2][:, i * 20:i * 20 + 20], lgT[:, i * P:(i + 1) * P], ident[0:20, 0:20])
            ins.then_inc(full[2], 1)
            pe.wait_ge(r_ab, 1)
            for i in range(NT):
                for j in range(i + 1):
                    t.matmul(bank[1][:, 16 * i:16 * i + 16], (trib if j == i else onesb)[:, :], ab[:, j, :],
                             start=j == 0, stop=j == i)
            for j in range(NT):
                ins = t.matmul(bank[1][:, 64:80], onesb[:, :], ab[:, j, :], start=j == 0, stop=j == NT - 1)
            ins.then_inc(full[1], 1)

            def expert_unit(u, out, lhs, first, last, b=None, m=None, per=12):
                su = u % RING
                pe.wait_ge(lo_ready, after(m, per, u + 1))
                for j in range(4):
                    ins = passes(out, (lhs[0][:, j, :], lhs[1][:, j, :]), (whi[:, su, j, :], wlo[:, su, j, :]),
                                 first and j == 0, last and j == 3)
                return ins

            def up_product(n, u, b, par, m=None, per=2, uper=12, between=None):
                for kh in range(2):
                    if kh == 0:
                        pe.wait_ge(free[b], after(m, per, B0[b] + n))
                        if b == 0:
                            for q in (4, 5):
                                pe.wait_ge(free[q], after(m, per, B0[q] + n + 1))
                    k = slice(4 * kh, 4 * kh + 4)
                    ins = expert_unit(u + kh, whole(b), (xTh[:, par, k, :], xTl[:, par, k, :]), kh == 0, kh == 1,
                                      m=m, per=uper)
                    if kh == 0:
                        ins.then_inc(unit_used, 1)
                        if between:
                            between()
                    else:
                        ins.then_inc(full[b], 1)

            def down_product(n, u, m=None, per=2, uper=12):
                pe.wait_ge(free[6], after(m, per, B0[6] + n + 1))
                for nh in range(2):
                    pe.wait_ge(free[2 + nh], after(m, per, B0[2 + nh] + n))
                    ins = expert_unit(u + nh, whole(2 + nh), (hdh, hdl), True, True, m=m, per=uper)
                    ins.then_inc(full[2 + nh], 1)

            def turn_rows(n, par, landed, m=None, per=2, lper=16):
                pe.wait_ge(xg_in[par], after(m, lper, landed))
                for half in range(2):
                    b = 4 + half
                    pe.wait_ge(free[b], after(m, per, B0[b] + n))
                    for q in range(4):
                        k = 4 * half + q
                        ins = t.transpose(bank[b][:, q * P:(q + 1) * P], xg[:, par, k * P:(k + 1) * P], ident[:, :])
                    ins.then_inc(full[b], 1)

            def turn_hid(n, m=None, per=2):
                pe.wait_ge(free[1], after(m, per, B0[1] + n + 1))
                pe.wait_ge(free[6], after(m, per, B0[6] + n))
                for j in range(4):
                    ins = t.transpose(bank[6][:, j * P:(j + 1) * P], hid[:, j * P:(j + 1) * P], ident[:, :])
                ins.then_inc(full[6], 1)

            def item(n, u, landed, m=None):
                up_product(n, u, 0, n % 2, m, between=lambda: turn_hid(n - 1, m))
                down_product(n - 1, u + 2, m)
                if n < NEXP - 1:
                    turn_rows(n + 1, (n + 1) % 2, landed, m)
                up_product(n, u + 4, 1, n % 2, m)

            turn_rows(0, 0, 16)
            u = U_MOE
            up_product(0, u, 0, 0)
            turn_rows(1, 1, 16)
            up_product(0, u + 2, 1, 0)
            with pe.Fori(0, 7) as m:
                item(1, u + 4, 32, m)
                item(2, u + 10, 32, m)
            item(15, u + 88, 0)
            turn_hid(15)
            down_product(15, u + 94)
            pe.wait_ge(r_slot, 2)
            count = pe.value_load(ovi[0:1, 0:1], min_val=0, max_val=OVF)
            with pe.If(count > 0):
                with pe.Fori(0, count) as m:
                    u = U_OVF
                    turn_rows(NEXP, 0, 16 * (NEXP // 2 + 1), m, 1, 16)
                    up_product(NEXP, u, 0, 0, m, 1, 6)
                    up_product(NEXP, u + 2, 1, 0, m, 1, 6)
                    turn_hid(NEXP, m, 1)
                    down_product(NEXP, u + 4, m, 1, 6)
                pe.nop()


_OUT = "out_dram"


def kernel(**inputs):
    from concourse import bacc
    from concourse.bass_utils import run_bass_kernel_spmd

    nc = bacc.Bacc("TRN2", target_bir_lowering=False, num_devices=1)
    arrays, args = {}, {}
    for name, value in inputs.items():
        a = np.ascontiguousarray(value)[0]
        arrays[f"in_{name}"] = a
        args[name] = nc.dram_tensor(f"in_{name}", a.shape, mybir.dt.from_np(a.dtype), kind="ExternalInput").ap()
    acc = nc.dram_tensor(_OUT, (T + P, D), F32, kind="ExternalOutput").ap()
    build(nc, acc=acc, **args)
    out = run_bass_kernel_spmd(nc, [arrays], core_ids=[0]).results[0][_OUT]
    return out[:T].reshape(1, T, D)
```
